# Optimizing a Trainium2 kernel written in Bass

```python
import math
import jax, jax.numpy as jnp
from jax import lax
import numpy as np

D_MODEL = 1024
BATCH = 1
SEQ = 512
DEPTH = 1

ROPE_THETA = 500000.0
EPS = 1e-6
Q_BLOCK = 128
NEG = -1e30

MLA_HEADS = 8
MLA_NOPE = 64
MLA_ROPE = 32
MLA_QK = MLA_NOPE + MLA_ROPE
MLA_V = 64
MLA_Q_LORA = 768
MLA_KV_LORA = 256

NSA_HEADS = 8
NSA_KV_GROUPS = 2
NSA_REP = NSA_HEADS // NSA_KV_GROUPS
NSA_HEAD = 64
NSA_ROT = NSA_HEAD // 4
CMP_LEN = 32
CMP_STRIDE = 16
CMP_HIDDEN = 256
SEL_LEN = 64
SEL_TOP = 8
SEL_Q_BLOCK = 64
WINDOW = 256
N_NSA_BRANCH = 3
FORCE_BONUS = 1e4
KV_W = NSA_KV_GROUPS * NSA_HEAD

N_BRANCH = 2
D_FF = -(-8 * D_MODEL // (3 * 256)) * 256
N_MOD = 6

IN_SIZES = (MLA_Q_LORA, MLA_KV_LORA, MLA_ROPE, NSA_HEADS * NSA_HEAD,
            KV_W, KV_W, KV_W, KV_W, KV_W, KV_W,
            NSA_HEADS * N_NSA_BRANCH, D_MODEL, D_MODEL)
D_IN = sum(IN_SIZES)


def rms_norm(x, gain):
    xf = x.astype(jnp.float32)
    y = xf * lax.rsqrt(jnp.mean(xf * xf, axis=-1, keepdims=True) + EPS)
    return (y * gain.astype(jnp.float32)).astype(x.dtype)

def rope_angles(pos, dim):
    inv = ROPE_THETA ** (-jnp.arange(0, dim, 2, dtype=jnp.float32) / dim)
    ang = pos.astype(jnp.float32)[..., None] * inv
    return jnp.cos(ang), jnp.sin(ang)

def apply_rope(x, cos, sin):
    x1, x2 = jnp.split(x, 2, axis=-1)
    cos = cos.astype(x.dtype)
    sin = sin.astype(x.dtype)
    return jnp.concatenate([x1 * cos - x2 * sin, x2 * cos + x1 * sin], axis=-1)

def partial_rope(x, cos, sin):
    return jnp.concatenate([apply_rope(x[..., :NSA_ROT], cos, sin), x[..., NSA_ROT:]], axis=-1)

def causal_block_attention(q, k, v, scale):
    B, S, H, Dk = q.shape
    nb = S // Q_BLOCK
    qb = q.reshape(B, nb, Q_BLOCK, H, Dk).transpose(1, 0, 2, 3, 4)
    kpos = jnp.arange(S)

    def one(args):
        qi, i = args
        s = jnp.einsum('bqhd,bkhd->bhqk', qi, k).astype(jnp.float32) * scale
        qpos = i * Q_BLOCK + jnp.arange(Q_BLOCK)
        s = jnp.where(kpos[None, :] <= qpos[:, None], s, NEG)
        p = jax.nn.softmax(s, axis=-1).astype(v.dtype)
        return jnp.einsum('bhqk,bkhd->bqhd', p, v)

    o = lax.map(one, (qb, jnp.arange(nb)))
    return o.transpose(1, 0, 2, 3, 4).reshape(B, S, H, v.shape[-1])

def mla_attention(c_q, c_kv, k_pe, cos, sin, q_a_gain, w_q_b, kv_a_gain, w_kv_b, q_gain, k_gain):
    B, S, _ = c_q.shape
    q = (rms_norm(c_q, q_a_gain) @ w_q_b).reshape(B, S, MLA_HEADS, MLA_QK)
    kv = (rms_norm(c_kv, kv_a_gain) @ w_kv_b).reshape(B, S, MLA_HEADS, MLA_NOPE + MLA_V)
    k_nope, v = kv[..., :MLA_NOPE], kv[..., MLA_NOPE:]
    k = jnp.concatenate([k_nope, jnp.broadcast_to(k_pe[:, :, None, :], (B, S, MLA_HEADS, MLA_ROPE))], axis=-1)
    q = rms_norm(q, q_gain)
    k = rms_norm(k, k_gain)
    cos_h, sin_h = cos[:, :, None], sin[:, :, None]
    q = jnp.concatenate([q[..., :MLA_NOPE], apply_rope(q[..., MLA_NOPE:], cos_h, sin_h)], axis=-1)
    k = jnp.concatenate([k[..., :MLA_NOPE], apply_rope(k[..., MLA_NOPE:], cos_h, sin_h)], axis=-1)
    o = causal_block_attention(q, k, v, MLA_QK ** -0.5)
    return o.reshape(B, S, MLA_HEADS * MLA_V)

def nsa_attention(q, k_c, v_c, k_s, v_s, k_w, v_w, g_logit, cos, sin,
                  q_gain, kc_gain, ks_gain, kw_gain,
                  cmp_pos_k, cmp_w1_k, cmp_w2_k, cmp_pos_v, cmp_w1_v, cmp_w2_v):
    B, S, H, Dh = q.shape
    G, R = NSA_KV_GROUPS, NSA_REP
    f32 = jnp.float32
    scale = Dh ** -0.5
    cos_t, sin_t = cos[:, :, None], sin[:, :, None]
    q = partial_rope(rms_norm(q, q_gain), cos_t, sin_t)
    qg = q.reshape(B, S, G, R, Dh)
    t_idx = jnp.arange(S)

    n_cmp = (S - CMP_LEN) // CMP_STRIDE + 1
    starts = jnp.arange(n_cmp) * CMP_STRIDE
    blk_idx = starts[:, None] + jnp.arange(CMP_LEN)[None, :]

    def compress(t, pos_emb, w1, w2):
        blocks = t[:, blk_idx] + pos_emb[None, None, :, None, :]
        flat = blocks.transpose(0, 1, 3, 2, 4).reshape(B, n_cmp, G, CMP_LEN * Dh)
        return jax.nn.silu(flat @ w1) @ w2

    cmp_end = starts + CMP_LEN - 1
    kc = compress(k_c, cmp_pos_k, cmp_w1_k, cmp_w2_k)
    vc = compress(v_c, cmp_pos_v, cmp_w1_v, cmp_w2_v)
    kc = partial_rope(rms_norm(kc, kc_gain), cos[:, cmp_end][:, :, None], sin[:, cmp_end][:, :, None])
    s_c = jnp.einsum('bsgrd,bngd->bgrsn', qg, kc).astype(f32) * scale
    valid_c = cmp_end[None, :] <= t_idx[:, None]
    p_c = jax.nn.softmax(jnp.where(valid_c, s_c, NEG), axis=-1) * valid_c
    o_c = jnp.einsum('bgrsn,bngd->bsgrd', p_c.astype(vc.dtype), vc)

    n_sel = S // SEL_LEN
    sel_start = jnp.arange(n_sel) * SEL_LEN
    overlap = ((starts[:, None] < sel_start[None, :] + SEL_LEN) &
               (starts[:, None] + CMP_LEN > sel_start[None, :])).astype(f32)
    imp = jnp.einsum('bgrsn,nj->bgsj', p_c, overlap)
    cur = t_idx // SEL_LEN
    j = jnp.arange(n_sel)
    forced = (j[None, :] == 0) | (j[None, :] == cur[:, None]) | (j[None, :] == cur[:, None] - 1)
    imp = jnp.where(forced, imp + FORCE_BONUS, imp)
    imp = jnp.where(j[None, :] <= cur[:, None], imp, NEG)
    top = min(SEL_TOP, n_sel)
    _, sel_idx = lax.top_k(imp, top)

    ks = partial_rope(rms_norm(k_s, ks_gain), cos_t, sin_t)
    k_blocks = ks.reshape(B, n_sel, SEL_LEN, G, Dh).transpose(0, 3, 1, 2, 4)
    v_blocks = v_s.reshape(B, n_sel, SEL_LEN, G, Dh).transpose(0, 3, 1, 2, 4)
    nqb = S // SEL_Q_BLOCK
    q_chunks = qg.reshape(B, nqb, SEL_Q_BLOCK, G, R, Dh).transpose(1, 0, 2, 3, 4, 5)
    idx_chunks = sel_idx.reshape(B, G, nqb, SEL_Q_BLOCK, top).transpose(2, 0, 1, 3, 4)
    gather = jax.vmap(jax.vmap(lambda blk, ix: blk[ix]))

    def sel_chunk(args):
        qi, ix, ci = args
        kg = gather(k_blocks, ix)
        vg = gather(v_blocks, ix)
        s = jnp.einsum('bqgrd,bgqnld->bgrqnl', qi, kg).astype(f32) * scale
        tok = ix[..., None] * SEL_LEN + jnp.arange(SEL_LEN)
        qt = ci * SEL_Q_BLOCK + jnp.arange(SEL_Q_BLOCK)
        mask = tok <= qt[None, None, :, None, None]
        s = jnp.where(mask[:, :, None], s, NEG)
        sh = s.shape
        p = jax.nn.softmax(s.reshape(sh[0], sh[1], sh[2], sh[3], -1), axis=-1).reshape(sh)
        return jnp.einsum('bgrqnl,bgqnld->bqgrd', p.astype(vg.dtype), vg)

    o_s = lax.map(sel_chunk, (q_chunks, idx_chunks, jnp.arange(nqb)))
    o_s = o_s.transpose(1, 0, 2, 3, 4, 5).reshape(B, S, G, R, Dh)

    kw = partial_rope(rms_norm(k_w, kw_gain), cos_t, sin_t)
    nqw = S // Q_BLOCK
    span = WINDOW + Q_BLOCK
    kw_pad = jnp.pad(kw, ((0, 0), (WINDOW, 0), (0, 0), (0, 0)))
    vw_pad = jnp.pad(v_w, ((0, 0), (WINDOW, 0), (0, 0), (0, 0)))
    band = jnp.arange(nqw)[:, None] * Q_BLOCK + jnp.arange(span)[None, :]
    kb = kw_pad[:, band]
    vb = vw_pad[:, band]
    qb = qg.reshape(B, nqw, Q_BLOCK, G, R, Dh)
    s_w = jnp.einsum('bcqgrd,bckgd->bcgrqk', qb, kb).astype(f32) * scale
    key_t = band - WINDOW
    q_t = jnp.arange(nqw)[:, None] * Q_BLOCK + jnp.arange(Q_BLOCK)[None, :]
    diff = q_t[:, :, None] - key_t[:, None, :]
    mask_w = (diff >= 0) & (diff < WINDOW) & (key_t[:, None, :] >= 0)
    s_w = jnp.where(mask_w[None, :, None, None], s_w, NEG)
    p_w = jax.nn.softmax(s_w, axis=-1).astype(vb.dtype)
    o_w = jnp.einsum('bcgrqk,bckgd->bcqgrd', p_w, vb).reshape(B, S, G, R, Dh)

    g = jax.nn.sigmoid(g_logit).reshape(B, S, G, R, N_NSA_BRANCH, 1)
    o = g[..., 0, :] * o_c + g[..., 1, :] * o_s + g[..., 2, :] * o_w
    return o.reshape(B, S, H * Dh)

def first_inputs(seed: int = 0) -> dict:
    key = jax.random.key(seed)

    def nrm(i, shape, scale):
        return jax.random.normal(jax.random.fold_in(key, i), shape, jnp.float32) * scale

    def gain(i, n):
        return 1.0 + nrm(i, (DEPTH, n), 0.02)

    L = DEPTH
    offset = jax.random.randint(jax.random.fold_in(key, 99), (BATCH, 1), 0, 4096)
    positions = (offset + jnp.arange(SEQ)[None, :]).astype(jnp.int32)
    return {
        "x": nrm(0, (BATCH, SEQ, D_MODEL), 1.0),
        "c": nrm(1, (BATCH, D_MODEL), 1.0),
        "positions": positions,
        "ada_w": nrm(2, (L, D_MODEL, N_MOD * D_MODEL), 0.5 * D_MODEL ** -0.5),
        "ada_b": nrm(3, (L, N_MOD * D_MODEL), 0.02),
        "norm1_gain": gain(4, D_MODEL),
        "w_in": nrm(5, (L, D_MODEL, D_IN), D_MODEL ** -0.5),
        "mla_q_a_gain": gain(6, MLA_Q_LORA),
        "mla_w_q_b": nrm(7, (L, MLA_Q_LORA, MLA_HEADS * MLA_QK), MLA_Q_LORA ** -0.5),
        "mla_kv_a_gain": gain(8, MLA_KV_LORA),
        "mla_w_kv_b": nrm(9, (L, MLA_KV_LORA, MLA_HEADS * (MLA_NOPE + MLA_V)), MLA_KV_LORA ** -0.5),
        "mla_q_gain": gain(10, MLA_QK),
        "mla_k_gain": gain(11, MLA_QK),
        "nsa_q_gain": gain(12, NSA_HEAD),
        "nsa_kc_gain": gain(13, NSA_HEAD),
        "nsa_ks_gain": gain(14, NSA_HEAD),
        "nsa_kw_gain": gain(15, NSA_HEAD),
        "cmp_pos_k": nrm(16, (L, CMP_LEN, NSA_HEAD), 0.1),
        "cmp_w1_k": nrm(17, (L, CMP_LEN * NSA_HEAD, CMP_HIDDEN), (CMP_LEN * NSA_HEAD) ** -0.5),
        "cmp_w2_k": nrm(18, (L, CMP_HIDDEN, NSA_HEAD), CMP_HIDDEN ** -0.5),
        "cmp_pos_v": nrm(19, (L, CMP_LEN, NSA_HEAD), 0.1),
        "cmp_w1_v": nrm(20, (L, CMP_LEN * NSA_HEAD, CMP_HIDDEN), (CMP_LEN * NSA_HEAD) ** -0.5),
        "cmp_w2_v": nrm(21, (L, CMP_HIDDEN, NSA_HEAD), CMP_HIDDEN ** -0.5),
        "w_o_mla": nrm(22, (L, MLA_HEADS * MLA_V, D_MODEL), (MLA_HEADS * MLA_V) ** -0.5),
        "w_o_nsa": nrm(23, (L, NSA_HEADS * NSA_HEAD, D_MODEL), (NSA_HEADS * NSA_HEAD) ** -0.5),
        "w_out": nrm(24, (L, D_MODEL, D_MODEL), D_MODEL ** -0.5),
        "norm2_gain": gain(25, D_MODEL),
        "ffn_w_gate": nrm(26, (L, D_MODEL, D_FF), D_MODEL ** -0.5),
        "ffn_w_up": nrm(27, (L, D_MODEL, D_FF), D_MODEL ** -0.5),
        "ffn_w_down": nrm(28, (L, D_FF, D_MODEL), D_FF ** -0.5),
    }

def first_block(x, c, positions, ada_w, ada_b, norm1_gain, w_in,
              mla_q_a_gain, mla_w_q_b, mla_kv_a_gain, mla_w_kv_b, mla_q_gain, mla_k_gain,
              nsa_q_gain, nsa_kc_gain, nsa_ks_gain, nsa_kw_gain,
              cmp_pos_k, cmp_w1_k, cmp_w2_k, cmp_pos_v, cmp_w1_v, cmp_w2_v,
              w_o_mla, w_o_nsa, w_out, norm2_gain, ffn_w_gate, ffn_w_up, ffn_w_down):
    B, S, _ = x.shape
    mla_cos, mla_sin = rope_angles(positions, MLA_ROPE)
    nsa_cos, nsa_sin = rope_angles(positions, NSA_ROT)
    split_at = np.cumsum(IN_SIZES)[:-1]
    for l in range(DEPTH):
        mod = jax.nn.silu(c) @ ada_w[l] + ada_b[l]
        sh1, sc1, gt1, sh2, sc2, gt2 = [m[:, None, :] for m in jnp.split(mod, N_MOD, axis=-1)]

        h = rms_norm(x, norm1_gain[l]) * (1.0 + sc1) + sh1
        z = h @ w_in[l]
        (c_q, c_kv, k_pe, q_n, k_c, v_c, k_s, v_s, k_w, v_w,
         g_nsa, g_mla_merge, g_nsa_merge) = jnp.split(z, split_at, axis=-1)
        y_mla = mla_attention(c_q, c_kv, k_pe, mla_cos, mla_sin,
                              mla_q_a_gain[l], mla_w_q_b[l], mla_kv_a_gain[l], mla_w_kv_b[l],
                              mla_q_gain[l], mla_k_gain[l]) @ w_o_mla[l]
        kvs = lambda t: t.reshape(B, S, NSA_KV_GROUPS, NSA_HEAD)
        y_nsa = nsa_attention(q_n.reshape(B, S, NSA_HEADS, NSA_HEAD),
                              kvs(k_c), kvs(v_c), kvs(k_s), kvs(v_s), kvs(k_w), kvs(v_w),
                              g_nsa.reshape(B, S, NSA_HEADS, N_NSA_BRANCH), nsa_cos, nsa_sin,
                              nsa_q_gain[l], nsa_kc_gain[l], nsa_ks_gain[l], nsa_kw_gain[l],
                              cmp_pos_k[l], cmp_w1_k[l], cmp_w2_k[l],
                              cmp_pos_v[l], cmp_w1_v[l], cmp_w2_v[l]) @ w_o_nsa[l]
        merged = jax.nn.sigmoid(g_mla_merge) * y_mla + jax.nn.sigmoid(g_nsa_merge) * y_nsa
        x = x + gt1 * (merged @ w_out[l])

        h2 = rms_norm(x, norm2_gain[l]) * (1.0 + sc2) + sh2
        x = x + gt2 * ((jax.nn.silu(h2 @ ffn_w_gate[l]) * (h2 @ ffn_w_up[l])) @ ffn_w_down[l])
    return x


DEPTH_2 = 2

HEAD_DIM = 64
N_HEADS = D_MODEL // HEAD_DIM
N_HEADS_A = N_HEADS // 4
N_HEADS_B = N_HEADS // 4
N_HEADS_C = N_HEADS - N_HEADS_A - N_HEADS_B
WIDTH_A = N_HEADS_A * HEAD_DIM
WIDTH_B = N_HEADS_B * HEAD_DIM
WIDTH_C = N_HEADS_C * HEAD_DIM
DIFF_DIM = HEAD_DIM // 2
ROPE_FRACTION = 4
MOBA_BLOCK = 256
MOBA_TOPK = 3
MOBA_Q_CHUNK = 32
DILATED_PATTERNS = ((128, 1), (512, 4), (2048, 16))
SW_BLOCK = 128
D_FF_2 = ((8 * D_MODEL // 3 + 255) // 256) * 256
CONV_WIDTH = 3
NEG_INF = -1e30


def rms_norm_2(x, g):
    xf = x.astype(jnp.float32)
    y = xf * lax.rsqrt(jnp.mean(xf * xf, axis=-1, keepdims=True) + EPS)
    return (y * g.astype(jnp.float32)).astype(x.dtype)

def partial_rope_2(x, positions):
    d = x.shape[-1]
    rot = d // ROPE_FRACTION
    half = rot // 2
    inv = jnp.power(jnp.float32(ROPE_THETA), -jnp.arange(half, dtype=jnp.float32) * 2.0 / rot)
    ang = positions.astype(jnp.float32)[..., None] * inv
    ang = ang.reshape((x.shape[0],) + (1,) * (x.ndim - 3) + ang.shape[1:])
    cos = jnp.cos(ang).astype(x.dtype)
    sin = jnp.sin(ang).astype(x.dtype)
    x1 = x[..., :half]
    x2 = x[..., half:rot]
    return jnp.concatenate([x1 * cos - x2 * sin, x2 * cos + x1 * sin, x[..., rot:]], axis=-1)

def to_heads(t, h):
    b, s, _ = t.shape
    return t.reshape(b, s, h, -1).transpose(0, 2, 1, 3)

def from_heads(t):
    b, h, s, d = t.shape
    return t.transpose(0, 2, 1, 3).reshape(b, s, h * d)

def differential_attention(q, k, v, positions, lam, g_head, lam_init):
    b, s, _ = q.shape
    h = N_HEADS_A
    q = partial_rope_2(q.reshape(b, s, h, 2, DIFF_DIM).transpose(0, 2, 3, 1, 4), positions)
    k = partial_rope_2(k.reshape(b, s, h, 2, DIFF_DIM).transpose(0, 2, 3, 1, 4), positions)
    vf = to_heads(v, h).astype(jnp.float32)
    nq = s // Q_BLOCK
    qb = q.reshape(b, h, 2, nq, Q_BLOCK, DIFF_DIM).transpose(3, 0, 1, 2, 4, 5)
    key_pos = jnp.arange(s)
    scale = DIFF_DIM ** -0.5

    def block(args):
        qi, i = args
        sc = jnp.einsum('bhcqd,bhckd->bhcqk', qi, k).astype(jnp.float32) * scale
        q_pos = i * Q_BLOCK + jnp.arange(Q_BLOCK)
        sc = jnp.where(key_pos[None, :] <= q_pos[:, None], sc, NEG_INF)
        p = jax.nn.softmax(sc, axis=-1)
        a = p[:, :, 0] - lam * p[:, :, 1]
        return jnp.einsum('bhqk,bhkd->bhqd', a, vf)

    o = lax.map(block, (qb, jnp.arange(nq)))
    o = o.transpose(1, 2, 0, 3, 4).reshape(b, h, s, HEAD_DIM)
    o = rms_norm_2(o, g_head) * (1.0 - lam_init)
    return from_heads(o)

def moba_attention(q, k, v, positions):
    b, s, _ = q.shape
    h = N_HEADS_B
    q = partial_rope_2(to_heads(q, h), positions)
    k = partial_rope_2(to_heads(k, h), positions)
    v = to_heads(v, h)
    nb = -(-s // MOBA_BLOCK)
    sp = nb * MOBA_BLOCK
    pad = ((0, 0), (0, 0), (0, sp - s), (0, 0))
    q, k, v = jnp.pad(q, pad), jnp.pad(k, pad), jnp.pad(v, pad)
    n_sel = max(1, min(MOBA_TOPK, nb - 1))
    kb = k.reshape(b, h, nb, MOBA_BLOCK, HEAD_DIM)
    vb = v.reshape(b, h, nb, MOBA_BLOCK, HEAD_DIM)
    k_mean = jnp.mean(kb.astype(jnp.float32), axis=3)
    gate = jnp.einsum('bhsd,bhnd->bhsn', q.astype(jnp.float32), k_mean)
    q_blk = jnp.arange(sp) // MOBA_BLOCK
    gate = jnp.where(jnp.arange(nb)[None, :] < q_blk[:, None], gate, NEG_INF)
    _, sel = lax.top_k(gate, n_sel)
    valid = jnp.arange(n_sel)[None, :] < q_blk[:, None]
    c = MOBA_Q_CHUNK
    nc = sp // c
    qc = q.reshape(b, h, nc, c, HEAD_DIM).transpose(2, 0, 1, 3, 4)
    selc = sel.reshape(b, h, nc, c, n_sel).transpose(2, 0, 1, 3, 4)
    validc = valid.reshape(nc, c, n_sel)
    b_idx = jnp.arange(b)[:, None, None, None]
    h_idx = jnp.arange(h)[None, :, None, None]
    scale = HEAD_DIM ** -0.5

    def chunk(args):
        qi, si, vi, ci = args
        kg = kb[b_idx, h_idx, si]
        vg = vb[b_idx, h_idx, si].astype(jnp.float32)
        q_pos = ci * c + jnp.arange(c)
        start = (ci * c) // MOBA_BLOCK * MOBA_BLOCK
        k_own = lax.dynamic_slice_in_dim(k, start, MOBA_BLOCK, axis=2)
        v_own = lax.dynamic_slice_in_dim(v, start, MOBA_BLOCK, axis=2).astype(jnp.float32)
        s_sel = jnp.einsum('bhqd,bhqnkd->bhqnk', qi, kg).astype(jnp.float32) * scale
        s_sel = jnp.where(vi[None, None, :, :, None], s_sel, NEG_INF).reshape(b, h, c, n_sel * MOBA_BLOCK)
        s_own = jnp.einsum('bhqd,bhkd->bhqk', qi, k_own).astype(jnp.float32) * scale
        k_pos = start + jnp.arange(MOBA_BLOCK)
        s_own = jnp.where(k_pos[None, :] <= q_pos[:, None], s_own, NEG_INF)
        p = jax.nn.softmax(jnp.concatenate([s_sel, s_own], axis=-1), axis=-1)
        p_sel = p[..., :n_sel * MOBA_BLOCK].reshape(b, h, c, n_sel, MOBA_BLOCK)
        p_own = p[..., n_sel * MOBA_BLOCK:]
        return (jnp.einsum('bhqnk,bhqnkd->bhqd', p_sel, vg)
                + jnp.einsum('bhqk,bhkd->bhqd', p_own, v_own))

    o = lax.map(chunk, (qc, selc, validc, jnp.arange(nc)))
    o = o.transpose(1, 2, 0, 3, 4).reshape(b, h, sp, HEAD_DIM)[:, :, :s]
    return from_heads(o)

def dilated_branch(q, k, v, window, dil):
    b, h, s, d = q.shape
    span = dil * SW_BLOCK
    sp = -(-s // span) * span
    m_len = sp // dil
    nb = m_len // SW_BLOCK
    w_sub = window // dil

    def sub(t):
        t = jnp.pad(t, ((0, 0), (0, 0), (0, sp - s), (0, 0)))
        return t.reshape(b, h, m_len, dil, d).transpose(0, 1, 3, 2, 4).reshape(b, h, dil, nb, SW_BLOCK, d)

    def band(t):
        prev = jnp.pad(t, ((0, 0), (0, 0), (0, 0), (1, 0), (0, 0), (0, 0)))[:, :, :, :-1]
        return jnp.concatenate([prev, t], axis=4)

    qs = sub(q)
    kw = band(sub(k))
    vw = band(sub(v)).astype(jnp.float32)
    sc = jnp.einsum('bhrnqd,bhrnkd->bhrnqk', qs, kw).astype(jnp.float32) * (d ** -0.5)
    qi = jnp.arange(SW_BLOCK)[:, None]
    kj = jnp.arange(2 * SW_BLOCK)[None, :] - SW_BLOCK
    dist = qi - kj
    blk = jnp.arange(nb)[:, None, None]
    mask = (dist >= 0) & (dist <= w_sub) & (blk * SW_BLOCK + kj >= 0)
    sc = jnp.where(mask, sc, NEG_INF)
    mx = jnp.max(sc, axis=-1, keepdims=True)
    e = jnp.exp(sc - mx)
    den = jnp.sum(e, axis=-1)
    o = jnp.einsum('bhrnqk,bhrnkd->bhrnqd', e, vw) / den[..., None]
    lse = mx[..., 0] + jnp.log(den)
    o = o.reshape(b, h, dil, m_len, d).transpose(0, 1, 3, 2, 4).reshape(b, h, sp, d)[:, :, :s]
    lse = lse.reshape(b, h, dil, m_len).transpose(0, 1, 3, 2).reshape(b, h, sp)[:, :, :s]
    return o, lse

def dilated_attention(q, k, v, positions):
    h = N_HEADS_C
    q = partial_rope_2(to_heads(q, h), positions)
    k = partial_rope_2(to_heads(k, h), positions)
    v = to_heads(v, h)
    outs, lses = [], []
    for window, dil in DILATED_PATTERNS:
        o, lse = dilated_branch(q, k, v, window, dil)
        outs.append(o)
        lses.append(lse)
    wts = jax.nn.softmax(jnp.stack(lses, axis=0), axis=0)
    o = jnp.sum(wts[..., None] * jnp.stack(outs, axis=0), axis=0)
    return from_heads(o)

def conv_gated_mlp(h, w_up, conv_w, conv_b, w_down):
    u = h @ w_up
    u = lax.conv_general_dilated(u, conv_w[:, None, :].astype(u.dtype), window_strides=(1,),
                                 padding=[(CONV_WIDTH - 1, 0)],
                                 dimension_numbers=('NWC', 'WIO', 'NWC'),
                                 feature_group_count=u.shape[-1]) + conv_b
    gate, val = jnp.split(u, 2, axis=-1)
    return (jax.nn.silu(gate) * val) @ w_down

def second_inputs(seed: int = 0) -> dict:
    key = jax.random.key(seed)
    ks = jax.random.split(key, 16)
    nrm = jax.random.normal
    return {
        'x': nrm(ks[0], (BATCH, SEQ, D_MODEL), jnp.float32),
        'positions': jnp.broadcast_to(jnp.arange(SEQ, dtype=jnp.int32)[None, :], (BATCH, SEQ)),
        'g_mix': 1.0 + 0.02 * nrm(ks[1], (DEPTH_2, D_MODEL), jnp.float32),
        'w_in': nrm(ks[2], (DEPTH_2, D_MODEL, 3 * D_MODEL), jnp.float32) * D_MODEL ** -0.5,
        'w_out': nrm(ks[3], (DEPTH_2, D_MODEL, D_MODEL), jnp.float32) * D_MODEL ** -0.5,
        'lambda_q1': 0.1 * nrm(ks[4], (DEPTH_2, DIFF_DIM), jnp.float32),
        'lambda_k1': 0.1 * nrm(ks[5], (DEPTH_2, DIFF_DIM), jnp.float32),
        'lambda_q2': 0.1 * nrm(ks[6], (DEPTH_2, DIFF_DIM), jnp.float32),
        'lambda_k2': 0.1 * nrm(ks[7], (DEPTH_2, DIFF_DIM), jnp.float32),
        'g_diff': 1.0 + 0.02 * nrm(ks[8], (DEPTH_2, HEAD_DIM), jnp.float32),
        'g_ffn': 1.0 + 0.02 * nrm(ks[9], (DEPTH_2, D_MODEL), jnp.float32),
        'w_up': nrm(ks[10], (DEPTH_2, D_MODEL, 2 * D_FF_2), jnp.float32) * D_MODEL ** -0.5,
        'conv_w': nrm(ks[11], (DEPTH_2, CONV_WIDTH, 2 * D_FF_2), jnp.float32) * CONV_WIDTH ** -0.5,
        'conv_b': 0.01 * nrm(ks[12], (DEPTH_2, 2 * D_FF_2), jnp.float32),
        'w_down': nrm(ks[13], (DEPTH_2, D_FF_2, D_MODEL), jnp.float32) * D_FF_2 ** -0.5,
        'g_final': 1.0 + 0.02 * nrm(ks[14], (D_MODEL,), jnp.float32),
    }

def second_block(x, positions, g_mix, w_in, w_out, lambda_q1, lambda_k1, lambda_q2, lambda_k2,
              g_diff, g_ffn, w_up, conv_w, conv_b, w_down, g_final):
    widths = [WIDTH_A] * 3 + [WIDTH_B] * 3 + [WIDTH_C] * 3
    cuts = []
    acc = 0
    for wd in widths[:-1]:
        acc += wd
        cuts.append(acc)
    for layer in range(DEPTH_2):
        h = rms_norm_2(x, g_mix[layer])
        qkv = h @ w_in[layer]
        qa, ka, va, qb, kb, vb, qc, kc, vc = jnp.split(qkv, cuts, axis=-1)
        lam_init = 0.8 - 0.6 * math.exp(-0.3 * layer)
        lam = (jnp.exp(jnp.sum(lambda_q1[layer].astype(jnp.float32) * lambda_k1[layer].astype(jnp.float32)))
               - jnp.exp(jnp.sum(lambda_q2[layer].astype(jnp.float32) * lambda_k2[layer].astype(jnp.float32)))
               + lam_init)
        o_a = differential_attention(qa, ka, va, positions, lam, g_diff[layer], lam_init).astype(x.dtype)
        o_b = moba_attention(qb, kb, vb, positions).astype(x.dtype)
        o_c = dilated_attention(qc, kc, vc, positions).astype(x.dtype)
        mix = jnp.concatenate([o_a, o_b, o_c], axis=-1)
        x = x + mix @ w_out[layer]
        h2 = rms_norm_2(x, g_ffn[layer])
        x = x + conv_gated_mlp(h2, w_up[layer], conv_w[layer], conv_b[layer], w_down[layer]).astype(x.dtype)
    return rms_norm_2(x, g_final)


def setup_inputs(seed=0):
    out = dict(first_inputs(seed))
    for name, value in second_inputs(seed + 1).items():
        if name != "x":
            out[name + "_2"] = value
    return out


def reference(
    x, c, positions, ada_w, ada_b, norm1_gain, w_in, mla_q_a_gain, mla_w_q_b, mla_kv_a_gain,
    mla_w_kv_b, mla_q_gain, mla_k_gain, nsa_q_gain, nsa_kc_gain, nsa_ks_gain, nsa_kw_gain,
    cmp_pos_k, cmp_w1_k, cmp_w2_k, cmp_pos_v, cmp_w1_v, cmp_w2_v, w_o_mla, w_o_nsa, w_out,
    norm2_gain, ffn_w_gate, ffn_w_up, ffn_w_down, positions_2, g_mix_2, w_in_2, w_out_2,
    lambda_q1_2, lambda_k1_2, lambda_q2_2, lambda_k2_2, g_diff_2, g_ffn_2, w_up_2, conv_w_2,
    conv_b_2, w_down_2, g_final_2,
):
    x = first_block(
        x, c, positions, ada_w, ada_b, norm1_gain, w_in, mla_q_a_gain, mla_w_q_b, mla_kv_a_gain,
        mla_w_kv_b, mla_q_gain, mla_k_gain, nsa_q_gain, nsa_kc_gain, nsa_ks_gain, nsa_kw_gain,
        cmp_pos_k, cmp_w1_k, cmp_w2_k, cmp_pos_v, cmp_w1_v, cmp_w2_v, w_o_mla, w_o_nsa, w_out,
        norm2_gain, ffn_w_gate, ffn_w_up, ffn_w_down,
    )
    return second_block(
        x, positions_2, g_mix_2, w_in_2, w_out_2, lambda_q1_2, lambda_k1_2, lambda_q2_2,
        lambda_k2_2, g_diff_2, g_ffn_2, w_up_2, conv_w_2, conv_b_2, w_down_2, g_final_2,
    )


_drawn_inputs = setup_inputs


def setup_inputs(seed=0):
    import zlib

    import numpy as np

    out = dict(_drawn_inputs(seed))
    spreads = {}
    factors = {'norm1_gain': 8.0,
     'mla_q_a_gain': 8.0,
     'mla_kv_a_gain': 8.0,
     'mla_q_gain': 8.0,
     'mla_k_gain': 8.0,
     'nsa_q_gain': 8.0,
     'nsa_kc_gain': 8.0,
     'nsa_ks_gain': 8.0,
     'nsa_kw_gain': 8.0,
     'cmp_pos_k': 8.0,
     'cmp_w1_k': 3.048,
     'cmp_w2_k': 3.172,
     'cmp_pos_v': 4.097,
     'norm2_gain': 7.092,
     'g_mix_2': 2.992,
     'lambda_k1_2': 4.108,
     'lambda_q2_2': 2.84,
     'g_diff_2': 42.848,
     'g_ffn_2': 7.945,
     'conv_b_2': 15.498,
     'g_final_2': 22.924}
    for name, (base, spread) in spreads.items():
        noise = np.random.default_rng([zlib.crc32(name.encode()), seed]).standard_normal(out[name].shape)
        drawn = base * np.exp(spread * noise) if base else spread * noise
        out[name] = __import__('jax').numpy.asarray(drawn.astype(out[name].dtype))
    for name, factor in factors.items():
        out[name] = (out[name] * factor).astype(out[name].dtype)
    return out
```

```python
import math
from contextlib import ExitStack

import numpy as np

import concourse.bass as bass
from concourse import mybir

D_MODEL, SEQ = 1024, 512
P = 128
KD = D_MODEL // P
TT = SEQ // P
LAYERS = 2
MLA_HEADS, MLA_NOPE, MLA_ROPE, MLA_V = 8, 64, 32, 64
MLA_QK = MLA_NOPE + MLA_ROPE
Q_LORA, KV_LORA = 768, 256
HEADS, GROUPS, HD = 8, 2, 64
REP = HEADS // GROUPS
ROT = HD // 4
CMP_LEN, CMP_STRIDE, CMP_HIDDEN = 32, 16, 256
N_CMP = (SEQ - CMP_LEN) // CMP_STRIDE + 1
CMP_CHUNKS = CMP_LEN * HD // P
WINDOW = 256
D_FF = 2816
FB = D_FF // P
SLAB = 2048
EPS = 1e-6
NEG = 1e30
N_MOD = 6
TAIL = 312
TAIL_VW, TAIL_G, TAIL_PE = 128, 256, 280
THETA = 500000.0
LAM_INIT = [0.8 - 0.6 * math.exp(-0.3 * layer) for layer in range(LAYERS)]
DIFF = 32

N_IN, N_TAIL, N_QB, N_KVB, N_GATE, N_OM, N_ON, N_WOUT = 8, 2, 3, 1, 8, 2, 2, 4
N_UP, N_DOWN, N_IN2 = D_FF // 128, FB // 2, 12
PER_LAYER = N_IN2 + N_WOUT + N_UP + N_DOWN
N_SLABS = (N_IN + N_TAIL + N_QB + N_KVB + N_GATE + N_OM + N_ON + N_WOUT + N_UP + N_DOWN
           + LAYERS * PER_LAYER)
N_ADA = N_MOD * KD

COLS = {}
for _name, _n in (("norm1", KD), ("norm2", KD), ("q_a", Q_LORA // P), ("kv_a", KV_LORA // P),
                  ("mix", LAYERS * KD), ("ffn", LAYERS * KD), ("final", KD), ("ada_b", N_ADA),
                  ("conv_w", LAYERS * 3 * 2 * FB), ("conv_b", LAYERS * 2 * FB)):
    COLS[_name] = sum(n for _, n in COLS.values()), _n
NCOL = sum(n for _, n in COLS.values())
ROWS = {}
for _name, _n in (("mla_q", MLA_QK), ("mla_k", MLA_QK), ("q", HD), ("kc", HD), ("ks", HD), ("kw", HD),
                  ("diff", LAYERS * HD), ("lq1", LAYERS * DIFF), ("lk1", LAYERS * DIFF),
                  ("lq2", LAYERS * DIFF), ("lk2", LAYERS * DIFF)):
    ROWS[_name] = sum(n for _, n in ROWS.values()), _n
NROW = sum(n for _, n in ROWS.values())
N_FREQ = MLA_ROPE // 2 + ROT // 2
CONSTS = {}
for _name, _n in (("ident", P), ("mean", P), ("freq", N_FREQ), ("rowvalid", TT), ("cmask", TT * N_CMP),
                  ("causal", SEQ)):
    CONSTS[_name] = sum(n for _, n in CONSTS.values()), _n
NCONST = sum(n for _, n in CONSTS.values())


def two_pi_parts():
    a = 6.28125
    b = float(np.float32(round((2 * math.pi - a) * 2 ** 20) / 2 ** 20))
    c = float(np.float32(2 * math.pi - a - b))
    return a, b, c


def build(nc, xT_d, slabs_d, ada_d, c_d, cols_d, rows_d, consts_d, strips_d, pos_d, cpos_d,
          cmpw_d, cmpp_d, cmpw2_d, out_d, stop=99):
    f32, f32r, i32 = mybir.dt.float32, mybir.dt.float32r, mybir.dt.int32
    ALU, ACT, AX = mybir.AluOpType, mybir.ActivationFunctionType, mybir.AxisListType
    ds = bass.ds
    ctx = ExitStack()
    with ctx:
        def sb(name, shape, dt=f32):
            return ctx.enter_context(nc.sbuf_tensor(name, shape, dt))

        def sem(name):
            return ctx.enter_context(nc.semaphore(name))

        xT = sb("xT", [P, KD, SEQ])
        raw = sb("raw", [P, 2, SLAB])
        w_hi = sb("w_hi", [P, 2, SLAB], f32r)
        w_lo = sb("w_lo", [P, 2, SLAB], f32r)
        aux = sb("aux", [P, 2, D_MODEL])
        cols = sb("cols", [P, NCOL])
        rows = sb("rows", [P, NROW])
        consts = sb("consts", [P, NCONST])
        strip2 = sb("strip2", [P, SEQ])
        mod = sb("mod", [P, N_ADA])
        trig = sb("trig", [P, 2, TT, N_FREQ])
        ctrig = sb("ctrig", [P, 2, ROT // 2])
        posi = sb("posi", [P, 2 * TT + 1], i32)
        stats = sb("stats", [P, 256])
        small = sb("small", [P, 64])
        zero_c = sb("zero_c", [P, 2])
        negmax = sb("negmax", [P, 8])
        rowsum = sb("rowsum", [P, 4, TT])
        arena_at = -(-nc.sbuf_base // 32) * 32
        arena_size = 122880
        sb("arena", [P, arena_size // 4])

        def at(name, offset, shape, dt=f32):
            n = 4 * int(np.prod(shape[1:]))
            assert offset + n <= arena_size, (name, offset + n)
            return nc.alloc_sbuf_tensor_at(name, shape, dt, offset=arena_at + offset)

        z_tail = at("z_tail", 0, [P, TT, TAIL])
        z = at("z", 4992, [P, 4, TT, 512])
        h_hi = at("h_hi", 37760, [P, KD, SEQ], f32r)
        h_lo = at("h_lo", 54144, [P, KD, SEQ], f32r)
        cmpw = at("cmpw", 70528, [P, 2, CMP_CHUNKS, CMP_HIDDEN])
        t1 = at("t1", 4992, [P, KD, SEQ])
        crow = at("crow", 103296, [P, D_MODEL])
        junk = at("junk", 107392, [P, D_MODEL])
        qT_n = at("qT_n", 37760, [P, 4, SEQ])
        kT_n = at("kT_n", 45952, [P, 2, SEQ])
        ring_n = at("ring_n", 50048, [P, 9, SEQ])
        n_sq = at("n_sq", 50048, [P, HEADS * TT * HD])
        n_rope = at("n_rope", 58240, [P, 4, HEADS * TT * ROT // 2])
        n_sq2 = at("n_sq2", 66432, [P, 2, TT * GROUPS * HD])
        c_sq = at("c_sq", 58240, [P, GROUPS * HD])
        c_stage = at("c_stage", 50048, [P, TT, 4, 2, HD])
        c_kT = at("c_kT", 58240, [P, 4, SEQ])
        flat = at("flat", 111488, [P, CMP_CHUNKS, GROUPS, N_CMP])
        c_sm = at("c_sm", 50048, [P, REP, TT, 32])
        c_p = at("c_p", 52096, [P, REP * TT, 32])
        c_pT = at("c_pT", 54144, [P, REP * TT, P])
        otmp_n = at("otmp_n", 68480, [P, TT, HD])
        O_nsa = at("O_nsa", 103296, [P, TT, HEADS * HD])
        cmpw2 = sb("cmpw2", [P, 2, 2, HD])
        cmpp = sb("cmpp", [P, 2, CMP_CHUNKS])
        c_hid = sb("c_hid", [P, 2, GROUPS * N_CMP])
        c_k = sb("c_k", [P, GROUPS, HD])
        c_v = sb("c_v", [P, GROUPS, HD])
        c_kkT = sb("c_kkT", [P, N_CMP])
        q_m = at("q_m", 4992, [P, TT, MLA_HEADS * MLA_QK])
        ring_m = at("ring_m", 4992, [P, 9, SEQ])
        k_m = at("k_m", 21376, [P, TT, MLA_HEADS, MLA_QK])
        kv_m = at("kv_m", 37760, [P, TT, MLA_HEADS * (MLA_NOPE + MLA_V)])
        m_sq = at("m_sq", 54144, [P, TT * MLA_HEADS * MLA_QK])
        m_sq2 = at("m_sq2", 70528, [P, TT * MLA_HEADS * MLA_QK])
        m_rope = at("m_rope", 54144, [P, 4, TT * MLA_HEADS * MLA_ROPE // 2])
        O_mla = at("O_mla", 54144, [P, TT, MLA_HEADS * MLA_V])
        c_hi = at("c_hi", 70528, [P, KD, SEQ], f32r)
        c_lo = at("c_lo", 86912, [P, KD, SEQ], f32r)
        qT_m = at("qT_m", 70528, [P, MLA_HEADS, SEQ])
        kT_m = at("kT_m", 86912, [P, MLA_HEADS, SEQ])
        gate = at("gate", 0, [P, 2 * KD, SEQ])
        t2 = at("t2", 0, [P, KD, SEQ])
        OmT_hi = at("OmT_hi", 32768, [P, 4, SEQ], f32r)
        OmT_lo = at("OmT_lo", 40960, [P, 4, SEQ], f32r)
        g_hi = at("g_hi", 70528, [P, KD, SEQ], f32r)
        g_lo = at("g_lo", 86912, [P, KD, SEQ], f32r)
        OnT_hi = at("OnT_hi", 70528, [P, 4, SEQ], f32r)
        OnT_lo = at("OnT_lo", 78720, [P, 4, SEQ], f32r)
        mrg = at("mrg", 86912, [P, KD, SEQ])
        m_hi = at("m_hi", 0, [P, KD, SEQ], f32r)
        m_lo = at("m_lo", 16384, [P, KD, SEQ], f32r)
        mtmp = at("mtmp", 49152, [P, 2, SEQ])
        t3 = at("t3", 49152, [P, KD, SEQ])
        f_hi = at("f_hi", 0, [P, KD, SEQ], f32r)
        f_lo = at("f_lo", 16384, [P, KD, SEQ], f32r)
        a_hi = at("a_hi", 32768, [P, FB, SEQ], f32r)
        a_lo = at("a_lo", 77824, [P, FB, SEQ], f32r)
        tg, tv = aux[:, 0, 0:SEQ], aux[:, 0, SEQ:2 * SEQ]
        ta, tsg = aux[:, 1, 0:SEQ], aux[:, 1, SEQ:2 * SEQ]
        z2 = at("z2", 32768, [P, 6, TT, 512])
        t4 = at("t4", 81920, [P, KD, SEQ])
        T2 = at("T2", 0, [P, 16, SEQ])
        ring_2 = at("ring_2", 81920, [P, 9, SEQ])
        rope_2 = at("rope_2", 81920, [P, 4, 512])
        O2 = at("O2", 100352, [P, TT, D_MODEL])
        otmp_2 = at("otmp_2", 120832, [P, TT, HD])
        sq_2 = at("sq_2", 116736, [P, TT * 4 * HD])
        o_hi = at("o_hi", 0, [P, KD, SEQ], f32r)
        o_lo = at("o_lo", 16384, [P, KD, SEQ], f32r)

        PS = ctx.enter_context(nc.psum_tensor("PS", [P, 8, 512], f32))

        def const(name):
            a, n = CONSTS[name]
            return consts[:, a:a + n]

        def col(name, i=0, n=1):
            a = COLS[name][0]
            return cols[:, a + i:a + i + n]

        def row(name, i=0, n=None):
            a, m = ROWS[name]
            return rows[:, a + i:a + i + (n or m)]

        ident, mean_w = const("ident"), const("mean")
        causal = const("causal")
        eps_c, halfpi_c = small[:, 0:1], small[:, 1:2]
        lam_c = small[:, 2:3]

        const_loaded = sem("const_loaded")
        cmpw_loaded = sem("cmpw_loaded")
        strip_loaded = sem("strip_loaded")
        slab_loaded = [sem("slab_loaded0"), sem("slab_loaded1")]
        hi_done, slab_split, slab_used = sem("hi_done"), sem("slab_split"), sem("slab_used")
        zero_ready = sem("zero_ready")
        ada_loaded = [sem("ada_loaded0"), sem("ada_loaded1")]
        ada_used = sem("ada_used")
        arrived = {"pe": sem("pe_arrived"), "act": sem("act_arrived"), "dve": sem("dve_arrived")}
        part_ready, part_hi = sem("part_ready"), sem("part_hi")
        banks_filled, banks_drained = sem("banks_filled"), sem("banks_drained")
        up_drained = sem("up_drained")
        silu_ready, prod_ready, act_hi_ready = sem("silu_ready"), sem("prod_ready"), sem("act_hi_ready")
        conv_started, conv_ready = sem("conv_started"), sem("conv_ready")
        turned = sem("turned")
        turned_act, turned_dve = sem("turned_act"), sem("turned_dve")
        scores_ready, scores_masked, probs_ready = sem("scores_ready"), sem("scores_masked"), sem("probs_ready")
        probsT_ready, copied_act, copied_dve = sem("probsT_ready"), sem("copied_act"), sem("copied_dve")
        pv_done, out_ready, out_used = sem("pv_done"), sem("out_ready"), sem("out_used")
        stored = sem("stored")

        block = ctx.enter_context(nc.Block())
        n_slabs = {2: 10, 3: 10, 4: 10, 5: 10, 6: 14, 7: 14, 8: 30, 9: 63, 10: 75, 11: 79, 12: 112}.get(stop, N_SLABS)

        @block.sync
        def _(sp):
            for dst, src in ((cols[:], cols_d), (rows[:], rows_d.partition_broadcast(P)),
                             (consts[:], consts_d), (strip2[:], strips_d[0]), (posi[:, 0:2 * TT], pos_d),
                             (crow[:], c_d.partition_broadcast(P)),
                             (xT[:], xT_d)):
                sp.dma_start(dst, src).then_inc(const_loaded, 16)

            def load_slab(slot, n):
                src = slabs_d[n] if isinstance(n, int) else slabs_d[ds(n, 1)].rearrange("o p f -> (o p) f")
                sp.dma_start(raw[:, slot, :], src).then_inc(slab_loaded[slot], 16)

            def load_ada(slot, n):
                src = ada_d[n] if isinstance(n, int) else ada_d[ds(n, 1)].rearrange("o p f -> (o p) f")
                sp.dma_start(aux[:, slot, :], src).then_inc(ada_loaded[slot], 16)

            for s in (0, 1):
                load_ada(s, s)
            for s in (0, 1):
                load_slab(s, s)
            with sp.Fori(1, 2 * KD // 2) as i:
                for s in (0, 1):
                    sp.wait_ge(ada_used, 2 * i + (s - 1))
                    load_ada(s, 2 * i + s)
            with sp.Fori(0, 4) as i:
                for s in (0, 1):
                    sp.wait_ge(slab_split, 2 * i + (s + 1))
                    load_slab(s, 2 * i + (s + 2))
                for k in range(8):
                    sp.wait_ge(ada_used, 8 * i + (2 * KD + k - 1))
                    load_ada(k % 2, 8 * i + (2 * KD + k))
            if n_slabs > 11:
              with sp.Fori(5, n_slabs // 2) as i:
                for s in (0, 1):
                    sp.wait_ge(slab_split, 2 * i + (s - 1))
                    load_slab(s, 2 * i + s)
            if n_slabs % 2:
                sp.wait_ge(slab_split, n_slabs - 2)
                load_slab(0, n_slabs - 1)

        @block.gpsimd
        def _(pool):
            nc.gpsimd.memset(zero_c[:], 0.0).then_inc(zero_ready, 1)
            pool.wait_ge(zero_ready, 1)
            zero = zero_c[:, 0:1].to_broadcast([P, SLAB])

            def split(slot, n, nth, first=False):
                pool.wait_ge(slab_loaded[slot], 16 * nth + 16)
                if not first:
                    pool.wait_ge(slab_used, n - 1)
                nc.gpsimd.tensor_tensor(w_hi[:, slot, :], raw[:, slot, :], zero, ALU.add).then_inc(hi_done, 1)
                pool.wait_ge(hi_done, n + 1)
                nc.gpsimd.tensor_tensor(w_lo[:, slot, :], raw[:, slot, :], w_hi[:, slot, :].bitcast(f32),
                                        ALU.subtract).then_inc(slab_split, 1)

            for s in (0, 1):
                split(s, s, 0, first=True)
            with pool.Fori(1, n_slabs // 2) as i:
                for s in (0, 1):
                    split(s, 2 * i + s, i)
            if n_slabs % 2:
                split(0, n_slabs - 1, n_slabs // 2)

        class Place:

            def __init__(self):
                self.meets = self.slab = self.fill = self.drain = 0
                self.tile = self.map = self.acopies = self.dcopies = 0
                self.turn = self.turn_a = self.turn_d = self.part = self.ffn = self.conv = 0

        def meeting(name, eng, at_):
            def meet(n=1):
                for _ in range(n):
                    at_.meets += 1
                    eng.drain().then_inc(arrived[name], 1)
                    for other in ("pe", "act", "dve"):
                        eng.wait_ge(arrived[other], at_.meets)
            return meet

        def slab_view(t, slot, k, n):
            return t[:, slot, 0:k * n].rearrange("p (k n) -> p k n", k=k)

        TURN_LAG, VALUE_LAG, TAKE_LAG = 3, 5, 6
        S_BANKS, PT_BANKS, O_BANKS = 4, 2, 2
        M_SLOTS, P_SLOTS, PT_SLOTS = 2, 4, 3

        FILL = (6, 1, 1, 1, 1)

        def map_tiles(jobs):
            return [(m, j) for m in range(len(jobs)) for j in (3, 0, 2, 1)]

        def masked_slot(ring, u, n):
            return ring[:, u % M_SLOTS, 0:n]

        def probs_slot(ring, u, cols_):
            return ring[:, M_SLOTS + u % P_SLOTS, cols_]

        def turned_slot(ring, u, cols_):
            return ring[:, M_SLOTS + P_SLOTS + u % PT_SLOTS, cols_]

        def last_of_map(u):
            return u % TT == TT - 1

        def key_range(job, j):
            lo = max(0, j - 2) if job["window"] else 0
            return lo, j - lo + 1

        def job(q, k, v, out, strip=None, window=False, coef=None, mode="set"):
            return dict(q=q, k=k, v=v, out=out, strip=strip, window=window, coef=coef, mode=mode)

        def sigm(h, b):
            return z_tail[:, :, TAIL_G + 3 * h + b]

        nsa_jobs = []
        for r in range(REP):
            for g in range(GROUPS):
                h, lo = g * REP + r, 64 * g
                for b, kslot, v in ((1, 0, lambda kb, g=g: z[:, 1, kb, 384 + 64 * g:448 + 64 * g]),
                                    (2, 1, lambda kb, g=g: z_tail[:, kb, TAIL_VW + 64 * g:TAIL_VW + 64 + 64 * g])):
                    nsa_jobs.append(job(qT_n[lo:lo + 64, r, :], kT_n[lo:lo + 64, kslot, :], v,
                                        O_nsa[:, :, 64 * h:64 * h + 64], strip2[:] if b == 2 else causal,
                                        window=b == 2, coef=sigm(h, b), mode="add"))
        mla_jobs = [job(qT_m[0:MLA_QK, h, :], kT_m[0:MLA_QK, h, :],
                        lambda kb, h=h: kv_m[:, kb, 128 * h + 64:128 * h + 128],
                        O_mla[:, :, 64 * h:64 * h + 64], causal) for h in range(MLA_HEADS)]
        two_jobs = []
        for h in range(8):
            lo = 64 * (h % 2)
            two_jobs.append(job(T2[lo:lo + 64, 8 + h // 2, :], T2[lo:lo + 64, 12 + h // 2, :],
                                lambda kb, h=h: z2[:, 5, kb, 64 * h:64 * h + 64],
                                O2[:, :, 512 + 64 * h:576 + 64 * h], strip2[:]))
        for h in range(4):
            lo = 64 * (h % 2)
            two_jobs.append(job(T2[lo:lo + 64, 4 + h // 2, :], T2[lo:lo + 64, 6 + h // 2, :],
                                lambda kb, h=h: z2[:, 2, kb, 256 + 64 * h:320 + 64 * h],
                                O2[:, :, 256 + 64 * h:320 + 64 * h], causal))
        for h in range(4):
            for c in range(2):
                at0 = (2 * h + c) % 4 * DIFF
                two_jobs.append(job(T2[at0:at0 + DIFF, h // 2, :], T2[at0:at0 + DIFF, 2 + h // 2, :],
                                    lambda kb, h=h: z2[:, 1, kb, 64 * h:64 * h + 64],
                                    O2[:, :, 64 * h:64 * h + 64], causal,
                                    coef="lam" if c else None, mode="sub" if c else "set"))

        def nsa_turns():
            out = [(lambda tt, r=r: z[:, 0, tt, 128 * r:128 * r + 128], P, qT_n[:, r, :], -HD ** -0.5)
                   for r in range(REP)]
            out.append((lambda tt: z[:, 1, tt, 256:384], P, kT_n[:, 0, :], 1.0))
            out.append((lambda tt: z_tail[:, tt, 0:128], P, kT_n[:, 1, :], 1.0))
            return out

        cmp_turns = [(lambda tt, i=i: c_stage[:, tt, i, :, :], P, c_kT[:, i, :], 1.0) for i in range(4)]
        mla_turns = []
        for h in range(MLA_HEADS):
            mla_turns.append((lambda tt, h=h: q_m[:, tt, MLA_QK * h:MLA_QK * h + MLA_QK], MLA_QK,
                              qT_m[0:MLA_QK, h, :], -MLA_QK ** -0.5))
            mla_turns.append((lambda tt, h=h: k_m[:, tt, h, :], MLA_QK, kT_m[0:MLA_QK, h, :], 1.0))
        two_turns = []
        for slot, (chunk, at0, n, scale) in zip(
                (0, 2, 4, 6, 8, 12),
                ((0, 0, 2, -DIFF ** -0.5), (0, 256, 2, 1.0), (1, 256, 2, -HD ** -0.5), (2, 0, 2, 1.0),
                 (3, 0, 4, -HD ** -0.5), (4, 0, 4, 1.0))):
            for i in range(n):
                two_turns.append((lambda tt, c=chunk, a=at0 + 128 * i: z2[:, c, tt, a:a + 128], P,
                                  T2[:, slot + i, :], scale))

        def turn_split(src, hi, lo, n, gains=None):
            return [(lambda tt, i=i: src(tt, i), hi[:, i, :], lo[:, i, :], gains[i] if gains else None)
                    for i in range(n)]

        c_splits = turn_split(lambda tt, i: z[:, 2, tt, 128 * i:128 * i + 128] if i < 4
                              else z[:, 3, tt, 128 * (i - 4):128 * (i - 4) + 128], c_hi, c_lo, 8,
                              [col("q_a", i) for i in range(6)] + [col("kv_a", i) for i in range(2)])
        om_splits = turn_split(lambda tt, i: O_mla[:, tt, 128 * i:128 * i + 128], OmT_hi, OmT_lo, 4)
        on_splits = turn_split(lambda tt, i: O_nsa[:, tt, 128 * i:128 * i + 128], OnT_hi, OnT_lo, 4)
        o2_splits = turn_split(lambda tt, i: O2[:, tt, 128 * i:128 * i + 128], o_hi, o_lo, 8)

        @block.tensor
        def _(pe):
            at_ = Place()
            meet = meeting("pe", pe, at_)

            def three(out, a_hi_, a_lo_, b_hi_, b_lo_, start, stop):
                nc.tensor.matmul(out, a_hi_, b_hi_, start=start, stop=False)
                nc.tensor.matmul(out, a_hi_, b_lo_, start=False, stop=False)
                return nc.tensor.matmul(out, a_lo_, b_hi_, start=False, stop=stop)

            def norm_sum(t):
                for k in range(KD):
                    nc.tensor.matmul(PS[:, 0, :], mean_w, t[:, k, :], start=k == 0, stop=k == KD - 1)

            def slab_tokens(slot, hi, lo, k0, nk, n, banks, halves, start, stop):
                wh, wl = slab_view(w_hi, slot, nk, n), slab_view(w_lo, slot, nk, n)
                w = n // halves
                for k in range(nk):
                    for tt in range(TT):
                        ts = slice(128 * tt, 128 * tt + 128)
                        for hf in range(halves):
                            last = three(PS[:, banks + halves * tt + hf, 0:w], hi[:, k0 + k, ts], lo[:, k0 + k, ts],
                                         wh[:, k, w * hf:w * hf + w], wl[:, k, w * hf:w * hf + w],
                                         start and k == 0, stop and k == nk - 1)
                last.then_inc(slab_used, 1)
                return last

            def input_tokens(hi, lo, n_chunks):
                def two(i, guarded):
                    for par in (0, 1):
                        if guarded:
                            pe.wait_ge(banks_drained, 2 * i + (at_.drain + par - 1))
                        for s in (0, 1):
                            pe.wait_ge(slab_split, 4 * i + (at_.slab + 2 * par + s + 1))
                            slab_tokens((at_.slab + s) % 2, hi, lo, 4 * s, 4, 512, 4 * par, 1, s == 0, s == 1)
                        pe.drain().then_inc(banks_filled, 1)
                two(0, False)
                with pe.Fori(1, n_chunks // 2) as i:
                    two(i, True)
                at_.slab += 2 * n_chunks
                at_.fill += n_chunks
                at_.drain += n_chunks

            def slab_features(slot, nk, n, hi_k, lo_k, bank_of, start, stop):
                wh, wl = slab_view(w_hi, slot, nk, n), slab_view(w_lo, slot, nk, n)
                for k in range(nk):
                    for b in range(n // 128):
                        bs = slice(128 * b, 128 * b + 128)
                        last = three(PS[:, bank_of(b), :], wh[:, k, bs], wl[:, k, bs], hi_k(k), lo_k(k),
                                     start and k == 0, stop and k == nk - 1)
                last.then_inc(slab_used, 1)

            def project(hi, lo, n):
                for s in range(n):
                    pe.wait_ge(slab_split, at_.slab + 1)
                    slab_features(at_.slab % 2, 2, 1024, lambda k: hi[:, 2 * s + k, :], lambda k: lo[:, 2 * s + k, :],
                                  lambda b: b, s == 0, s == n - 1)
                    at_.slab += 1

            def project_ffn():
                def one(slot, n, k0, start, stop):
                    pe.wait_ge(slab_split, n + 1)

                    def part(t, k):
                        kk = k0 + k
                        return (t[:, kk, :] if isinstance(kk, int)
                                else t[:, ds(kk, 1), :].rearrange("p o f -> p (o f)"))
                    slab_features(slot, 2, 1024, lambda k: part(a_hi, k), lambda k: part(a_lo, k),
                                  lambda b: b, start, stop)
                base, par = at_.slab, at_.slab % 2
                one(par, base, 0, True, False)
                with pe.Fori(0, N_DOWN // 2 - 1) as i:
                    for s in (1, 2):
                        one((par + s) % 2, 2 * i + (base + s), 4 * i + 2 * s, False, False)
                for s in (N_DOWN - 2, N_DOWN - 1):
                    one((par + s) % 2, base + s, 2 * s, False, s == N_DOWN - 1)
                at_.slab += N_DOWN

            def feature_slab_fill(slot, quarter, n, hi, lo):
                pe.wait_ge(slab_split, n + 1)
                slab_features(slot, 8, 256, lambda k: hi[:, k, :], lambda k: lo[:, k, :],
                              lambda b: 2 * quarter + b, True, True)
                pe.drain().then_inc(banks_filled, 1)

            def gates():
                par = at_.slab % 2
                for q in range(4):
                    feature_slab_fill((par + q) % 2, q, at_.slab + q, g_hi, g_lo)
                for q in range(4):
                    pe.wait_ge(banks_drained, at_.drain + q + 1)
                    feature_slab_fill((par + q) % 2, q, at_.slab + 4 + q, g_hi, g_lo)
                at_.slab += N_GATE
                at_.fill += N_GATE
                at_.drain += N_GATE

            def ffn_up():
                base, par, drained = at_.slab, at_.slab % 2, at_.ffn

                def pair(i, half, guarded):
                    for u in (0, 1):
                        if guarded:
                            pe.wait_ge(up_drained, 4 * i + (drained + 2 * half - 2))
                        feature_slab_fill((par + u) % 2, 2 * half + u, 4 * i + (base + 2 * half + u), f_hi, f_lo)
                pair(0, 0, False)
                pair(0, 1, False)
                with pe.Fori(1, FB // 4) as i:
                    pair(i, 0, True)
                    pair(i, 1, True)
                pair(FB // 4, 0, True)
                at_.slab += N_UP
                at_.fill += N_UP
                at_.ffn += FB

            def turn(items, split=False):
                for n, it in enumerate(items):
                    src, w = it[0], (P if split else it[1])
                    if n >= 8:
                        pe.wait_ge(turned_dve if n % 2 else turned_act,
                                   (at_.turn_d if n % 2 else at_.turn_a) + (n - 8) // 2 + 1)
                    for tt in range(TT):
                        last = nc.tensor.transpose(PS[0:w, n % 8, 128 * tt:128 * tt + 128], src(tt), ident)
                    last.then_inc(turned, 1)
                at_.turn += len(items)
                at_.turn_a += len(items) if split else (len(items) + 1) // 2
                at_.turn_d += len(items) if split else len(items) // 2

            def release_clock(n):
                for _ in range(n):
                    nc.tensor.matmul(PS[:, 7, :], ident, causal, start=True, stop=True)

            def attend(jobs, ring):
                tiles = map_tiles(jobs)
                g0, m0 = at_.tile, at_.map
                copies = []
                a, d = at_.acopies, at_.dcopies
                for m, j in tiles:
                    if j == TT - 1:
                        d += 1
                        copies.append((copied_dve, d))
                    else:
                        a += 1
                        copies.append((copied_act, a))
                n = len(tiles)
                for step in range(n + VALUE_LAG):
                    if step < n:
                        m, j = tiles[step]
                        lo, nb = key_range(jobs[m], j)
                        if step >= S_BANKS:
                            pe.wait_ge(scores_masked, g0 + step - S_BANKS + 1)
                        nc.tensor.matmul(PS[:, step % S_BANKS, 0:128 * nb], jobs[m]["q"][:, 128 * j:128 * j + 128],
                                         jobs[m]["k"][:, 128 * lo:128 * (lo + nb)], start=True, stop=True
                                         ).then_inc(scores_ready, 1)
                    if TURN_LAG <= step < TURN_LAG + len(FILL):
                        release_clock(FILL[step - TURN_LAG])
                    u = step - TURN_LAG
                    if 0 <= u < n:
                        m, j = tiles[u]
                        lo, nb = key_range(jobs[m], j)
                        pe.wait_ge(probs_ready, g0 + u + 1)
                        if u >= PT_BANKS:
                            pe.wait_ge(*copies[u - PT_BANKS])
                        for b in range(nb):
                            last = nc.tensor.transpose(PS[:, S_BANKS + u % PT_BANKS, 128 * b:128 * b + 128],
                                                       probs_slot(ring, u, slice(128 * b, 128 * b + 128)), ident)
                        last.then_inc(probsT_ready, 1)
                    u = step - VALUE_LAG
                    if 0 <= u < n:
                        m, j = tiles[u]
                        lo, nb = key_range(jobs[m], j)
                        pe.wait_ge(*copies[u])
                        if u % TT == 0 and m >= O_BANKS:
                            pe.wait_ge(out_used, m0 + m - O_BANKS + 1)
                        for b in range(nb):
                            last = nc.tensor.matmul(PS[:, 6 + m % O_BANKS, 64 * j:64 * j + 64],
                                                    turned_slot(ring, u, slice(128 * b, 128 * b + 128)),
                                                    jobs[m]["v"](lo + b), start=b == 0, stop=b == nb - 1)
                        last.then_inc(pv_done, 1)
                at_.tile += n
                at_.map += len(jobs)
                at_.acopies, at_.dcopies = a, d

            def norm(t):
                meet()
                norm_sum(t)
                meet(3)

            meet()
            norm(t1)
            input_tokens(h_hi, h_lo, 4)
            pe.wait_ge(banks_drained, at_.drain - 1)
            for s in (0, 1):
                pe.wait_ge(slab_split, at_.slab + 1)
                slab_tokens(s, h_hi, h_lo, 4 * s, 4, TAIL, 0, 1, s == 0, s == 1)
                at_.slab += 1
            pe.drain().then_inc(banks_filled, 1)
            at_.fill += 1
            at_.drain += 1
            meet()
            if stop <= 2:
                return
            meet()
            turn(cmp_turns)
            meet()
            for kv in (0, 1):
                meet()
                for hf in (0, 1):
                    for c in range(CMP_CHUNKS):
                        nc.tensor.matmul(PS[:, hf, 0:GROUPS * N_CMP], cmpw[:, kv, c, 128 * hf:128 * hf + 128],
                                         flat[:, c, :, :], start=c == 0, stop=c == CMP_CHUNKS - 1)
                meet(2)
                for g in range(GROUPS):
                    for hf in (0, 1):
                        nc.tensor.matmul(PS[0:N_CMP, 2, HD * g:HD * g + HD], c_hid[:, hf, N_CMP * g:N_CMP * g + N_CMP],
                                         cmpw2[:, kv, hf, :], start=hf == 0, stop=hf == 1)
                meet(2)
            meet(4)
            nc.tensor.transpose(PS[:, 7, 0:N_CMP], c_k[0:N_CMP, :, :].rearrange("p g d -> p (g d)"),
                                ident[0:N_CMP, 0:N_CMP])
            turn(nsa_turns())
            meet()
            if stop <= 3:
                return
            for g in range(GROUPS):
                lo = 64 * g
                for i in range(REP * TT):
                    r, tt = divmod(i, TT)
                    nc.tensor.matmul(PS[:, 0, 32 * i:32 * i + N_CMP], qT_n[lo:lo + 64, r, 128 * tt:128 * tt + 128],
                                     c_kkT[lo:lo + 64, :], start=True, stop=True)
                meet(3)
                for i in range(REP * TT):
                    nc.tensor.transpose(PS[0:N_CMP, 1 + i // 4, 128 * (i % 4):128 * (i % 4) + 128],
                                        c_p[:, i, 0:N_CMP], ident)
                meet(2)
                for i in range(REP * TT):
                    nc.tensor.matmul(PS[:, 5 + i // 8, 64 * (i % 8):64 * (i % 8) + 64], c_pT[0:N_CMP, i, :],
                                     c_v[0:N_CMP, g, :], start=True, stop=True)
                meet(2)
            if stop <= 4:
                return
            attend(nsa_jobs, ring_n)
            meet()
            if stop <= 5:
                return
            meet(4)
            turn(c_splits, split=True)
            meet()
            for s in range(N_QB):
                pe.wait_ge(slab_split, at_.slab + 1)
                slab_tokens(at_.slab % 2, c_hi, c_lo, 2 * s, 2, Q_LORA, 0, 2, s == 0, s == N_QB - 1)
                at_.slab += 1
            meet(2)
            pe.wait_ge(slab_split, at_.slab + 1)
            slab_tokens(at_.slab % 2, c_hi, c_lo, 6, 2, 1024, 0, 2, True, True)
            at_.slab += 1
            meet(2)
            if stop <= 6:
                return
            meet(5)
            turn(mla_turns)
            meet()
            attend(mla_jobs, ring_m)
            meet()
            if stop <= 7:
                return
            norm(t2)
            turn(om_splits, split=True)
            meet()
            gates()
            meet()
            turn(on_splits, split=True)
            meet()
            project(OmT_hi, OmT_lo, N_OM)
            meet(2)
            project(OnT_hi, OnT_lo, N_ON)
            meet(2)
            project(m_hi, m_lo, N_WOUT)
            meet(2)
            if stop <= 8:
                return

            def mlp():
                norm(t3)
                ffn_up()
                meet()
                project_ffn()
                meet(2)

            mlp()
            if stop <= 9:
                return
            for layer in range(LAYERS):
                norm(t4)
                input_tokens(f_hi, f_lo, 6)
                meet(2)
                turn(two_turns)
                meet()
                attend(two_jobs, ring_2)
                meet()
                if stop <= 10:
                    return
                meet(4)
                turn(o2_splits, split=True)
                meet()
                project(o_hi, o_lo, N_WOUT)
                meet(2)
                if stop <= 11:
                    return
                mlp()
                if stop <= 12:
                    return
            meet()
            norm_sum(t3)
            meet(3)

        @block.scalar
        def _(act):
            at_ = Place()
            meet = meeting("act", act, at_)
            A = nc.scalar.activation
            for dst, src in ((cmpw[:], cmpw_d), (cmpp[:], cmpp_d), (cmpw2[:], cmpw2_d),
                             (posi[0:N_CMP, TT * 2:TT * 2 + 1], cpos_d)):
                act.dma_start(dst, src).then_inc(cmpw_loaded, 16)

            def norm(t, hi):
                A(t[:], xT[:], ACT.Square)
                meet(2)
                A(PS[:, 1, :], PS[:, 0, :], ACT.Sqrt, bias=eps_c)
                meet()
                high_parts(t, hi)
                meet()

            def high_parts(t, hi):
                for k in range(KD):
                    act.wait_ge(part_ready, at_.part + k + 1)
                    A(hi[:, k, :], t[:, k, :], ACT.Copy).then_inc(part_hi, 1)
                at_.part += KD

            def evacuate(dst, n_chunks):
                with act.Fori(0, n_chunks // 2) as i:
                    for par in (0, 1):
                        act.wait_ge(banks_filled, 2 * i + (at_.fill + par + 1))
                        A(dst(2 * i + par), PS[:, 4 * par:4 * par + 4, :], ACT.Copy).then_inc(banks_drained, 1)
                at_.fill += n_chunks

            def turn(items):
                for n, (_, w, dst, scale) in enumerate(items):
                    if n % 2 == 0:
                        act.wait_ge(turned, at_.turn + n + 1)
                        A(dst, PS[0:w, n % 8, :], ACT.Copy, scale=scale).then_inc(turned_act, 1)
                at_.turn += len(items)

            def turn_split_high(items):
                for n, (_, hi, lo, gain) in enumerate(items):
                    act.wait_ge(turned, at_.turn + n + 1)
                    A(hi, PS[:, n % 8, :], ACT.Copy, scale=1.0 if gain is None else gain).then_inc(turned_act, 1)
                at_.turn += len(items)

            def root(v, d):
                A(v, v, ACT.Sqrt, scale=1.0 / d, bias=eps_c[0:v.shape[0]])

            def attend(jobs, ring):
                tiles = map_tiles(jobs)
                g0 = at_.tile
                n = len(tiles)
                for step in range(n + TURN_LAG):
                    if step < n:
                        m, j = tiles[step]
                        _, nb = key_range(jobs[m], j)
                        act.wait_ge(scores_masked, g0 + step + 1)
                        if step >= P_SLOTS:
                            act.wait_ge(probsT_ready, g0 + step - P_SLOTS + 1)
                        A(probs_slot(ring, step, slice(0, 128 * nb)), masked_slot(ring, step, 128 * nb), ACT.Exp,
                          scale=-1.0,
                          bias=negmax[:, step % 8:step % 8 + 1],
                          accum_out=rowsum[:, m % 4, j:j + 1]).then_inc(probs_ready, 1)
                    u = step - TURN_LAG
                    if u >= 0 and tiles[u][1] != TT - 1:
                        _, nb = key_range(jobs[tiles[u][0]], tiles[u][1])
                        act.wait_ge(probsT_ready, g0 + u + 1)
                        if u >= PT_SLOTS:
                            act.wait_ge(pv_done, g0 + u - PT_SLOTS + 1)
                        A(turned_slot(ring, u, slice(0, 128 * nb)), PS[:, S_BANKS + u % PT_BANKS, 0:128 * nb],
                          ACT.Copy).then_inc(copied_act, 1)
                at_.tile += n

            act.wait_ge(const_loaded, 16 * 7)
            A(crow[:], crow[:], ACT.Silu)
            meet()
            A(trig[:].rearrange("p c t f -> p (c t f)"), trig[:].rearrange("p c t f -> p (c t f)"), ACT.Sin)
            A(ctrig[0:N_CMP, :, :], ctrig[0:N_CMP, :, :], ACT.Sin)
            norm(t1, h_hi)
            evacuate(lambda c: z[:, ds(c, 1), :, :], 4)
            act.wait_ge(banks_filled, at_.fill + 1)
            A(z_tail[:], PS[:, 0:4, 0:TAIL], ACT.Copy).then_inc(banks_drained, 1)
            at_.fill += 1
            meet()
            if stop <= 2:
                return
            A(z_tail[:, :, TAIL_G:TAIL_G + 24], z_tail[:, :, TAIL_G:TAIL_G + 24], ACT.Sigmoid)
            meet()
            turn(cmp_turns)
            meet()
            for kv in (0, 1):
                meet(2)
                A(c_hid[:], PS[:, 0:2, 0:GROUPS * N_CMP], ACT.Silu)
                meet(2)
                A((c_v if kv else c_k)[0:N_CMP, :, :].rearrange("p g d -> p (g d)"), PS[0:N_CMP, 2, 0:GROUPS * HD],
                  ACT.Copy)
                meet()
            A(n_sq[:], z[:, 0, :, :].rearrange("p t f -> p (t f)"), ACT.Square)
            A(n_sq2[:, 0, :], z[:, 1, :, 256:384], ACT.Square)
            A(n_sq2[:, 1, :], z_tail[:, :, 0:128], ACT.Square)
            A(c_sq[0:N_CMP, :], c_k[0:N_CMP, :, :].rearrange("p g d -> p (g d)"), ACT.Square)
            meet(2)
            root(stats[:, 0:48], HD)
            root(stats[0:N_CMP, 48:50], HD)
            meet(2)
            turn(nsa_turns())
            A(c_kkT[:], PS[:, 7, 0:N_CMP], ACT.Copy)
            meet()
            if stop <= 3:
                return
            for g in range(GROUPS):
                meet(2)
                A(c_p[:, :, 0:N_CMP], c_sm[:, :, :, 0:N_CMP].rearrange("p r t n -> p (r t) n"), ACT.Exp, scale=-1.0)
                meet(2)
                A(c_pT[0:N_CMP, :, :].rearrange("p i q -> p (i q)"),
                  PS[0:N_CMP, 1:5, :].rearrange("p b f -> p (b f)"), ACT.Copy)
                meet(3)
            if stop <= 4:
                return
            attend(nsa_jobs, ring_n)
            meet()
            if stop <= 5:
                return
            for tt in range(TT):
                A(m_sq[:, 0:512], z[:, 2, tt, :], ACT.Square, accum_out=stats[:, tt:tt + 1])
                act.drain()
                A(m_sq[:, 0:256], z[:, 3, tt, 0:256], ACT.Square, accum_out=stats[:, 4 + tt:5 + tt])
                act.drain()
                A(m_sq[:, 0:256], z[:, 3, tt, 256:512], ACT.Square, accum_out=stats[:, 8 + tt:9 + tt])
                act.drain()
            meet(2)
            root(stats[:, 0:4], Q_LORA)
            root(stats[:, 8:12], KV_LORA)
            meet(2)
            turn_split_high(c_splits)
            meet(2)
            for tt in (0, 1):
                A(q_m[:, tt, :].rearrange("p (a b) -> p a b", a=2), PS[:, 2 * tt:2 * tt + 2, 0:Q_LORA // 2], ACT.Copy)
            meet(2)
            for tt in (0, 1):
                A(kv_m[:, tt, :].rearrange("p (a b) -> p a b", a=2), PS[:, 2 * tt:2 * tt + 2, :], ACT.Copy)
            meet()
            if stop <= 6:
                return
            A(k_m[:, :, :, MLA_NOPE:MLA_QK],
              z_tail[:, :, TAIL_PE:TAIL].unsqueeze(2).to_broadcast([P, TT, MLA_HEADS, MLA_ROPE]), ACT.Copy)
            meet()
            A(m_sq[:], q_m[:].rearrange("p t f -> p (t f)"), ACT.Square)
            A(m_sq2[:], k_m[:].rearrange("p t h d -> p (t h d)"), ACT.Square)
            meet(2)
            root(stats[:, 0:64], MLA_QK)
            meet(2)
            turn(mla_turns)
            meet()
            attend(mla_jobs, ring_m)
            meet()
            if stop <= 7:
                return
            norm(t2, g_hi)
            turn_split_high(om_splits)
            meet()
            for q in range(N_GATE):
                act.wait_ge(banks_filled, at_.fill + q + 1)
                A(gate[:, 2 * q:2 * q + 2, :], PS[:, 2 * (q % 4):2 * (q % 4) + 2, :],
                  ACT.Sigmoid).then_inc(banks_drained, 1)
            at_.fill += N_GATE
            meet()
            turn_split_high(on_splits)
            meet(4)
            high_parts(mrg, m_hi)
            meet(3)
            if stop <= 8:
                return

            def mlp(layer):
                norm(t3, f_hi)
                fill0, f0 = at_.fill, at_.ffn

                def one(i, half, b):
                    f = 4 * i + (2 * half + b)
                    fi = ds(f, 1)
                    if layer is None:
                        act.wait_ge(banks_filled, 4 * i + (fill0 + 2 * half + 1))
                        A(tsg, PS[:, 4 * half + b, :], ACT.Silu).then_inc(silu_ready, 1)
                    else:
                        act.wait_ge(banks_filled, 4 * i + (fill0 + 2 * half + 2))
                        for t, bank, fb in ((tg, 4 * half + b, 0), (tv, 4 * half + 2 + b, FB)):
                            w = COLS["conv_w"][0] + (layer * 3 + 2) * 2 * FB + fb
                            c = COLS["conv_b"][0] + layer * 2 * FB + fb
                            last = A(t, PS[:, bank, :], ACT.Identity, scale=cols[:, ds(f + w, 1)],
                                     bias=cols[:, ds(f + c, 1)])
                        last.then_inc(conv_started, 1)
                        act.wait_ge(conv_ready, 4 * i + (at_.conv + 2 * half + b + 1))
                        A(tsg, tg, ACT.Silu).then_inc(silu_ready, 1)
                    act.wait_ge(prod_ready, 4 * i + (f0 + 2 * half + b + 1))
                    A(a_hi[:, fi, :], ta, ACT.Copy).then_inc(act_hi_ready, 1)

                with act.Fori(0, FB // 4) as i:
                    for half in (0, 1):
                        for b in (0, 1):
                            one(i, half, b)
                for b in (0, 1):
                    one(FB // 4, 0, b)
                at_.fill += N_UP
                at_.ffn += FB
                if layer is not None:
                    at_.conv += FB
                meet(3)

            mlp(None)
            if stop <= 9:
                return
            act.dma_start(strip2[:], strips_d[1]).then_inc(strip_loaded, 16)
            for layer in range(LAYERS):
                norm(t4, f_hi)
                evacuate(lambda c: z2[:, ds(c, 1), :, :], 6)
                meet(2)
                A(small[:, 4:6], small[:, 4:6], ACT.Exp)
                turn(two_turns)
                meet()
                attend(two_jobs, ring_2)
                meet()
                if stop <= 10:
                    return
                A(sq_2[:], O2[:, :, 0:256], ACT.Square)
                meet(2)
                root(stats[:, 0:16], HD)
                meet(2)
                turn_split_high(o2_splits)
                meet(3)
                if stop <= 11:
                    return
                mlp(layer)
                if stop <= 12:
                    return
            A(t3[:], xT[:], ACT.Square)
            meet(2)
            A(PS[:, 1, :], PS[:, 0, :], ACT.Sqrt, bias=eps_c)
            meet(2)
            act.dma_start(out_d, t3[:]).then_inc(stored, 16)
            act.wait_ge(stored, 16)

        @block.vector
        def _(dve):
            at_ = Place()
            meet = meeting("dve", dve, at_)
            V = nc.vector

            def then(_ins):
                dve.drain()

            def low_parts(t, hi, lo):
                for k in range(KD):
                    dve.wait_ge(part_hi, at_.part + k + 1)
                    V.tensor_tensor(lo[:, k, :], t[:, k, :], hi[:, k, :].bitcast(f32), ALU.subtract)
                at_.part += KD

            def norm(t, hi, lo, scale, shift=None):
                meet(3)
                then(V.reciprocal(PS[:, 2, :], PS[:, 1, :]))
                then(V.tensor_tensor(t[:], xT[:], PS[:, 2:3, :].to_broadcast([P, KD, SEQ]), ALU.mult))
                for k in range(KD):
                    if shift is None:
                        V.tensor_scalar(t[:, k, :], t[:, k, :], scale[:, k:k + 1], None, ALU.mult
                                        ).then_inc(part_ready, 1)
                    else:
                        V.tensor_scalar(t[:, k, :], t[:, k, :], scale[:, k:k + 1], shift[:, k:k + 1],
                                        ALU.mult, ALU.add).then_inc(part_ready, 1)
                dve.drain()
                low_parts(t, hi, lo)
                meet()

            def turn(items):
                for n, (_, w, dst, scale) in enumerate(items):
                    if n % 2:
                        dve.wait_ge(turned, at_.turn + n + 1)
                        V.tensor_scalar(dst, PS[0:w, n % 8, :], scale, None, ALU.mult).then_inc(turned_dve, 1)
                at_.turn += len(items)

            def turn_split_low(items):
                for n, (_, hi, lo, gain) in enumerate(items):
                    dve.wait_ge(turned_act, at_.turn_a + n + 1)
                    V.scalar_tensor_tensor(out=lo, in0=PS[:, n % 8, :], scalar=1.0 if gain is None else gain,
                                           in1=hi.bitcast(f32), op0=ALU.mult, op1=ALU.subtract
                                           ).then_inc(turned_dve, 1)
                at_.turn += len(items)
                at_.turn_a += len(items)

            def turn_counted(items):
                turn(items)
                at_.turn_a += (len(items) + 1) // 2

            def reduce_angles(ang, k, cosv, sinv):
                magic = 1.5 * 2.0 ** 23
                then(V.tensor_scalar(k, ang, 1.0 / (2 * math.pi), magic, ALU.mult, ALU.add))
                then(V.tensor_scalar(k, k, magic, None, ALU.subtract))
                for part in two_pi_parts():
                    then(V.scalar_tensor_tensor(out=ang, in0=k, scalar=-part, in1=ang, op0=ALU.mult, op1=ALU.add))
                then(V.tensor_scalar(sinv, ang, 3.1415925, -3.1415925, ALU.min, ALU.max))
                then(V.tensor_scalar(k, sinv, -1.0, None, ALU.mult))
                then(V.tensor_tensor(k, k, sinv, ALU.max))
                then(V.tensor_scalar(cosv, k, -1.0, math.pi / 2, ALU.mult, ALU.add))

            def rotate(x1, x2, cosv, sinv, tmp, n):
                shape = list(x1.shape)
                c, s = (v.unsqueeze(2).to_broadcast(shape) for v in (cosv, sinv))
                a, b, e, f = (tmp[0:shape[0], i, 0:n].rearrange("p (t h f) -> p t h f", t=shape[1], h=shape[2])
                              for i in range(4))
                V.tensor_tensor(a, x1, c, ALU.mult)
                V.tensor_tensor(b, x2, s, ALU.mult)
                V.tensor_tensor(e, x2, c, ALU.mult)
                then(V.tensor_tensor(f, x1, s, ALU.mult))
                V.tensor_tensor(x1, a, b, ALU.subtract)
                then(V.tensor_tensor(x2, e, f, ALU.add))

            def scale_heads(x, inv, gain):
                shape = list(x.shape)
                then(V.tensor_tensor(x, x, inv.rearrange("p (t h) -> p t h", t=shape[1]).unsqueeze(3)
                                     .to_broadcast(shape), ALU.mult))
                then(V.tensor_tensor(x, x, gain[0:shape[0]].unsqueeze(1).unsqueeze(1).to_broadcast(shape), ALU.mult))

            def attend(jobs, ring):
                tiles = map_tiles(jobs)
                g0, m0 = at_.tile, at_.map
                n = len(tiles)
                for step in range(n + TAKE_LAG):
                    if step < n:
                        m, j = tiles[step]
                        _, nb = key_range(jobs[m], j)
                        dve.wait_ge(scores_ready, g0 + step + 1)
                        if step >= M_SLOTS:
                            dve.wait_ge(probs_ready, g0 + step - M_SLOTS + 1)
                        V.tensor_tensor_reduce(out=masked_slot(ring, step, 128 * nb),
                                               in0=PS[:, step % S_BANKS, 0:128 * nb],
                                               in1=jobs[m]["strip"][:, SEQ - 128 * nb:SEQ], scale=1.0, scalar=NEG,
                                               op0=ALU.add, op1=ALU.min,
                                               accum_out=negmax[:, step % 8:step % 8 + 1]).then_inc(scores_masked, 1)
                    u = step - TURN_LAG
                    if 0 <= u < n and tiles[u][1] == TT - 1:
                        _, nb = key_range(jobs[tiles[u][0]], tiles[u][1])
                        dve.wait_ge(probsT_ready, g0 + u + 1)
                        if u >= PT_SLOTS:
                            dve.wait_ge(pv_done, g0 + u - PT_SLOTS + 1)
                        V.tensor_copy(turned_slot(ring, u, slice(0, 128 * nb)),
                                      PS[:, S_BANKS + u % PT_BANKS, 0:128 * nb]).then_inc(copied_dve, 1)
                    u = step - TAKE_LAG
                    if u >= 0 and last_of_map(u):
                        m = tiles[u][0]
                        dve.wait_ge(pv_done, g0 + u + 1)
                        finish(jobs[m], m)
                at_.tile += n
                at_.map += len(jobs)

            def finish(jb, m):
                inv = stats[:, 200 + 4 * (m % 2):204 + 4 * (m % 2)]
                then(V.reciprocal(inv, rowsum[:, m % 4, :]))
                if jb["coef"] == "lam":
                    then(V.tensor_scalar(inv, inv, lam_c, None, ALU.mult))
                elif jb["coef"] is not None:
                    then(V.tensor_tensor(inv, inv, jb["coef"], ALU.mult))
                o = PS[:, 6 + m % O_BANKS, 0:TT * HD].rearrange("p (t d) -> p t d", t=TT)
                by = inv.unsqueeze(2).to_broadcast([P, TT, HD])
                if jb["mode"] == "set":
                    V.tensor_tensor(jb["out"], o, by, ALU.mult)
                    dve.drain().then_inc(out_used, 1)
                else:
                    tmp = (otmp_2 if jb["mode"] == "sub" else otmp_n)[:]
                    V.tensor_tensor(tmp, o, by, ALU.mult)
                    dve.drain().then_inc(out_used, 1)
                    then(V.tensor_tensor(jb["out"], jb["out"], tmp, ALU.add if jb["mode"] == "add" else ALU.subtract))

            V.memset(small[:], EPS)
            dve.wait_ge(const_loaded, 16 * 7)
            dve.wait_ge(cmpw_loaded, 16 * 4)
            posf = stats[:, 0:9]
            V.memset(trig[:].rearrange("p c t f -> p (c t f)"), 0.0)
            dve.drain()
            V.tensor_copy(posf[:, 0:8], posi[:, 0:8])
            then(V.tensor_copy(posf[0:N_CMP, 8:9], posi[0:N_CMP, 8:9]))
            ang = stats[:, 16:16 + TT * N_FREQ].rearrange("p (t f) -> p t f", t=TT)
            turns = stats[:, 120:120 + TT * N_FREQ].rearrange("p (t f) -> p t f", t=TT)
            freq = const("freq")
            for blk, a, n in ((0, 0, MLA_ROPE // 2), (1, MLA_ROPE // 2, ROT // 2)):
                V.tensor_tensor(ang[:, :, a:a + n], posf[:, 4 * blk:4 * blk + 4].unsqueeze(2).to_broadcast([P, TT, n]),
                                freq[:, a:a + n].unsqueeze(1).to_broadcast([P, TT, n]), ALU.mult)
            dve.drain()
            reduce_angles(ang, turns, trig[:, 0, :, :], trig[:, 1, :, :])
            cang, cturns = stats[0:N_CMP, 16:24], stats[0:N_CMP, 120:128]
            then(V.tensor_scalar(cang, freq[0:N_CMP, 0:MLA_ROPE // 2:2], posf[0:N_CMP, 8:9], None, ALU.mult))
            reduce_angles(cang, cturns, ctrig[0:N_CMP, 0, :], ctrig[0:N_CMP, 1, :])
            meet()

            def modulate(slot, n, nth):
                dve.wait_ge(ada_loaded[slot], 16 * nth + 16)
                V.scalar_tensor_tensor(out=junk[:], in0=aux[:, slot, :], scalar=1.0, in1=crow[:], op0=ALU.mult,
                                       op1=ALU.mult, accum_out=mod[:, ds(n, 1)])
                dve.drain().then_inc(ada_used, 1)

            with dve.Fori(0, KD) as i:
                for s in (0, 1):
                    modulate(s, 2 * i + s, i)
            then(V.tensor_tensor(mod[:, 0:2 * KD], mod[:, 0:2 * KD], col("ada_b", 0, 2 * KD), ALU.add))
            sh1, sc1, gt1, sh2, sc2, gt2 = (mod[:, KD * i:KD * i + KD] for i in range(N_MOD))
            then(V.scalar_tensor_tensor(out=sc1, in0=sc1, scalar=1.0, in1=col("norm1", 0, KD), op0=ALU.add,
                                        op1=ALU.mult))
            norm(t1, h_hi, h_lo, sc1, sh1)
            with dve.Fori(KD, N_ADA // 2) as i:
                for s in (0, 1):
                    modulate(s, 2 * i + s, i)
            then(V.tensor_tensor(mod[:, 2 * KD:], mod[:, 2 * KD:], col("ada_b", 2 * KD, 4 * KD), ALU.add))
            then(V.scalar_tensor_tensor(out=sc2, in0=sc2, scalar=1.0, in1=col("norm2", 0, KD), op0=ALU.add,
                                        op1=ALU.mult))
            meet()
            if stop <= 2:
                return
            src = z[:, 1, :, 0:256].rearrange("p t (i d) -> p t i d", i=4)
            for dup in (0, 1):
                V.tensor_copy(c_stage[:, :, :, dup, :], src)
            meet()
            turn_counted(cmp_turns)
            meet()
            for kv in (0, 1):
                for half in (0, 1):
                    ps_ = slice(64 * half, 64 * half + 64)
                    for g in range(GROUPS):
                        v = c_kT[ps_, 2 * kv + g, :].rearrange("p (n m two) -> p m n two", m=8, two=2)
                        for mh in (0, 1):
                            V.tensor_tensor(flat[ps_, 8 * mh:8 * mh + 8, g, :], v[:, :, mh:mh + N_CMP, half],
                                            cmpp[ps_, kv, 8 * mh:8 * mh + 8].unsqueeze(2)
                                            .to_broadcast([64, 8, N_CMP]), ALU.add)
                meet(5)
            meet()
            V.tensor_reduce(out=stats[:, 0:32], in_=n_sq[:].rearrange("p (a d) -> p a d", d=HD), op=ALU.add, axis=AX.X)
            V.tensor_reduce(out=stats[:, 32:48], in_=n_sq2[:].rearrange("p a (b d) -> p (a b) d", d=HD), op=ALU.add,
                            axis=AX.X)
            V.tensor_reduce(out=stats[0:N_CMP, 48:50], in_=c_sq[0:N_CMP, :].rearrange("p (a d) -> p a d", d=HD),
                            op=ALU.add, axis=AX.X)
            meet(2)
            V.reciprocal(stats[:, 0:48], stats[:, 0:48])
            then(V.reciprocal(stats[0:N_CMP, 48:50], stats[0:N_CMP, 48:50]))
            qv = z[:, 0, :, :].rearrange("p t (h d) -> p t h d", d=HD)
            ksv = z[:, 1, :, 256:384].rearrange("p t (h d) -> p t h d", d=HD)
            kwv = z_tail[:, :, 0:128].rearrange("p t (h d) -> p t h d", d=HD)
            kcv = c_k[0:N_CMP, :, :].unsqueeze(1)
            cosn, sinn = (trig[:, i, :, 0:MLA_ROPE // 2:2] for i in (0, 1))
            half = ROT // 2
            for x, a, n, gain, c, s in ((qv, 0, 32, "q", cosn, sinn), (ksv, 32, 8, "ks", cosn, sinn),
                                        (kwv, 40, 8, "kw", cosn, sinn),
                                        (kcv, 48, 2, "kc", ctrig[0:N_CMP, 0:1, :], ctrig[0:N_CMP, 1:2, :])):
                pn = x.shape[0]
                scale_heads(x, stats[0:pn, a:a + n], row(gain))
                rotate(x[:, :, :, 0:half], x[:, :, :, half:ROT], c, s, n_rope, n * half)
            meet()
            turn_counted(nsa_turns())
            meet()
            if stop <= 3:
                return
            for g in range(GROUPS):
                meet()
                sv = PS[:, 0, :].rearrange("p (r t n) -> p r t n", r=REP, t=TT)[:, :, :, 0:N_CMP]
                cm = const("cmask").rearrange("p (t n) -> p t n", t=TT)
                mv = c_sm[:, :, :, 0:N_CMP]
                for r in range(REP):
                    V.tensor_tensor(mv[:, r], sv[:, r], cm, ALU.add)
                dve.drain()
                mn = stats[:, 64:80]
                then(V.tensor_reduce(out=mn, in_=mv.rearrange("p r t n -> p (r t) n"), op=ALU.min, axis=AX.X))
                mvf = mv.rearrange("p r t n -> p (r t) n")
                V.tensor_tensor(mvf, mvf, mn.unsqueeze(2).to_broadcast([P, REP * TT, N_CMP]), ALU.subtract)
                meet(2)
                sums = stats[:, 80:96]
                then(V.tensor_reduce(out=sums, in_=c_p[:, :, 0:N_CMP], op=ALU.add, axis=AX.X))
                then(V.reciprocal(sums, sums))
                s3 = sums.rearrange("p (r t) -> p r t", r=REP)
                then(V.tensor_tensor(s3, s3, const("rowvalid").unsqueeze(1).to_broadcast([P, REP, TT]), ALU.mult))
                for r in range(REP):
                    V.tensor_tensor(s3[:, r, :], s3[:, r, :], sigm(g * REP + r, 0), ALU.mult)
                meet(3)
                for r in range(REP):
                    h = g * REP + r
                    o = PS[:, 5 + r // 2, 256 * (r % 2):256 * (r % 2) + 256].rearrange("p (t d) -> p t d", t=TT)
                    V.tensor_tensor(O_nsa[:, :, 64 * h:64 * h + 64], o,
                                    s3[:, r, :].unsqueeze(2).to_broadcast([P, TT, HD]), ALU.mult)
                meet()
            if stop <= 4:
                return
            attend(nsa_jobs, ring_n)
            meet()
            if stop <= 5:
                return
            meet()
            V.tensor_tensor(stats[:, 0:4], stats[:, 0:4], stats[:, 4:8], ALU.add)
            meet(2)
            then(V.reciprocal(stats[:, 0:12], stats[:, 0:12]))
            for tt in range(TT):
                V.tensor_scalar(z[:, 2, tt, :], z[:, 2, tt, :], stats[:, tt:tt + 1], None, ALU.mult)
                V.tensor_scalar(z[:, 3, tt, 0:256], z[:, 3, tt, 0:256], stats[:, tt:tt + 1], None, ALU.mult)
                V.tensor_scalar(z[:, 3, tt, 256:512], z[:, 3, tt, 256:512], stats[:, 8 + tt:9 + tt], None, ALU.mult)
            meet()
            turn_split_low(c_splits)
            meet(2)
            for tt in (2, 3):
                V.tensor_copy(q_m[:, tt, :].rearrange("p (a b) -> p a b", a=2), PS[:, 2 * tt:2 * tt + 2, 0:Q_LORA // 2])
            meet(2)
            for tt in (2, 3):
                V.tensor_copy(kv_m[:, tt, :].rearrange("p (a b) -> p a b", a=2), PS[:, 2 * tt:2 * tt + 2, :])
            meet()
            if stop <= 6:
                return
            V.tensor_copy(k_m[:, :, :, 0:MLA_NOPE],
                          kv_m[:].rearrange("p t (h d) -> p t h d", d=MLA_NOPE + MLA_V)[:, :, :, 0:MLA_NOPE])
            meet(2)
            V.tensor_reduce(out=stats[:, 0:32], in_=m_sq[:].rearrange("p (a d) -> p a d", d=MLA_QK), op=ALU.add,
                            axis=AX.X)
            V.tensor_reduce(out=stats[:, 32:64], in_=m_sq2[:].rearrange("p (a d) -> p a d", d=MLA_QK), op=ALU.add,
                            axis=AX.X)
            meet(2)
            then(V.reciprocal(stats[:, 0:64], stats[:, 0:64]))
            qmv = q_m[:].rearrange("p t (h d) -> p t h d", d=MLA_QK)
            half = MLA_ROPE // 2
            for x, a, gain in ((qmv, 0, "mla_q"), (k_m[:], 32, "mla_k")):
                scale_heads(x, stats[:, a:a + 32], row(gain))
                rotate(x[:, :, :, MLA_NOPE:MLA_NOPE + half], x[:, :, :, MLA_NOPE + half:MLA_QK],
                       trig[:, 0, :, 0:half], trig[:, 1, :, 0:half], m_rope, 32 * half)
            meet()
            turn_counted(mla_turns)
            meet()
            attend(mla_jobs, ring_m)
            meet()
            if stop <= 7:
                return
            norm(t2, g_hi, g_lo, sc1, sh1)
            turn_split_low(om_splits)
            meet(2)
            turn_split_low(on_splits)
            meet(2)
            for k in range(KD):
                V.tensor_tensor(mrg[:, k, :], PS[:, k, :], gate[:, k, :], ALU.mult)
            meet(2)
            for k in range(KD):
                then(V.tensor_tensor(mtmp[:, k % 2, :], PS[:, k, :], gate[:, KD + k, :], ALU.mult))
                V.tensor_tensor(mrg[:, k, :], mrg[:, k, :], mtmp[:, k % 2, :], ALU.add).then_inc(part_ready, 1)
            dve.drain()
            low_parts(mrg, m_hi, m_lo)
            meet(2)
            for k in range(KD):
                V.scalar_tensor_tensor(out=xT[:, k, :], in0=PS[:, k, :], scalar=gt1[:, k:k + 1], in1=xT[:, k, :],
                                       op0=ALU.mult, op1=ALU.add)
            meet()
            if stop <= 8:
                return

            def mlp(layer):
                if layer is None:
                    norm(t3, f_hi, f_lo, sc2, sh2)
                else:
                    norm(t3, f_hi, f_lo, col("ffn", layer * KD, KD))
                f0 = at_.ffn

                def one(i, half, b):
                    f = 4 * i + (2 * half + b)
                    n = 4 * i + (f0 + 2 * half + b + 1)
                    dve.drain()
                    if layer is None:
                        dve.wait_ge(banks_filled, 4 * i + (at_.fill + 2 * half + 2))
                        dve.wait_ge(silu_ready, n)
                        V.tensor_tensor(ta, tsg, PS[:, 4 * half + 2 + b, :], ALU.mult)
                        dve.drain().then_inc(up_drained, 1)
                        dve.drain().then_inc(prod_ready, 1)
                    else:
                        dve.wait_ge(conv_started, 4 * i + (at_.conv + 2 * half + b + 1))
                        for tap in (1, 0):
                            for t, bank, fb in ((tg, 4 * half + b, 0), (tv, 4 * half + 2 + b, FB)):
                                w = COLS["conv_w"][0] + (layer * 3 + tap) * 2 * FB + fb
                                sh = 2 - tap
                                V.scalar_tensor_tensor(out=t[:, sh:], in0=PS[:, bank, 0:SEQ - sh],
                                                       scalar=cols[:, ds(f + w, 1)], in1=t[:, sh:],
                                                       op0=ALU.mult, op1=ALU.add)
                            last = dve.drain()
                        last.then_inc(conv_ready, 1)
                        dve.drain().then_inc(up_drained, 1)
                        dve.wait_ge(silu_ready, n)
                        V.tensor_tensor(ta, tsg, tv, ALU.mult).then_inc(prod_ready, 1)
                    dve.wait_ge(act_hi_ready, n)
                    V.tensor_tensor(a_lo[:, ds(f, 1), :], ta, a_hi[:, ds(f, 1), :].bitcast(f32), ALU.subtract)

                with dve.Fori(0, FB // 4) as i:
                    for half in (0, 1):
                        for b in (0, 1):
                            one(i, half, b)
                for b in (0, 1):
                    one(FB // 4, 0, b)
                at_.fill += N_UP
                at_.ffn += FB
                if layer is not None:
                    at_.conv += FB
                meet(2)
                for k in range(KD):
                    if layer is None:
                        V.scalar_tensor_tensor(out=xT[:, k, :], in0=PS[:, k, :], scalar=gt2[:, k:k + 1],
                                               in1=xT[:, k, :], op0=ALU.mult, op1=ALU.add)
                    else:
                        V.tensor_tensor(xT[:, k, :], xT[:, k, :], PS[:, k, :], ALU.add)
                meet()

            at_.fill = N_IN // 2 + 1 + N_GATE
            mlp(None)
            if stop <= 9:
                return
            dve.wait_ge(strip_loaded, 16)
            for layer in range(LAYERS):
                norm(t4, f_hi, f_lo, col("mix", layer * KD, KD))
                at_.fill += 6
                meet()
                for chunk, a, n, d in ((0, 0, 8, DIFF), (0, 256, 8, DIFF), (1, 256, 4, HD), (2, 0, 4, HD),
                                       (3, 0, 8, HD), (4, 0, 8, HD)):
                    x = z2[:, chunk, :, a:a + n * d].rearrange("p t (h d) -> p t h d", d=d)
                    half, step = d // 8, (2 if d == DIFF else 1)
                    f1 = MLA_ROPE // 2
                    rotate(x[:, :, :, 0:half], x[:, :, :, half:2 * half], trig[:, 0, :, f1:f1 + 8:step],
                           trig[:, 1, :, f1:f1 + 8:step], rope_2, TT * n * half)
                for i, (a, b) in enumerate((("lq1", "lk1"), ("lq2", "lk2"))):
                    then(V.tensor_tensor_reduce(out=otmp_2[:, 0, 0:DIFF], in0=row(a, layer * DIFF, DIFF),
                                                in1=row(b, layer * DIFF, DIFF), scale=1.0, scalar=0.0, op0=ALU.mult,
                                                op1=ALU.add, accum_out=small[:, 4 + i:5 + i]))
                meet()
                turn_counted(two_turns)
                meet()
                then(V.tensor_tensor(lam_c, small[:, 4:5], small[:, 5:6], ALU.subtract))
                then(V.tensor_scalar(lam_c, lam_c, LAM_INIT[layer], None, ALU.add))
                attend(two_jobs, ring_2)
                meet()
                if stop <= 10:
                    return
                meet()
                V.tensor_reduce(out=stats[:, 0:16], in_=sq_2[:].rearrange("p (a d) -> p a d", d=HD), op=ALU.add,
                                axis=AX.X)
                meet(2)
                then(V.reciprocal(stats[:, 0:16], stats[:, 0:16]))
                then(V.tensor_scalar(stats[:, 0:16], stats[:, 0:16], 1.0 - LAM_INIT[layer], None, ALU.mult))
                scale_heads(O2[:, :, 0:256].rearrange("p t (h d) -> p t h d", d=HD), stats[:, 0:16],
                            row("diff", layer * HD, HD))
                meet()
                turn_split_low(o2_splits)
                meet(2)
                for k in range(KD):
                    V.tensor_tensor(xT[:, k, :], xT[:, k, :], PS[:, k, :], ALU.add)
                meet()
                if stop <= 11:
                    return
                mlp(layer)
                if stop <= 12:
                    return
            meet(3)
            then(V.reciprocal(PS[:, 2, :], PS[:, 1, :]))
            then(V.tensor_tensor(t3[:], xT[:], PS[:, 2:3, :].to_broadcast([P, KD, SEQ]), ALU.mult))
            for k in range(KD):
                V.tensor_scalar(t3[:, k, :], t3[:, k, :], col("final", k), None, ALU.mult)
            meet()


def kernel(**inputs):
    import numpy as np
    import concourse.bacc as bacc
    from concourse import mybir
    from concourse.bass_utils import run_bass_kernel_spmd

    arrays = host_arrays({k: np.asarray(v) for k, v in inputs.items()})
    nc = bacc.Bacc("TRN2", target_bir_lowering=False, num_devices=1)
    args = [nc.dram_tensor(n, a.shape, mybir.dt.from_np(a.dtype), kind="ExternalInput").ap()
            for n, a in arrays.items()]
    out = nc.dram_tensor("out_dram", (P, KD, SEQ), mybir.dt.float32, kind="ExternalOutput").ap()
    build(nc, *args, out)
    r = run_bass_kernel_spmd(nc, [arrays], core_ids=[0])
    got = r.results[0]["out_dram"]
    return np.ascontiguousarray(got.transpose(2, 1, 0).reshape(1, SEQ, D_MODEL))


def host_arrays(a):
    def column(v):
        return v.reshape(-1, P).T

    def padded(s):
        s = s.reshape(P, -1)
        return np.concatenate([s, np.zeros((P, SLAB - s.shape[1]), s.dtype)], 1) if s.shape[1] < SLAB else s

    def slabs(w, k, n):
        kk, nn = w.shape[0] // P, w.shape[1] // n
        v = w.reshape(kk // k, k, P, nn, n).transpose(3, 0, 2, 1, 4)
        return [padded(v[c, s]) for c in range(nn) for s in range(kk // k)]

    w = a["w_in"][0]
    edges = np.cumsum([0, Q_LORA, KV_LORA, MLA_ROPE, HEADS * HD] + [GROUPS * HD] * 6 + [3 * HEADS, D_MODEL, D_MODEL])
    cq, ckv, kpe, qn, kc, vc, ks, vs, kw, vw, gn, gm1, gm2 = (w[:, edges[i]:edges[i + 1]] for i in range(13))
    qn = qn.reshape(D_MODEL, GROUPS, REP, HD).transpose(0, 2, 1, 3).reshape(D_MODEL, -1)
    first = np.concatenate([qn, kc, vc, ks, vs, cq, ckv], 1)
    tail = np.concatenate([kw, vw, gn, kpe], 1)

    def up_slabs(wg, wu):
        g, u = slabs(wg, KD, 256), slabs(wu, KD, 256)
        return [s for pair in zip(g, u) for s in pair]

    stream = slabs(first, 4, 512) + slabs(tail, 4, TAIL) + slabs(a["mla_w_q_b"][0], 2, MLA_HEADS * MLA_QK)
    stream += slabs(a["mla_w_kv_b"][0], 2, 1024) + slabs(np.concatenate([gm1, gm2], 1), KD, 256)
    stream += slabs(a["w_o_mla"][0], 2, 1024) + slabs(a["w_o_nsa"][0], 2, 1024) + slabs(a["w_out"][0], 2, 1024)
    stream += up_slabs(a["ffn_w_gate"][0], a["ffn_w_up"][0]) + slabs(a["ffn_w_down"][0], 2, 1024)
    for layer in range(LAYERS):
        stream += slabs(a["w_in_2"][layer], 4, 512) + slabs(a["w_out_2"][layer], 2, 1024)
        stream += up_slabs(a["w_up_2"][layer][:, :D_FF], a["w_up_2"][layer][:, D_FF:])
        stream += slabs(a["w_down_2"][layer], 2, 1024)
    assert len(stream) == N_SLABS

    col_src = {"norm1": a["norm1_gain"], "norm2": a["norm2_gain"], "q_a": a["mla_q_a_gain"],
               "kv_a": a["mla_kv_a_gain"], "mix": a["g_mix_2"], "ffn": a["g_ffn_2"], "final": a["g_final_2"],
               "ada_b": a["ada_b"], "conv_w": a["conv_w_2"], "conv_b": a["conv_b_2"]}
    row_src = {"mla_q": a["mla_q_gain"], "mla_k": a["mla_k_gain"], "q": a["nsa_q_gain"], "kc": a["nsa_kc_gain"],
               "ks": a["nsa_ks_gain"], "kw": a["nsa_kw_gain"], "diff": a["g_diff_2"], "lq1": a["lambda_q1_2"],
               "lk1": a["lambda_k1_2"], "lq2": a["lambda_q2_2"], "lk2": a["lambda_k2_2"]}
    pos, pos2 = a["positions"].reshape(-1), a["positions_2"].reshape(-1)
    cmp_end = np.arange(N_CMP) * CMP_STRIDE + CMP_LEN - 1
    out = {
        "xT": a["x"].reshape(SEQ, KD, P).transpose(2, 1, 0),
        "slabs": np.stack(stream),
        "ada": a["ada_w"][0].T.reshape(N_ADA, P, D_MODEL),
        "c": a["c"].reshape(-1),
        "cols": np.concatenate([column(col_src[n]) for n in COLS], 1),
        "rows": np.concatenate([row_src[n].reshape(-1) for n in ROWS]),
        "consts": shape_constants(),
        "strips": mask_strips(),
        "pos": np.concatenate([column(pos), column(pos2)], 1).astype(np.int32),
        "cpos": pos[cmp_end].reshape(-1, 1).astype(np.int32),
        "cmpw": np.stack([a[n][0].reshape(CMP_CHUNKS, P, CMP_HIDDEN).transpose(1, 0, 2)
                          for n in ("cmp_w1_k", "cmp_w1_v")], 1),
        "cmpp": np.stack([a[n][0].reshape(CMP_CHUNKS, P).T for n in ("cmp_pos_k", "cmp_pos_v")], 1),
        "cmpw2": np.stack([a[n][0].reshape(2, P, HD).transpose(1, 0, 2) for n in ("cmp_w2_k", "cmp_w2_v")], 1),
    }
    return {f"{k}_dram": np.ascontiguousarray(v) for k, v in out.items()}


def mask_strips():
    dist = np.arange(P)[:, None] - (np.arange(SEQ)[None, :] - (SEQ - P))
    window = np.where((dist >= 0) & (dist < WINDOW), 0.0, NEG)
    count = (dist <= 128).astype(int) + (dist % 4 == 0) + (dist % 16 == 0)
    dilated = np.where((dist >= 0) & (count > 0), -np.log(np.maximum(count, 1)), NEG)
    return np.stack([window, dilated]).astype(np.float32)


def shape_constants():
    token = np.arange(SEQ).reshape(TT, P).T
    ends = np.arange(N_CMP) * CMP_STRIDE + CMP_LEN - 1
    dist = np.arange(P)[:, None] - (np.arange(SEQ)[None, :] - (SEQ - P))
    freq = np.concatenate([THETA ** (-np.arange(0, MLA_ROPE, 2) / MLA_ROPE), THETA ** (-np.arange(0, ROT, 2) / ROT)])
    parts = {"ident": np.eye(P), "mean": np.full((P, P), 1.0 / D_MODEL),
             "freq": np.broadcast_to(freq, (P, N_FREQ)), "rowvalid": token >= ends[0],
             "cmask": np.where(ends <= token[:, :, None], 0.0, NEG).reshape(P, -1),
             "causal": np.where(dist >= 0, 0.0, NEG)}
    return np.concatenate([np.asarray(parts[n], np.float32) for n in CONSTS], 1)
```

```python
import math
from contextlib import ExitStack

import numpy as np

import concourse.bass as bass
from concourse import mybir

D_MODEL, SEQ = 1024, 512
P = 128
KD = D_MODEL // P
TT = SEQ // P
LAYERS = 2
MLA_HEADS, MLA_NOPE, MLA_ROPE, MLA_V = 8, 64, 32, 64
MLA_QK = MLA_NOPE + MLA_ROPE
Q_LORA, KV_LORA = 768, 256
HEADS, GROUPS, HD = 8, 2, 64
REP = HEADS // GROUPS
ROT = HD // 4
CMP_LEN, CMP_STRIDE, CMP_HIDDEN = 32, 16, 256
N_CMP = (SEQ - CMP_LEN) // CMP_STRIDE + 1
CMP_CHUNKS = CMP_LEN * HD // P
WINDOW = 256
D_FF = 2816
FB = D_FF // P
SLAB = 2048
EPS = 1e-6
NEG = 1e30
N_MOD = 6
TAIL = 312
TAIL_VW, TAIL_G, TAIL_PE = 128, 256, 280
THETA = 500000.0
LAM_INIT = [0.8 - 0.6 * math.exp(-0.3 * layer) for layer in range(LAYERS)]
DIFF = 32

N_IN, N_TAIL, N_QB, N_KVB, N_GATE, N_OM, N_ON, N_WOUT = 8, 2, 3, 1, 8, 2, 2, 4
N_UP, N_DOWN, N_IN2 = D_FF // 128, FB // 2, 12
PER_LAYER = N_IN2 + N_WOUT + N_UP + N_DOWN
N_SLABS = (N_IN + N_TAIL + N_QB + N_KVB + N_GATE + N_OM + N_ON + N_WOUT + N_UP + N_DOWN
           + LAYERS * PER_LAYER)
N_ADA = N_MOD * KD

COLS = {}
for _name, _n in (("norm1", KD), ("norm2", KD), ("q_a", Q_LORA // P), ("kv_a", KV_LORA // P),
                  ("mix", LAYERS * KD), ("ffn", LAYERS * KD), ("final", KD), ("ada_b", N_ADA),
                  ("conv_w", LAYERS * 3 * 2 * FB), ("conv_b", LAYERS * 2 * FB)):
    COLS[_name] = sum(n for _, n in COLS.values()), _n
NCOL = sum(n for _, n in COLS.values())
ROWS = {}
for _name, _n in (("mla_q", MLA_QK), ("mla_k", MLA_QK), ("q", HD), ("kc", HD), ("ks", HD), ("kw", HD),
                  ("diff", LAYERS * HD), ("lq1", LAYERS * DIFF), ("lk1", LAYERS * DIFF),
                  ("lq2", LAYERS * DIFF), ("lk2", LAYERS * DIFF)):
    ROWS[_name] = sum(n for _, n in ROWS.values()), _n
NROW = sum(n for _, n in ROWS.values())
N_FREQ = MLA_ROPE // 2 + ROT // 2
CONSTS = {}
for _name, _n in (("ident", P), ("mean", P), ("freq", N_FREQ), ("rowvalid", TT), ("cmask", TT * N_CMP),
                  ("causal", SEQ)):
    CONSTS[_name] = sum(n for _, n in CONSTS.values()), _n
NCONST = sum(n for _, n in CONSTS.values())


def two_pi_parts():
    a = 6.28125
    b = float(np.float32(round((2 * math.pi - a) * 2 ** 20) / 2 ** 20))
    c = float(np.float32(2 * math.pi - a - b))
    return a, b, c


def build(nc, xT_d, slabs_d, ada_d, c_d, cols_d, rows_d, consts_d, strips_d, pos_d, cpos_d,
          cmpw_d, cmpp_d, cmpw2_d, out_d, stop=99):
    f32, f32r, i32 = mybir.dt.float32, mybir.dt.float32r, mybir.dt.int32
    ALU, ACT, AX = mybir.AluOpType, mybir.ActivationFunctionType, mybir.AxisListType
    ds = bass.ds
    ctx = ExitStack()
    with ctx:
        def sb(name, shape, dt=f32):
            return ctx.enter_context(nc.sbuf_tensor(name, shape, dt))

        def sem(name):
            return ctx.enter_context(nc.semaphore(name))

        xT = sb("xT", [P, KD, SEQ])
        raw = sb("raw", [P, 2, SLAB])
        w_hi = sb("w_hi", [P, 2, SLAB], f32r)
        w_lo = sb("w_lo", [P, 2, SLAB], f32r)
        aux = sb("aux", [P, 2, D_MODEL])
        cols = sb("cols", [P, NCOL])
        rows = sb("rows", [P, NROW])
        consts = sb("consts", [P, NCONST])
        strip2 = sb("strip2", [P, SEQ])
        mod = sb("mod", [P, N_ADA])
        trig = sb("trig", [P, 2, TT, N_FREQ])
        ctrig = sb("ctrig", [P, 2, ROT // 2])
        posi = sb("posi", [P, 2 * TT + 1], i32)
        stats = sb("stats", [P, 256])
        small = sb("small", [P, 64])
        zero_c = sb("zero_c", [P, 2])
        negmax = sb("negmax", [P, 8])
        rowsum = sb("rowsum", [P, 4, TT])
        arena_at = -(-nc.sbuf_base // 32) * 32
        arena_size = 122880
        sb("arena", [P, arena_size // 4])

        def at(name, offset, shape, dt=f32):
            n = 4 * int(np.prod(shape[1:]))
            assert offset + n <= arena_size, (name, offset + n)
            return nc.alloc_sbuf_tensor_at(name, shape, dt, offset=arena_at + offset)

        z_tail = at("z_tail", 0, [P, TT, TAIL])
        z = at("z", 4992, [P, 4, TT, 512])
        h_hi = at("h_hi", 37760, [P, KD, SEQ], f32r)
        h_lo = at("h_lo", 54144, [P, KD, SEQ], f32r)
        cmpw = at("cmpw", 70528, [P, 2, CMP_CHUNKS, CMP_HIDDEN])
        t1 = at("t1", 4992, [P, KD + 1, SEQ])
        crow = at("crow", 103296, [P, D_MODEL])
        junk = at("junk", 107392, [P, D_MODEL])
        qT_n = at("qT_n", 37760, [P, 4, SEQ])
        kT_n = at("kT_n", 45952, [P, 2, SEQ])
        ring_n = at("ring_n", 50048, [P, 9, SEQ])
        n_sq = at("n_sq", 50048, [P, HEADS * TT * HD])
        n_rope = at("n_rope", 58240, [P, 4, HEADS * TT * ROT // 2])
        n_sq2 = at("n_sq2", 66432, [P, 2, TT * GROUPS * HD])
        c_sq = at("c_sq", 58240, [P, GROUPS * HD])
        c_stage = at("c_stage", 50048, [P, TT, 4, 2, HD])
        c_kT = at("c_kT", 58240, [P, 4, SEQ])
        flat = at("flat", 111488, [P, CMP_CHUNKS, GROUPS, N_CMP])
        c_sm = at("c_sm", 50048, [P, REP, TT, 32])
        c_p = at("c_p", 52096, [P, REP * TT, 32])
        c_pT = at("c_pT", 54144, [P, REP * TT, P])
        otmp_n = at("otmp_n", 68480, [P, TT, HD])
        O_nsa = at("O_nsa", 103296, [P, TT, HEADS * HD])
        cmpw2 = sb("cmpw2", [P, 2, 2, HD])
        cmpp = sb("cmpp", [P, 2, CMP_CHUNKS])
        c_hid = sb("c_hid", [P, 2, GROUPS * N_CMP])
        c_k = sb("c_k", [P, GROUPS, HD])
        c_v = sb("c_v", [P, GROUPS, HD])
        c_kkT = sb("c_kkT", [P, N_CMP])
        q_m = at("q_m", 4992, [P, TT, MLA_HEADS * MLA_QK])
        ring_m = at("ring_m", 4992, [P, 9, SEQ])
        k_m = at("k_m", 21376, [P, TT, MLA_HEADS, MLA_QK])
        kv_m = at("kv_m", 37760, [P, TT, MLA_HEADS * (MLA_NOPE + MLA_V)])
        m_sq = at("m_sq", 54144, [P, TT * MLA_HEADS * MLA_QK])
        m_sq2 = at("m_sq2", 70528, [P, TT * MLA_HEADS * MLA_QK])
        m_rope = at("m_rope", 54144, [P, 4, TT * MLA_HEADS * MLA_ROPE // 2])
        O_mla = at("O_mla", 54144, [P, TT, MLA_HEADS * MLA_V])
        c_hi = at("c_hi", 70528, [P, KD, SEQ], f32r)
        c_lo = at("c_lo", 86912, [P, KD, SEQ], f32r)
        qT_m = at("qT_m", 70528, [P, MLA_HEADS, SEQ])
        kT_m = at("kT_m", 86912, [P, MLA_HEADS, SEQ])
        gate = at("gate", 0, [P, 2 * KD, SEQ])
        t2 = at("t2", 0, [P, KD + 1, SEQ])
        OmT_hi = at("OmT_hi", 32768, [P, 4, SEQ], f32r)
        OmT_lo = at("OmT_lo", 40960, [P, 4, SEQ], f32r)
        g_hi = at("g_hi", 70528, [P, KD, SEQ], f32r)
        g_lo = at("g_lo", 86912, [P, KD, SEQ], f32r)
        OnT_hi = at("OnT_hi", 70528, [P, 4, SEQ], f32r)
        OnT_lo = at("OnT_lo", 78720, [P, 4, SEQ], f32r)
        mrg = at("mrg", 86912, [P, KD, SEQ])
        m_hi = at("m_hi", 0, [P, KD, SEQ], f32r)
        m_lo = at("m_lo", 16384, [P, KD, SEQ], f32r)
        mtmp = at("mtmp", 49152, [P, 2, SEQ])
        t3 = at("t3", 49152, [P, KD + 1, SEQ])
        f_hi = at("f_hi", 0, [P, KD, SEQ], f32r)
        f_lo = at("f_lo", 16384, [P, KD, SEQ], f32r)
        a_hi = at("a_hi", 32768, [P, FB, SEQ], f32r)
        a_lo = at("a_lo", 77824, [P, FB, SEQ], f32r)
        tg, tv = aux[:, 0, 0:SEQ], aux[:, 0, SEQ:2 * SEQ]
        ta, tsg = aux[:, 1, 0:SEQ], aux[:, 1, SEQ:2 * SEQ]
        z2 = at("z2", 32768, [P, 6, TT, 512])
        t4 = at("t4", 81920, [P, KD + 1, SEQ])
        T2 = at("T2", 0, [P, 16, SEQ])
        ring_2 = at("ring_2", 81920, [P, 9, SEQ])
        rope_2 = at("rope_2", 81920, [P, 4, 512])
        O2 = at("O2", 100352, [P, TT, D_MODEL])
        otmp_2 = at("otmp_2", 120832, [P, TT, HD])
        sq_2 = at("sq_2", 116736, [P, TT * 4 * HD])
        o_hi = at("o_hi", 0, [P, KD, SEQ], f32r)
        o_lo = at("o_lo", 16384, [P, KD, SEQ], f32r)

        PS = ctx.enter_context(nc.psum_tensor("PS", [P, 8, 512], f32))

        def const(name):
            a, n = CONSTS[name]
            return consts[:, a:a + n]

        def col(name, i=0, n=1):
            a = COLS[name][0]
            return cols[:, a + i:a + i + n]

        def row(name, i=0, n=None):
            a, m = ROWS[name]
            return rows[:, a + i:a + i + (n or m)]

        ident, mean_w = const("ident"), const("mean")
        causal = const("causal")
        eps_c, halfpi_c = small[:, 0:1], small[:, 1:2]
        lam_c = small[:, 2:3]

        const_loaded = sem("const_loaded")
        cmpw_loaded = sem("cmpw_loaded")
        strip_loaded = sem("strip_loaded")
        slab_loaded = [sem("slab_loaded0"), sem("slab_loaded1")]
        hi_done, slab_split, slab_used = sem("hi_done"), sem("slab_split"), sem("slab_used")
        zero_ready = sem("zero_ready")
        ada_loaded = [sem("ada_loaded0"), sem("ada_loaded1")]
        ada_used = sem("ada_used")
        arrived = {"pe": sem("pe_arrived"), "act": sem("act_arrived"), "dve": sem("dve_arrived")}
        x_ready, sq_ready, mean_ready, root_ready = sem("x_ready"), sem("sq_ready"), sem("mean_ready"), sem("root_ready")
        part_ready, part_hi, part_low = sem("part_ready"), sem("part_hi"), sem("part_low")
        banks_drained, bank_done, bank_free = sem("banks_drained"), sem("bank_done"), sem("bank_free")
        act_low_ready, rotated, lam_summed = sem("act_low_ready"), sem("rotated"), sem("lam_summed")
        diff_sq, diff_sum, diff_root, diff_ready = sem("diff_sq"), sem("diff_sum"), sem("diff_root"), sem("diff_ready")
        up_drained = sem("up_drained")
        silu_ready, prod_ready, act_hi_ready = sem("silu_ready"), sem("prod_ready"), sem("act_hi_ready")
        conv_started, conv_ready = sem("conv_started"), sem("conv_ready")
        turned = sem("turned")
        turned_act, turned_dve = sem("turned_act"), sem("turned_dve")
        scores_ready, scores_masked, probs_ready = sem("scores_ready"), sem("scores_masked"), sem("probs_ready")
        probsT_ready, copied_act, copied_dve = sem("probsT_ready"), sem("copied_act"), sem("copied_dve")
        pv_done, out_ready, out_used = sem("pv_done"), sem("out_ready"), sem("out_used")
        stored = sem("stored")

        block = ctx.enter_context(nc.Block())
        n_slabs = {2: 10, 3: 10, 4: 10, 5: 10, 6: 14, 7: 14, 8: 30, 9: 63, 10: 75, 11: 79, 12: 112}.get(stop, N_SLABS)

        @block.sync
        def _(sp):
            for dst, src in ((cols[:], cols_d), (rows[:], rows_d.partition_broadcast(P)),
                             (consts[:], consts_d), (strip2[:], strips_d[0]), (posi[:, 0:2 * TT], pos_d),
                             (crow[:], c_d.partition_broadcast(P)),
                             (xT[:], xT_d)):
                sp.dma_start(dst, src).then_inc(const_loaded, 16)

            def load_slab(slot, n):
                src = slabs_d[n] if isinstance(n, int) else slabs_d[ds(n, 1)].rearrange("o p f -> (o p) f")
                sp.dma_start(raw[:, slot, :], src).then_inc(slab_loaded[slot], 16)

            def load_ada(slot, n):
                src = ada_d[n] if isinstance(n, int) else ada_d[ds(n, 1)].rearrange("o p f -> (o p) f")
                sp.dma_start(aux[:, slot, :], src).then_inc(ada_loaded[slot], 16)

            for s in (0, 1):
                load_ada(s, s)
            for s in (0, 1):
                load_slab(s, s)
            with sp.Fori(1, 2 * KD // 2) as i:
                for s in (0, 1):
                    sp.wait_ge(ada_used, 2 * i + (s - 1))
                    load_ada(s, 2 * i + s)
            with sp.Fori(0, 4) as i:
                for s in (0, 1):
                    sp.wait_ge(slab_split, 2 * i + (s + 1))
                    load_slab(s, 2 * i + (s + 2))
                for k in range(8):
                    sp.wait_ge(ada_used, 8 * i + (2 * KD + k - 1))
                    load_ada(k % 2, 8 * i + (2 * KD + k))
            if n_slabs > 11:
              with sp.Fori(5, n_slabs // 2) as i:
                for s in (0, 1):
                    sp.wait_ge(slab_split, 2 * i + (s - 1))
                    load_slab(s, 2 * i + s)
            if n_slabs % 2:
                sp.wait_ge(slab_split, n_slabs - 2)
                load_slab(0, n_slabs - 1)
            if stop == 99:
                first = KD * (4 + 2 * LAYERS)
                for k in range(0, KD, 2):
                    sp.wait_ge(part_ready, first + k + 2)
                    sp.dma_start(out_d[:, k:k + 2, :], t3[:, k:k + 2, :]).then_inc(stored, 16)
                sp.wait_ge(stored, 16 * KD // 2)

        @block.gpsimd
        def _(pool):
            nc.gpsimd.memset(zero_c[:], 0.0).then_inc(zero_ready, 1)
            pool.wait_ge(zero_ready, 1)
            zero = zero_c[:, 0:1].to_broadcast([P, SLAB])

            def split(slot, n, nth, first=False):
                pool.wait_ge(slab_loaded[slot], 16 * nth + 16)
                if not first:
                    pool.wait_ge(slab_used, n - 1)
                nc.gpsimd.tensor_tensor(w_hi[:, slot, :], raw[:, slot, :], zero, ALU.add).then_inc(hi_done, 1)
                pool.wait_ge(hi_done, n + 1)
                nc.gpsimd.tensor_tensor(w_lo[:, slot, :], raw[:, slot, :], w_hi[:, slot, :].bitcast(f32),
                                        ALU.subtract).then_inc(slab_split, 1)

            for s in (0, 1):
                split(s, s, 0, first=True)
            with pool.Fori(1, n_slabs // 2) as i:
                for s in (0, 1):
                    split(s, 2 * i + s, i)
            if n_slabs % 2:
                split(0, n_slabs - 1, n_slabs // 2)

        class Place:

            def __init__(self):
                self.meets = self.slab = self.drain = self.norms = self.bank = 0
                self.tile = self.map = self.acopies = self.dcopies = 0
                self.turn = self.turn_a = self.turn_d = self.part = self.ffn = self.conv = 0
                self.x = self.free = 0

        def meeting(name, eng, at_):
            def meet(n=1):
                for _ in range(n):
                    at_.meets += 1
                    eng.drain().then_inc(arrived[name], 1)
                    for other in ("pe", "act", "dve"):
                        eng.wait_ge(arrived[other], at_.meets)
            return meet

        def slab_view(t, slot, k, n):
            return t[:, slot, 0:k * n].rearrange("p (k n) -> p k n", k=k)

        TURN_LAG, VALUE_LAG, TAKE_LAG = 3, 5, 6
        S_BANKS, PT_BANKS, O_BANKS = 4, 2, 2
        M_SLOTS, P_SLOTS, PT_SLOTS = 2, 4, 3

        FILL = (6, 1, 1, 1, 1)

        def map_tiles(jobs):
            return [(m, j) for m in range(len(jobs)) for j in (3, 0, 2, 1)]

        def masked_slot(ring, u, n):
            return ring[:, u % M_SLOTS, 0:n]

        def probs_slot(ring, u, cols_):
            return ring[:, M_SLOTS + u % P_SLOTS, cols_]

        def turned_slot(ring, u, cols_):
            return ring[:, M_SLOTS + P_SLOTS + u % PT_SLOTS, cols_]

        def last_of_map(u):
            return u % TT == TT - 1

        def key_range(job, j):
            lo = max(0, j - 2) if job["window"] else 0
            return lo, j - lo + 1

        def job(q, k, v, out, strip=None, window=False, coef=None, mode="set"):
            return dict(q=q, k=k, v=v, out=out, strip=strip, window=window, coef=coef, mode=mode)

        def sigm(h, b):
            return z_tail[:, :, TAIL_G + 3 * h + b]

        nsa_jobs = []
        for r in range(REP):
            for g in range(GROUPS):
                h, lo = g * REP + r, 64 * g
                for b, kslot, v in ((1, 0, lambda kb, g=g: z[:, 1, kb, 384 + 64 * g:448 + 64 * g]),
                                    (2, 1, lambda kb, g=g: z_tail[:, kb, TAIL_VW + 64 * g:TAIL_VW + 64 + 64 * g])):
                    nsa_jobs.append(job(qT_n[lo:lo + 64, r, :], kT_n[lo:lo + 64, kslot, :], v,
                                        O_nsa[:, :, 64 * h:64 * h + 64], strip2[:] if b == 2 else causal,
                                        window=b == 2, coef=sigm(h, b), mode="add"))
        mla_jobs = [job(qT_m[0:MLA_QK, h, :], kT_m[0:MLA_QK, h, :],
                        lambda kb, h=h: kv_m[:, kb, 128 * h + 64:128 * h + 128],
                        O_mla[:, :, 64 * h:64 * h + 64], causal) for h in range(MLA_HEADS)]
        two_jobs = []
        for h in range(8):
            lo = 64 * (h % 2)
            two_jobs.append(job(T2[lo:lo + 64, 8 + h // 2, :], T2[lo:lo + 64, 12 + h // 2, :],
                                lambda kb, h=h: z2[:, 5, kb, 64 * h:64 * h + 64],
                                O2[:, :, 64 * h:64 * h + 64], strip2[:]))
        for h in range(4):
            lo = 64 * (h % 2)
            two_jobs.append(job(T2[lo:lo + 64, 4 + h // 2, :], T2[lo:lo + 64, 6 + h // 2, :],
                                lambda kb, h=h: z2[:, 2, kb, 256 + 64 * h:320 + 64 * h],
                                O2[:, :, 512 + 64 * h:576 + 64 * h], causal))
        for h in range(4):
            for c in range(2):
                at0 = (2 * h + c) % 4 * DIFF
                two_jobs.append(job(T2[at0:at0 + DIFF, h // 2, :], T2[at0:at0 + DIFF, 2 + h // 2, :],
                                    lambda kb, h=h: z2[:, 1, kb, 64 * h:64 * h + 64],
                                    O2[:, :, 768 + 64 * h:832 + 64 * h], causal,
                                    coef="lam" if c else None, mode="sub" if c else "set"))

        def nsa_turns():
            out = [(lambda tt, r=r: z[:, 0, tt, 128 * r:128 * r + 128], P, qT_n[:, r, :], -HD ** -0.5)
                   for r in range(REP)]
            out.append((lambda tt: z[:, 1, tt, 256:384], P, kT_n[:, 0, :], 1.0))
            out.append((lambda tt: z_tail[:, tt, 0:128], P, kT_n[:, 1, :], 1.0))
            return out

        cmp_turns = [(lambda tt, i=i: c_stage[:, tt, i, :, :], P, c_kT[:, i, :], 1.0) for i in range(4)]
        mla_turns = []
        for h in range(MLA_HEADS):
            mla_turns.append((lambda tt, h=h: q_m[:, tt, MLA_QK * h:MLA_QK * h + MLA_QK], MLA_QK,
                              qT_m[0:MLA_QK, h, :], -MLA_QK ** -0.5))
            mla_turns.append((lambda tt, h=h: k_m[:, tt, h, :], MLA_QK, kT_m[0:MLA_QK, h, :], 1.0))
        two_turns, two_turn_chunk = [], []
        for slot, (chunk, at0, n, scale) in zip(
                (0, 2, 4, 6, 8, 12),
                ((0, 0, 2, -DIFF ** -0.5), (0, 256, 2, 1.0), (1, 256, 2, -HD ** -0.5), (2, 0, 2, 1.0),
                 (3, 0, 4, -HD ** -0.5), (4, 0, 4, 1.0))):
            for i in range(n):
                two_turns.append((lambda tt, c=chunk, a=at0 + 128 * i: z2[:, c, tt, a:a + 128], P,
                                  T2[:, slot + i, :], scale))
                two_turn_chunk.append(chunk)

        def turn_split(src, hi, lo, n, gains=None):
            return [(lambda tt, i=i: src(tt, i), hi[:, i, :], lo[:, i, :], gains[i] if gains else None)
                    for i in range(n)]

        c_splits = turn_split(lambda tt, i: z[:, 2, tt, 128 * i:128 * i + 128] if i < 4
                              else z[:, 3, tt, 128 * (i - 4):128 * (i - 4) + 128], c_hi, c_lo, 8,
                              [col("q_a", i) for i in range(6)] + [col("kv_a", i) for i in range(2)])
        om_splits = turn_split(lambda tt, i: O_mla[:, tt, 128 * i:128 * i + 128], OmT_hi, OmT_lo, 4)
        on_splits = turn_split(lambda tt, i: O_nsa[:, tt, 128 * i:128 * i + 128], OnT_hi, OnT_lo, 4)
        o2_splits = turn_split(lambda tt, i: O2[:, tt, 128 * i:128 * i + 128], o_hi, o_lo, 8)

        @block.tensor
        def _(pe):
            at_ = Place()
            meet = meeting("pe", pe, at_)

            def three(out, a_hi_, a_lo_, b_hi_, b_lo_, start, stop):
                nc.tensor.matmul(out, a_hi_, b_hi_, start=start, stop=False)
                nc.tensor.matmul(out, a_hi_, b_lo_, start=False, stop=False)
                return nc.tensor.matmul(out, a_lo_, b_hi_, start=False, stop=stop)

            def norm(t):
                for k in range(KD):
                    pe.wait_ge(sq_ready, KD * at_.norms + k + 1)
                    last = nc.tensor.matmul(PS[:, 0, :], mean_w, t[:, k, :], start=k == 0, stop=k == KD - 1)
                last.then_inc(mean_ready, 1)
                at_.norms += 1

            def part_waits(n=KD):
                base = at_.part
                at_.part += n
                return lambda k: pe.wait_ge(part_low, base + k + 1)

            def slab_tokens(slot, hi, lo, k0, nk, n, banks, halves, start, stop, ready=None):
                wh, wl = slab_view(w_hi, slot, nk, n), slab_view(w_lo, slot, nk, n)
                w = n // halves
                for k in range(nk):
                    if ready:
                        ready(k0 + k)
                    for tt in range(TT):
                        ts = slice(128 * tt, 128 * tt + 128)
                        for hf in range(halves):
                            last = three(PS[:, banks + halves * tt + hf, 0:w], hi[:, k0 + k, ts], lo[:, k0 + k, ts],
                                         wh[:, k, w * hf:w * hf + w], wl[:, k, w * hf:w * hf + w],
                                         start and k == 0, stop and k == nk - 1)
                last.then_inc(slab_used, 1)
                return last

            def input_tokens(hi, lo, n_chunks):
                ready = part_waits()

                def two(i, first):
                    for par in (0, 1):
                        if not first:
                            pe.wait_ge(banks_drained, 2 * i + (at_.drain + par - 1))
                        for s in (0, 1):
                            pe.wait_ge(slab_split, 4 * i + (at_.slab + 2 * par + s + 1))
                            slab_tokens((at_.slab + s) % 2, hi, lo, 4 * s, 4, 512, 4 * par, 1, s == 0, s == 1,
                                        ready if first and par == 0 else None)
                two(0, True)
                with pe.Fori(1, n_chunks // 2) as i:
                    two(i, False)
                at_.slab += 2 * n_chunks
                at_.drain += n_chunks

            def slab_features(slot, nk, n, hi_k, lo_k, bank_of, start, stop, ready=None, bank_ready=None,
                              order=None, banks_signal=False):
                wh, wl = slab_view(w_hi, slot, nk, n), slab_view(w_lo, slot, nk, n)
                for k in range(nk):
                    if ready:
                        ready(k)
                    for b in (order if order and k == 0 else range(n // 128)):
                        if bank_ready and k == 0:
                            bank_ready(b)
                        bs = slice(128 * b, 128 * b + 128)
                        last = three(PS[:, bank_of(b), :], wh[:, k, bs], wl[:, k, bs], hi_k(k), lo_k(k),
                                     start and k == 0, stop and k == nk - 1)
                        if banks_signal and k == nk - 1 and b < n // 128 - 1:
                            last.then_inc(bank_done, 1)
                last.then_inc(slab_used, 1)

            def project(hi, lo, n, ready, bank_ready=None):
                for s in range(n):
                    pe.wait_ge(slab_split, at_.slab + 1)
                    slab_features(at_.slab % 2, 2, 1024, lambda k: hi[:, 2 * s + k, :], lambda k: lo[:, 2 * s + k, :],
                                  lambda b: b, s == 0, s == n - 1, ready=lambda k: ready(2 * s + k),
                                  bank_ready=bank_ready if s == 0 else None, banks_signal=s == n - 1)
                    at_.slab += 1

            def project_ffn():
                def bank_ready(b):
                    pe.wait_ge(up_drained, at_.ffn - (2 if b >= 4 else 0))

                def one(slot, n, k0, start, stop):
                    pe.wait_ge(slab_split, n + 1)

                    def part(t, k):
                        kk = k0 + k
                        return (t[:, kk, :] if isinstance(kk, int)
                                else t[:, ds(kk, 1), :].rearrange("p o f -> p (o f)"))
                    slab_features(slot, 2, 1024, lambda k: part(a_hi, k), lambda k: part(a_lo, k),
                                  lambda b: b, start, stop, bank_ready=bank_ready if start else None,
                                  order=(4, 5, 6, 7, 0, 1, 2, 3) if start else None, banks_signal=stop)
                base, par = at_.slab, at_.slab % 2
                pe.wait_ge(act_low_ready, at_.ffn - 2)
                one(par, base, 0, True, False)
                with pe.Fori(0, N_DOWN // 2 - 1) as i:
                    for s in (1, 2):
                        one((par + s) % 2, 2 * i + (base + s), 4 * i + 2 * s, False, False)
                for s in (N_DOWN - 2, N_DOWN - 1):
                    if s == N_DOWN - 1:
                        pe.wait_ge(act_low_ready, at_.ffn)
                    one((par + s) % 2, base + s, 2 * s, False, s == N_DOWN - 1)
                at_.slab += N_DOWN

            def feature_slab_fill(slot, quarter, n, hi, lo, ready=None):
                pe.wait_ge(slab_split, n + 1)
                slab_features(slot, 8, 256, lambda k: hi[:, k, :], lambda k: lo[:, k, :],
                              lambda b: 2 * quarter + b, True, True, ready=ready)

            def gates():
                ready, par = part_waits(), at_.slab % 2
                for q in range(4):
                    if q >= 2:
                        pe.wait_ge(turned_dve, at_.turn_d - (2 if q == 2 else 0))
                    feature_slab_fill((par + q) % 2, q, at_.slab + q, g_hi, g_lo, ready if q == 0 else None)
                for q in range(4):
                    pe.wait_ge(banks_drained, at_.drain + q + 1)
                    feature_slab_fill((par + q) % 2, q, at_.slab + 4 + q, g_hi, g_lo)
                at_.slab += N_GATE
                at_.drain += N_GATE

            def ffn_up():
                base, par, drained = at_.slab, at_.slab % 2, at_.ffn

                ready = part_waits()

                def pair(i, half, guarded):
                    for u in (0, 1):
                        if guarded:
                            pe.wait_ge(up_drained, 4 * i + (drained + 2 * half - 2))
                        feature_slab_fill((par + u) % 2, 2 * half + u, 4 * i + (base + 2 * half + u), f_hi, f_lo,
                                          ready if not guarded and half == u == 0 else None)
                pair(0, 0, False)
                pair(0, 1, False)
                with pe.Fori(1, FB // 4) as i:
                    pair(i, 0, True)
                    pair(i, 1, True)
                pair(FB // 4, 0, True)
                at_.slab += N_UP
                at_.ffn += FB

            def turn(items, split=False, bank0=0, ready=None):
                for n, it in enumerate(items):
                    src, w = it[0], (P if split else it[1])
                    if ready:
                        ready(n)
                    if n >= 8:
                        pe.wait_ge(turned_dve if n % 2 else turned_act,
                                   (at_.turn_d if n % 2 else at_.turn_a) + (n - 8) // 2 + 1)
                    for tt in range(TT):
                        last = nc.tensor.transpose(PS[0:w, (bank0 + n) % 8, 128 * tt:128 * tt + 128], src(tt), ident)
                    last.then_inc(turned, 1)
                at_.turn += len(items)
                at_.turn_a += len(items) if split else (len(items) + 1) // 2
                at_.turn_d += len(items) if split else len(items) // 2

            def release_clock(n):
                for _ in range(n):
                    nc.tensor.matmul(PS[:, 7, :], ident, causal, start=True, stop=True)

            def attend(jobs, ring):
                tiles = map_tiles(jobs)
                g0, m0 = at_.tile, at_.map
                copies = []
                a, d = at_.acopies, at_.dcopies
                for m, j in tiles:
                    if j == TT - 1:
                        d += 1
                        copies.append((copied_dve, d))
                    else:
                        a += 1
                        copies.append((copied_act, a))
                n = len(tiles)
                for step in range(n + VALUE_LAG):
                    if step < n:
                        m, j = tiles[step]
                        lo, nb = key_range(jobs[m], j)
                        if step >= S_BANKS:
                            pe.wait_ge(scores_masked, g0 + step - S_BANKS + 1)
                        nc.tensor.matmul(PS[:, step % S_BANKS, 0:128 * nb], jobs[m]["q"][:, 128 * j:128 * j + 128],
                                         jobs[m]["k"][:, 128 * lo:128 * (lo + nb)], start=True, stop=True
                                         ).then_inc(scores_ready, 1)
                    if TURN_LAG <= step < TURN_LAG + len(FILL):
                        release_clock(FILL[step - TURN_LAG])
                    u = step - TURN_LAG
                    if 0 <= u < n:
                        m, j = tiles[u]
                        lo, nb = key_range(jobs[m], j)
                        pe.wait_ge(probs_ready, g0 + u + 1)
                        if u >= PT_BANKS:
                            pe.wait_ge(*copies[u - PT_BANKS])
                        for b in range(nb):
                            last = nc.tensor.transpose(PS[:, S_BANKS + u % PT_BANKS, 128 * b:128 * b + 128],
                                                       probs_slot(ring, u, slice(128 * b, 128 * b + 128)), ident)
                        last.then_inc(probsT_ready, 1)
                    u = step - VALUE_LAG
                    if 0 <= u < n:
                        m, j = tiles[u]
                        lo, nb = key_range(jobs[m], j)
                        pe.wait_ge(*copies[u])
                        if u % TT == 0 and m >= O_BANKS:
                            pe.wait_ge(out_used, m0 + m - O_BANKS + 1)
                        for b in range(nb):
                            last = nc.tensor.matmul(PS[:, 6 + m % O_BANKS, 64 * j:64 * j + 64],
                                                    turned_slot(ring, u, slice(128 * b, 128 * b + 128)),
                                                    jobs[m]["v"](lo + b), start=b == 0, stop=b == nb - 1)
                        last.then_inc(pv_done, 1)
                at_.tile += n
                at_.map += len(jobs)
                at_.acopies, at_.dcopies = a, d

            meet()
            norm(t1)
            input_tokens(h_hi, h_lo, 4)
            pe.wait_ge(banks_drained, at_.drain - 1)
            for s in (0, 1):
                pe.wait_ge(slab_split, at_.slab + 1)
                slab_tokens(s, h_hi, h_lo, 4 * s, 4, TAIL, 0, 1, s == 0, s == 1)
                at_.slab += 1
            at_.drain += 1
            meet()
            if stop <= 2:
                return
            meet()
            turn(cmp_turns)
            meet()
            for kv in (0, 1):
                meet()
                for hf in (0, 1):
                    for c in range(CMP_CHUNKS):
                        nc.tensor.matmul(PS[:, hf, 0:GROUPS * N_CMP], cmpw[:, kv, c, 128 * hf:128 * hf + 128],
                                         flat[:, c, :, :], start=c == 0, stop=c == CMP_CHUNKS - 1)
                meet(2)
                for g in range(GROUPS):
                    for hf in (0, 1):
                        nc.tensor.matmul(PS[0:N_CMP, 2, HD * g:HD * g + HD], c_hid[:, hf, N_CMP * g:N_CMP * g + N_CMP],
                                         cmpw2[:, kv, hf, :], start=hf == 0, stop=hf == 1)
                meet(2)
            meet(4)
            nc.tensor.transpose(PS[:, 7, 0:N_CMP], c_k[0:N_CMP, :, :].rearrange("p g d -> p (g d)"),
                                ident[0:N_CMP, 0:N_CMP])
            turn(nsa_turns())
            meet()
            if stop <= 3:
                return
            for g in range(GROUPS):
                lo = 64 * g
                for i in range(REP * TT):
                    r, tt = divmod(i, TT)
                    nc.tensor.matmul(PS[:, 0, 32 * i:32 * i + N_CMP], qT_n[lo:lo + 64, r, 128 * tt:128 * tt + 128],
                                     c_kkT[lo:lo + 64, :], start=True, stop=True)
                meet(3)
                for i in range(REP * TT):
                    nc.tensor.transpose(PS[0:N_CMP, 1 + i // 4, 128 * (i % 4):128 * (i % 4) + 128],
                                        c_p[:, i, 0:N_CMP], ident)
                meet(2)
                for i in range(REP * TT):
                    nc.tensor.matmul(PS[:, 5 + i // 8, 64 * (i % 8):64 * (i % 8) + 64], c_pT[0:N_CMP, i, :],
                                     c_v[0:N_CMP, g, :], start=True, stop=True)
                meet(2)
            if stop <= 4:
                return
            attend(nsa_jobs, ring_n)
            meet()
            if stop <= 5:
                return
            meet(4)
            turn(c_splits, split=True)
            meet()
            for s in range(N_QB):
                pe.wait_ge(slab_split, at_.slab + 1)
                slab_tokens(at_.slab % 2, c_hi, c_lo, 2 * s, 2, Q_LORA, 0, 2, s == 0, s == N_QB - 1)
                at_.slab += 1
            meet(2)
            pe.wait_ge(slab_split, at_.slab + 1)
            slab_tokens(at_.slab % 2, c_hi, c_lo, 6, 2, 1024, 0, 2, True, True)
            at_.slab += 1
            meet(2)
            if stop <= 6:
                return
            meet(5)
            turn(mla_turns)
            meet()
            attend(mla_jobs, ring_m)
            meet()
            if stop <= 7:
                return
            norm(t2)
            turn(om_splits, split=True, bank0=4)
            gates()

            def on_bank_ready(n):
                pe.wait_ge(banks_drained, at_.drain - (3 if n < 2 else 2))

            turn(on_splits, split=True, ready=on_bank_ready)
            on_turned = at_.turn_d

            def om_bank_ready(b):
                if b < 4:
                    pe.wait_ge(turned_dve, on_turned - 3 + b)
                else:
                    pe.wait_ge(banks_drained, at_.drain - (1 if b < 6 else 0))

            project(OmT_hi, OmT_lo, N_OM, lambda k: None, om_bank_ready)
            project(OnT_hi, OnT_lo, N_ON, lambda k: None,
                    lambda b: pe.wait_ge(bank_free, at_.free + b + 1))
            project(m_hi, m_lo, N_WOUT, part_waits(),
                    lambda b: pe.wait_ge(bank_free, at_.free + 8 + b + 1))
            at_.free += 16
            if stop <= 8:
                meet()
                return

            def mlp():
                norm(t3)
                ffn_up()
                project_ffn()

            mlp()
            if stop <= 9:
                meet()
                return
            for layer in range(LAYERS):
                norm(t4)
                input_tokens(f_hi, f_lo, 6)

                def two_ready(n):
                    pe.wait_ge(rotated, 5 * layer + two_turn_chunk[n] + 1)
                    if n in (0, 4):
                        pe.wait_ge(banks_drained, at_.drain - (1 if n == 0 else 0))
                turn(two_turns, ready=two_ready)
                meet()
                attend(two_jobs, ring_2)
                meet()
                if stop <= 10:
                    return
                turn(o2_splits, split=True,
                     ready=lambda n: pe.wait_ge(diff_ready, layer + 1) if n == 6 else None)
                base = at_.turn_d - 8
                project(o_hi, o_lo, N_WOUT, lambda k: pe.wait_ge(turned_dve, base + k + 1),
                        lambda b: pe.wait_ge(turned_dve, base + b + 1))
                if stop <= 11:
                    meet()
                    return
                mlp()
                if stop <= 12:
                    meet()
                    return
            norm(t3)
            meet()

        @block.scalar
        def _(act):
            at_ = Place()
            meet = meeting("act", act, at_)
            A = nc.scalar.activation
            for dst, src in ((cmpw[:], cmpw_d), (cmpp[:], cmpp_d), (cmpw2[:], cmpw2_d),
                             (posi[0:N_CMP, TT * 2:TT * 2 + 1], cpos_d)):
                act.dma_start(dst, src).then_inc(cmpw_loaded, 16)

            def norm(t, hi, shift=None, residual=True):
                A(small[:, 8:9], eps_c, ACT.Sqrt)
                for k in range(KD):
                    if residual:
                        act.wait_ge(x_ready, at_.x + k + 1)
                    A(t[:, k, :], xT[:, k, :], ACT.Square).then_inc(sq_ready, 1)
                if residual:
                    at_.x += KD
                at_.norms += 1
                act.wait_ge(mean_ready, at_.norms)
                A(t[:, KD, :], PS[:, 0, :], ACT.Sqrt, bias=eps_c).then_inc(root_ready, 1)
                if hi is not None:
                    high_parts(t, hi, shift)

            def high_parts(t, hi, shift=None):
                for k in range(KD):
                    act.wait_ge(part_ready, at_.part + k + 1)
                    if shift is None:
                        A(hi[:, k, :], t[:, k, :], ACT.Copy).then_inc(part_hi, 1)
                    else:
                        A(hi[:, k, :], t[:, k, :], ACT.Identity, bias=shift[:, k:k + 1]).then_inc(part_hi, 1)
                at_.part += KD

            def evacuate(dst, n_chunks):
                with act.Fori(0, n_chunks // 2) as i:
                    for par in (0, 1):
                        act.wait_ge(slab_used, 4 * i + (at_.slab + 2 * par + 2))
                        A(dst(2 * i + par), PS[:, 4 * par:4 * par + 4, :], ACT.Copy).then_inc(banks_drained, 1)
                at_.slab += 2 * n_chunks

            def turn(items):
                for n, (_, w, dst, scale) in enumerate(items):
                    if n % 2 == 0:
                        act.wait_ge(turned, at_.turn + n + 1)
                        A(dst, PS[0:w, n % 8, :], ACT.Copy, scale=scale).then_inc(turned_act, 1)
                at_.turn += len(items)

            def turn_split_high(items, bank0=0):
                for n, (_, hi, lo, gain) in enumerate(items):
                    act.wait_ge(turned, at_.turn + n + 1)
                    A(hi, PS[:, (bank0 + n) % 8, :], ACT.Copy, scale=1.0 if gain is None else gain).then_inc(turned_act, 1)
                at_.turn += len(items)

            def root(v, d):
                A(v, v, ACT.Sqrt, scale=1.0 / d, bias=eps_c[0:v.shape[0]])

            def attend(jobs, ring):
                tiles = map_tiles(jobs)
                g0 = at_.tile
                n = len(tiles)
                for step in range(n + TURN_LAG):
                    if step < n:
                        m, j = tiles[step]
                        _, nb = key_range(jobs[m], j)
                        act.wait_ge(scores_masked, g0 + step + 1)
                        if step >= P_SLOTS:
                            act.wait_ge(probsT_ready, g0 + step - P_SLOTS + 1)
                        A(probs_slot(ring, step, slice(0, 128 * nb)), masked_slot(ring, step, 128 * nb), ACT.Exp,
                          scale=-1.0,
                          bias=negmax[:, step % 8:step % 8 + 1],
                          accum_out=rowsum[:, m % 4, j:j + 1]).then_inc(probs_ready, 1)
                    u = step - TURN_LAG
                    if u >= 0 and tiles[u][1] != TT - 1:
                        _, nb = key_range(jobs[tiles[u][0]], tiles[u][1])
                        act.wait_ge(probsT_ready, g0 + u + 1)
                        if u >= PT_SLOTS:
                            act.wait_ge(pv_done, g0 + u - PT_SLOTS + 1)
                        A(turned_slot(ring, u, slice(0, 128 * nb)), PS[:, S_BANKS + u % PT_BANKS, 0:128 * nb],
                          ACT.Copy).then_inc(copied_act, 1)
                at_.tile += n

            act.wait_ge(const_loaded, 16 * 7)
            A(crow[:], crow[:], ACT.Silu)
            meet()
            A(trig[:].rearrange("p c t f -> p (c t f)"), trig[:].rearrange("p c t f -> p (c t f)"), ACT.Sin)
            A(ctrig[0:N_CMP, :, :], ctrig[0:N_CMP, :, :], ACT.Sin)
            norm(t1, h_hi, mod[:, 0:KD], residual=False)
            evacuate(lambda c: z[:, ds(c, 1), :, :], 4)
            act.wait_ge(slab_used, at_.slab + N_TAIL)
            A(z_tail[:], PS[:, 0:4, 0:TAIL], ACT.Copy).then_inc(banks_drained, 1)
            at_.slab += N_TAIL
            meet()
            if stop <= 2:
                return
            A(z_tail[:, :, TAIL_G:TAIL_G + 24], z_tail[:, :, TAIL_G:TAIL_G + 24], ACT.Sigmoid)
            meet()
            turn(cmp_turns)
            meet()
            for kv in (0, 1):
                meet(2)
                A(c_hid[:], PS[:, 0:2, 0:GROUPS * N_CMP], ACT.Silu)
                meet(2)
                A((c_v if kv else c_k)[0:N_CMP, :, :].rearrange("p g d -> p (g d)"), PS[0:N_CMP, 2, 0:GROUPS * HD],
                  ACT.Copy)
                meet()
            A(n_sq[:], z[:, 0, :, :].rearrange("p t f -> p (t f)"), ACT.Square)
            A(n_sq2[:, 0, :], z[:, 1, :, 256:384], ACT.Square)
            A(n_sq2[:, 1, :], z_tail[:, :, 0:128], ACT.Square)
            A(c_sq[0:N_CMP, :], c_k[0:N_CMP, :, :].rearrange("p g d -> p (g d)"), ACT.Square)
            meet(2)
            root(stats[:, 0:48], HD)
            root(stats[0:N_CMP, 48:50], HD)
            meet(2)
            turn(nsa_turns())
            A(c_kkT[:], PS[:, 7, 0:N_CMP], ACT.Copy)
            meet()
            if stop <= 3:
                return
            for g in range(GROUPS):
                meet(2)
                A(c_p[:, :, 0:N_CMP], c_sm[:, :, :, 0:N_CMP].rearrange("p r t n -> p (r t) n"), ACT.Exp, scale=-1.0)
                meet(2)
                A(c_pT[0:N_CMP, :, :].rearrange("p i q -> p (i q)"),
                  PS[0:N_CMP, 1:5, :].rearrange("p b f -> p (b f)"), ACT.Copy)
                meet(3)
            if stop <= 4:
                return
            attend(nsa_jobs, ring_n)
            meet()
            if stop <= 5:
                return
            for tt in range(TT):
                A(m_sq[:, 0:512], z[:, 2, tt, :], ACT.Square, accum_out=stats[:, tt:tt + 1])
                act.drain()
                A(m_sq[:, 0:256], z[:, 3, tt, 0:256], ACT.Square, accum_out=stats[:, 4 + tt:5 + tt])
                act.drain()
                A(m_sq[:, 0:256], z[:, 3, tt, 256:512], ACT.Square, accum_out=stats[:, 8 + tt:9 + tt])
                act.drain()
            meet(2)
            root(stats[:, 0:4], Q_LORA)
            root(stats[:, 8:12], KV_LORA)
            meet(2)
            turn_split_high(c_splits)
            meet(2)
            for tt in (0, 1):
                A(q_m[:, tt, :].rearrange("p (a b) -> p a b", a=2), PS[:, 2 * tt:2 * tt + 2, 0:Q_LORA // 2], ACT.Copy)
            meet(2)
            for tt in (0, 1):
                A(kv_m[:, tt, :].rearrange("p (a b) -> p a b", a=2), PS[:, 2 * tt:2 * tt + 2, :], ACT.Copy)
            meet()
            if stop <= 6:
                return
            A(k_m[:, :, :, MLA_NOPE:MLA_QK],
              z_tail[:, :, TAIL_PE:TAIL].unsqueeze(2).to_broadcast([P, TT, MLA_HEADS, MLA_ROPE]), ACT.Copy)
            meet()
            A(m_sq[:], q_m[:].rearrange("p t f -> p (t f)"), ACT.Square)
            A(m_sq2[:], k_m[:].rearrange("p t h d -> p (t h d)"), ACT.Square)
            meet(2)
            root(stats[:, 0:64], MLA_QK)
            meet(2)
            turn(mla_turns)
            meet()
            attend(mla_jobs, ring_m)
            meet()
            if stop <= 7:
                return
            at_.slab += N_QB + N_KVB
            norm(t2, g_hi, mod[:, 0:KD], residual=False)
            turn_split_high(om_splits, bank0=4)
            for q in range(N_GATE):
                act.wait_ge(slab_used, at_.slab + q + 1)
                A(gate[:, 2 * q:2 * q + 2, :], PS[:, 2 * (q % 4):2 * (q % 4) + 2, :],
                  ACT.Sigmoid).then_inc(banks_drained, 1)
            turn_split_high(on_splits)
            high_parts(mrg, m_hi)
            at_.slab += N_GATE + N_OM + N_ON + N_WOUT
            if stop <= 8:
                meet()
                return

            def mlp(layer):
                norm(t3, f_hi, mod[:, 3 * KD:4 * KD] if layer is None else None)
                fill0, f0 = at_.slab, at_.ffn

                def one(i, half, b):
                    f = 4 * i + (2 * half + b)
                    fi = ds(f, 1)
                    if layer is None:
                        act.wait_ge(slab_used, 4 * i + (fill0 + 2 * half + 1))
                        A(tsg, PS[:, 4 * half + b, :], ACT.Silu).then_inc(silu_ready, 1)
                    else:
                        act.wait_ge(slab_used, 4 * i + (fill0 + 2 * half + 2))
                        for t, bank, fb in ((tg, 4 * half + b, 0), (tv, 4 * half + 2 + b, FB)):
                            w = COLS["conv_w"][0] + (layer * 3 + 2) * 2 * FB + fb
                            c = COLS["conv_b"][0] + layer * 2 * FB + fb
                            last = A(t, PS[:, bank, :], ACT.Identity, scale=cols[:, ds(f + w, 1)],
                                     bias=cols[:, ds(f + c, 1)])
                        last.then_inc(conv_started, 1)
                        act.wait_ge(conv_ready, 4 * i + (at_.conv + 2 * half + b + 1))
                        A(tsg, tg, ACT.Silu).then_inc(silu_ready, 1)
                    act.wait_ge(prod_ready, 4 * i + (f0 + 2 * half + b + 1))
                    A(a_hi[:, fi, :], ta, ACT.Copy).then_inc(act_hi_ready, 1)

                with act.Fori(0, FB // 4) as i:
                    for half in (0, 1):
                        for b in (0, 1):
                            one(i, half, b)
                for b in (0, 1):
                    one(FB // 4, 0, b)
                at_.slab += N_UP + N_DOWN
                at_.ffn += FB
                if layer is not None:
                    at_.conv += FB

            mlp(None)
            if stop <= 9:
                meet()
                return
            act.dma_start(strip2[:], strips_d[1]).then_inc(strip_loaded, 16)
            for layer in range(LAYERS):
                norm(t4, f_hi)
                evacuate(lambda c: z2[:, ds(c, 1), :, :], 6)
                act.wait_ge(lam_summed, layer + 1)
                A(small[:, 4:6], small[:, 4:6], ACT.Exp)
                turn(two_turns)
                meet()
                attend(two_jobs, ring_2)
                meet()
                if stop <= 10:
                    return
                A(sq_2[:], O2[:, :, 768:1024], ACT.Square).then_inc(diff_sq, 1)
                turn_split_high(o2_splits[0:2])
                act.wait_ge(diff_sum, layer + 1)
                A(stats[:, 0:16], stats[:, 0:16], ACT.Sqrt, scale=1.0 / HD, bias=eps_c).then_inc(diff_root, 1)
                turn_split_high(o2_splits[2:8], bank0=2)
                at_.slab += N_WOUT
                if stop <= 11:
                    meet()
                    return
                mlp(layer)
                if stop <= 12:
                    meet()
                    return
            norm(t3, None)
            meet()

        @block.vector
        def _(dve):
            at_ = Place()
            meet = meeting("dve", dve, at_)
            V = nc.vector

            def then(_ins):
                dve.drain()

            def low_part(k, t, hi, lo, shift=None):
                dve.wait_ge(part_hi, at_.part + k + 1)
                if shift is None:
                    V.tensor_tensor(lo[:, k, :], t[:, k, :], hi[:, k, :].bitcast(f32), ALU.subtract
                                    ).then_inc(part_low, 1)
                else:
                    V.scalar_tensor_tensor(out=lo[:, k, :], in0=t[:, k, :], scalar=shift[:, k:k + 1],
                                           in1=hi[:, k, :].bitcast(f32), op0=ALU.add, op1=ALU.subtract
                                           ).then_inc(part_low, 1)

            def norm(t, hi, lo, scale, shift=None):
                at_.norms += 1
                dve.wait_ge(root_ready, at_.norms)
                then(V.reciprocal(t[:, KD, :], t[:, KD, :]))
                for k in range(KD + 1):
                    if k < KD:
                        V.scalar_tensor_tensor(out=t[:, k, :], in0=xT[:, k, :], scalar=scale[:, k:k + 1],
                                               in1=t[:, KD, :], op0=ALU.mult, op1=ALU.mult
                                               ).then_inc(part_ready, 1)
                    if hi is not None and k > 0:
                        low_part(k - 1, t, hi, lo, shift)
                at_.part += KD

            def banks(use):
                for b in range(8):
                    if b < 7:
                        dve.wait_ge(bank_done, at_.bank + b + 1)
                    else:
                        dve.wait_ge(slab_used, at_.slab)
                    use(b)
                at_.bank += 7

            def residual(n, factor=None):
                at_.slab += n

                def use(k):
                    if factor is None:
                        i_ = V.tensor_tensor(xT[:, k, :], xT[:, k, :], PS[:, k, :], ALU.add)
                    else:
                        i_ = V.scalar_tensor_tensor(out=xT[:, k, :], in0=PS[:, k, :], scalar=factor[:, k:k + 1],
                                                    in1=xT[:, k, :], op0=ALU.mult, op1=ALU.add)
                    i_.then_inc(x_ready, 1)
                banks(use)

            def turn(items):
                for n, (_, w, dst, scale) in enumerate(items):
                    if n % 2:
                        dve.wait_ge(turned, at_.turn + n + 1)
                        V.tensor_scalar(dst, PS[0:w, n % 8, :], scale, None, ALU.mult).then_inc(turned_dve, 1)
                at_.turn += len(items)

            def turn_split_low(items, bank0=0):
                for n, (_, hi, lo, gain) in enumerate(items):
                    dve.wait_ge(turned_act, at_.turn_a + n + 1)
                    V.scalar_tensor_tensor(out=lo, in0=PS[:, (bank0 + n) % 8, :], scalar=1.0 if gain is None else gain,
                                           in1=hi.bitcast(f32), op0=ALU.mult, op1=ALU.subtract
                                           ).then_inc(turned_dve, 1)
                at_.turn += len(items)
                at_.turn_a += len(items)

            def turn_counted(items):
                turn(items)
                at_.turn_a += (len(items) + 1) // 2

            def reduce_angles(ang, k, cosv, sinv):
                magic = 1.5 * 2.0 ** 23
                then(V.tensor_scalar(k, ang, 1.0 / (2 * math.pi), magic, ALU.mult, ALU.add))
                then(V.tensor_scalar(k, k, magic, None, ALU.subtract))
                for part in two_pi_parts():
                    then(V.scalar_tensor_tensor(out=ang, in0=k, scalar=-part, in1=ang, op0=ALU.mult, op1=ALU.add))
                then(V.tensor_scalar(sinv, ang, 3.1415925, -3.1415925, ALU.min, ALU.max))
                then(V.tensor_scalar(k, sinv, -1.0, None, ALU.mult))
                then(V.tensor_tensor(k, k, sinv, ALU.max))
                then(V.tensor_scalar(cosv, k, -1.0, math.pi / 2, ALU.mult, ALU.add))

            def rotate(x1, x2, cosv, sinv, tmp, n):
                shape = list(x1.shape)
                c, s = (v.unsqueeze(2).to_broadcast(shape) for v in (cosv, sinv))
                a, b, e, f = (tmp[0:shape[0], i, 0:n].rearrange("p (t h f) -> p t h f", t=shape[1], h=shape[2])
                              for i in range(4))
                V.tensor_tensor(a, x1, c, ALU.mult)
                V.tensor_tensor(b, x2, s, ALU.mult)
                V.tensor_tensor(e, x2, c, ALU.mult)
                then(V.tensor_tensor(f, x1, s, ALU.mult))
                V.tensor_tensor(x1, a, b, ALU.subtract)
                then(V.tensor_tensor(x2, e, f, ALU.add))

            def scale_heads(x, inv, gain):
                shape = list(x.shape)
                then(V.tensor_tensor(x, x, inv.rearrange("p (t h) -> p t h", t=shape[1]).unsqueeze(3)
                                     .to_broadcast(shape), ALU.mult))
                then(V.tensor_tensor(x, x, gain[0:shape[0]].unsqueeze(1).unsqueeze(1).to_broadcast(shape), ALU.mult))

            def attend(jobs, ring):
                tiles = map_tiles(jobs)
                g0, m0 = at_.tile, at_.map
                n = len(tiles)
                for step in range(n + TAKE_LAG):
                    if step < n:
                        m, j = tiles[step]
                        _, nb = key_range(jobs[m], j)
                        dve.wait_ge(scores_ready, g0 + step + 1)
                        if step >= M_SLOTS:
                            dve.wait_ge(probs_ready, g0 + step - M_SLOTS + 1)
                        V.tensor_tensor_reduce(out=masked_slot(ring, step, 128 * nb),
                                               in0=PS[:, step % S_BANKS, 0:128 * nb],
                                               in1=jobs[m]["strip"][:, SEQ - 128 * nb:SEQ], scale=1.0, scalar=NEG,
                                               op0=ALU.add, op1=ALU.min,
                                               accum_out=negmax[:, step % 8:step % 8 + 1]).then_inc(scores_masked, 1)
                    u = step - TURN_LAG
                    if 0 <= u < n and tiles[u][1] == TT - 1:
                        _, nb = key_range(jobs[tiles[u][0]], tiles[u][1])
                        dve.wait_ge(probsT_ready, g0 + u + 1)
                        if u >= PT_SLOTS:
                            dve.wait_ge(pv_done, g0 + u - PT_SLOTS + 1)
                        V.tensor_copy(turned_slot(ring, u, slice(0, 128 * nb)),
                                      PS[:, S_BANKS + u % PT_BANKS, 0:128 * nb]).then_inc(copied_dve, 1)
                    u = step - TAKE_LAG
                    if u >= 0 and last_of_map(u):
                        m = tiles[u][0]
                        dve.wait_ge(pv_done, g0 + u + 1)
                        finish(jobs[m], m)
                at_.tile += n
                at_.map += len(jobs)

            def finish(jb, m):
                inv = stats[:, 200 + 4 * (m % 2):204 + 4 * (m % 2)]
                then(V.reciprocal(inv, rowsum[:, m % 4, :]))
                if jb["coef"] == "lam":
                    then(V.tensor_scalar(inv, inv, lam_c, None, ALU.mult))
                elif jb["coef"] is not None:
                    then(V.tensor_tensor(inv, inv, jb["coef"], ALU.mult))
                o = PS[:, 6 + m % O_BANKS, 0:TT * HD].rearrange("p (t d) -> p t d", t=TT)
                by = inv.unsqueeze(2).to_broadcast([P, TT, HD])
                if jb["mode"] == "set":
                    V.tensor_tensor(jb["out"], o, by, ALU.mult)
                    dve.drain().then_inc(out_used, 1)
                else:
                    tmp = (otmp_2 if jb["mode"] == "sub" else otmp_n)[:]
                    V.tensor_tensor(tmp, o, by, ALU.mult)
                    dve.drain().then_inc(out_used, 1)
                    then(V.tensor_tensor(jb["out"], jb["out"], tmp, ALU.add if jb["mode"] == "add" else ALU.subtract))

            V.memset(small[:], EPS)
            dve.wait_ge(const_loaded, 16 * 7)
            dve.wait_ge(cmpw_loaded, 16 * 4)
            posf = stats[:, 0:9]
            V.memset(trig[:].rearrange("p c t f -> p (c t f)"), 0.0)
            dve.drain()
            V.tensor_copy(posf[:, 0:8], posi[:, 0:8])
            then(V.tensor_copy(posf[0:N_CMP, 8:9], posi[0:N_CMP, 8:9]))
            ang = stats[:, 16:16 + TT * N_FREQ].rearrange("p (t f) -> p t f", t=TT)
            turns = stats[:, 120:120 + TT * N_FREQ].rearrange("p (t f) -> p t f", t=TT)
            freq = const("freq")
            for blk, a, n in ((0, 0, MLA_ROPE // 2), (1, MLA_ROPE // 2, ROT // 2)):
                V.tensor_tensor(ang[:, :, a:a + n], posf[:, 4 * blk:4 * blk + 4].unsqueeze(2).to_broadcast([P, TT, n]),
                                freq[:, a:a + n].unsqueeze(1).to_broadcast([P, TT, n]), ALU.mult)
            dve.drain()
            reduce_angles(ang, turns, trig[:, 0, :, :], trig[:, 1, :, :])
            cang, cturns = stats[0:N_CMP, 16:24], stats[0:N_CMP, 120:128]
            then(V.tensor_scalar(cang, freq[0:N_CMP, 0:MLA_ROPE // 2:2], posf[0:N_CMP, 8:9], None, ALU.mult))
            reduce_angles(cang, cturns, ctrig[0:N_CMP, 0, :], ctrig[0:N_CMP, 1, :])
            meet()

            def modulate(slot, n, nth):
                dve.wait_ge(ada_loaded[slot], 16 * nth + 16)
                V.scalar_tensor_tensor(out=junk[:], in0=aux[:, slot, :], scalar=1.0, in1=crow[:], op0=ALU.mult,
                                       op1=ALU.mult, accum_out=mod[:, ds(n, 1)])
                dve.drain().then_inc(ada_used, 1)

            with dve.Fori(0, KD) as i:
                for s in (0, 1):
                    modulate(s, 2 * i + s, i)
            then(V.tensor_tensor(mod[:, 0:2 * KD], mod[:, 0:2 * KD], col("ada_b", 0, 2 * KD), ALU.add))
            sh1, sc1, gt1, sh2, sc2, gt2 = (mod[:, KD * i:KD * i + KD] for i in range(N_MOD))
            then(V.scalar_tensor_tensor(out=sc1, in0=sc1, scalar=1.0, in1=col("norm1", 0, KD), op0=ALU.add,
                                        op1=ALU.mult))
            norm(t1, h_hi, h_lo, sc1, sh1)
            with dve.Fori(KD, N_ADA // 2) as i:
                for s in (0, 1):
                    modulate(s, 2 * i + s, i)
            then(V.tensor_tensor(mod[:, 2 * KD:], mod[:, 2 * KD:], col("ada_b", 2 * KD, 4 * KD), ALU.add))
            then(V.scalar_tensor_tensor(out=sc2, in0=sc2, scalar=1.0, in1=col("norm2", 0, KD), op0=ALU.add,
                                        op1=ALU.mult))
            meet()
            if stop <= 2:
                return
            src = z[:, 1, :, 0:256].rearrange("p t (i d) -> p t i d", i=4)
            for dup in (0, 1):
                V.tensor_copy(c_stage[:, :, :, dup, :], src)
            meet()
            turn_counted(cmp_turns)
            meet()
            for kv in (0, 1):
                for half in (0, 1):
                    ps_ = slice(64 * half, 64 * half + 64)
                    for g in range(GROUPS):
                        v = c_kT[ps_, 2 * kv + g, :].rearrange("p (n m two) -> p m n two", m=8, two=2)
                        for mh in (0, 1):
                            V.tensor_tensor(flat[ps_, 8 * mh:8 * mh + 8, g, :], v[:, :, mh:mh + N_CMP, half],
                                            cmpp[ps_, kv, 8 * mh:8 * mh + 8].unsqueeze(2)
                                            .to_broadcast([64, 8, N_CMP]), ALU.add)
                meet(5)
            meet()
            V.tensor_reduce(out=stats[:, 0:32], in_=n_sq[:].rearrange("p (a d) -> p a d", d=HD), op=ALU.add, axis=AX.X)
            V.tensor_reduce(out=stats[:, 32:48], in_=n_sq2[:].rearrange("p a (b d) -> p (a b) d", d=HD), op=ALU.add,
                            axis=AX.X)
            V.tensor_reduce(out=stats[0:N_CMP, 48:50], in_=c_sq[0:N_CMP, :].rearrange("p (a d) -> p a d", d=HD),
                            op=ALU.add, axis=AX.X)
            meet(2)
            V.reciprocal(stats[:, 0:48], stats[:, 0:48])
            then(V.reciprocal(stats[0:N_CMP, 48:50], stats[0:N_CMP, 48:50]))
            qv = z[:, 0, :, :].rearrange("p t (h d) -> p t h d", d=HD)
            ksv = z[:, 1, :, 256:384].rearrange("p t (h d) -> p t h d", d=HD)
            kwv = z_tail[:, :, 0:128].rearrange("p t (h d) -> p t h d", d=HD)
            kcv = c_k[0:N_CMP, :, :].unsqueeze(1)
            cosn, sinn = (trig[:, i, :, 0:MLA_ROPE // 2:2] for i in (0, 1))
            half = ROT // 2
            for x, a, n, gain, c, s in ((qv, 0, 32, "q", cosn, sinn), (ksv, 32, 8, "ks", cosn, sinn),
                                        (kwv, 40, 8, "kw", cosn, sinn),
                                        (kcv, 48, 2, "kc", ctrig[0:N_CMP, 0:1, :], ctrig[0:N_CMP, 1:2, :])):
                pn = x.shape[0]
                scale_heads(x, stats[0:pn, a:a + n], row(gain))
                rotate(x[:, :, :, 0:half], x[:, :, :, half:ROT], c, s, n_rope, n * half)
            meet()
            turn_counted(nsa_turns())
            meet()
            if stop <= 3:
                return
            for g in range(GROUPS):
                meet()
                sv = PS[:, 0, :].rearrange("p (r t n) -> p r t n", r=REP, t=TT)[:, :, :, 0:N_CMP]
                cm = const("cmask").rearrange("p (t n) -> p t n", t=TT)
                mv = c_sm[:, :, :, 0:N_CMP]
                for r in range(REP):
                    V.tensor_tensor(mv[:, r], sv[:, r], cm, ALU.add)
                dve.drain()
                mn = stats[:, 64:80]
                then(V.tensor_reduce(out=mn, in_=mv.rearrange("p r t n -> p (r t) n"), op=ALU.min, axis=AX.X))
                mvf = mv.rearrange("p r t n -> p (r t) n")
                V.tensor_tensor(mvf, mvf, mn.unsqueeze(2).to_broadcast([P, REP * TT, N_CMP]), ALU.subtract)
                meet(2)
                sums = stats[:, 80:96]
                then(V.tensor_reduce(out=sums, in_=c_p[:, :, 0:N_CMP], op=ALU.add, axis=AX.X))
                then(V.reciprocal(sums, sums))
                s3 = sums.rearrange("p (r t) -> p r t", r=REP)
                then(V.tensor_tensor(s3, s3, const("rowvalid").unsqueeze(1).to_broadcast([P, REP, TT]), ALU.mult))
                for r in range(REP):
                    V.tensor_tensor(s3[:, r, :], s3[:, r, :], sigm(g * REP + r, 0), ALU.mult)
                meet(3)
                for r in range(REP):
                    h = g * REP + r
                    o = PS[:, 5 + r // 2, 256 * (r % 2):256 * (r % 2) + 256].rearrange("p (t d) -> p t d", t=TT)
                    V.tensor_tensor(O_nsa[:, :, 64 * h:64 * h + 64], o,
                                    s3[:, r, :].unsqueeze(2).to_broadcast([P, TT, HD]), ALU.mult)
                meet()
            if stop <= 4:
                return
            attend(nsa_jobs, ring_n)
            meet()
            if stop <= 5:
                return
            meet()
            V.tensor_tensor(stats[:, 0:4], stats[:, 0:4], stats[:, 4:8], ALU.add)
            meet(2)
            then(V.reciprocal(stats[:, 0:12], stats[:, 0:12]))
            for tt in range(TT):
                V.tensor_scalar(z[:, 2, tt, :], z[:, 2, tt, :], stats[:, tt:tt + 1], None, ALU.mult)
                V.tensor_scalar(z[:, 3, tt, 0:256], z[:, 3, tt, 0:256], stats[:, tt:tt + 1], None, ALU.mult)
                V.tensor_scalar(z[:, 3, tt, 256:512], z[:, 3, tt, 256:512], stats[:, 8 + tt:9 + tt], None, ALU.mult)
            meet()
            turn_split_low(c_splits)
            meet(2)
            for tt in (2, 3):
                V.tensor_copy(q_m[:, tt, :].rearrange("p (a b) -> p a b", a=2), PS[:, 2 * tt:2 * tt + 2, 0:Q_LORA // 2])
            meet(2)
            for tt in (2, 3):
                V.tensor_copy(kv_m[:, tt, :].rearrange("p (a b) -> p a b", a=2), PS[:, 2 * tt:2 * tt + 2, :])
            meet()
            if stop <= 6:
                return
            V.tensor_copy(k_m[:, :, :, 0:MLA_NOPE],
                          kv_m[:].rearrange("p t (h d) -> p t h d", d=MLA_NOPE + MLA_V)[:, :, :, 0:MLA_NOPE])
            meet(2)
            V.tensor_reduce(out=stats[:, 0:32], in_=m_sq[:].rearrange("p (a d) -> p a d", d=MLA_QK), op=ALU.add,
                            axis=AX.X)
            V.tensor_reduce(out=stats[:, 32:64], in_=m_sq2[:].rearrange("p (a d) -> p a d", d=MLA_QK), op=ALU.add,
                            axis=AX.X)
            meet(2)
            then(V.reciprocal(stats[:, 0:64], stats[:, 0:64]))
            qmv = q_m[:].rearrange("p t (h d) -> p t h d", d=MLA_QK)
            half = MLA_ROPE // 2
            for x, a, gain in ((qmv, 0, "mla_q"), (k_m[:], 32, "mla_k")):
                scale_heads(x, stats[:, a:a + 32], row(gain))
                rotate(x[:, :, :, MLA_NOPE:MLA_NOPE + half], x[:, :, :, MLA_NOPE + half:MLA_QK],
                       trig[:, 0, :, 0:half], trig[:, 1, :, 0:half], m_rope, 32 * half)
            meet()
            turn_counted(mla_turns)
            meet()
            attend(mla_jobs, ring_m)
            meet()
            if stop <= 7:
                return
            norm(t2, g_hi, g_lo, sc1, sh1)
            turn_split_low(om_splits, bank0=4)
            turn_split_low(on_splits)
            at_.slab = N_IN + N_TAIL + N_QB + N_KVB + N_GATE + N_OM

            def gate_mla(k):
                V.tensor_tensor(mrg[:, k, :], PS[:, k, :], gate[:, k, :], ALU.mult).then_inc(bank_free, 1)

            def gate_nsa(k):
                then(V.tensor_tensor(mtmp[:, k % 2, :], PS[:, k, :], gate[:, KD + k, :], ALU.mult
                                     ).then_inc(bank_free, 1))
                V.tensor_tensor(mrg[:, k, :], mrg[:, k, :], mtmp[:, k % 2, :], ALU.add).then_inc(part_ready, 1)
            dve.wait_ge(banks_drained, N_IN // 2 + 1 + N_GATE)
            banks(gate_mla)
            at_.slab += N_ON
            banks(gate_nsa)
            for k in range(KD):
                low_part(k, mrg, m_hi, m_lo)
            at_.part += KD
            residual(N_WOUT, gt1)
            if stop <= 8:
                meet()
                return

            def mlp(layer):
                if layer is None:
                    norm(t3, f_hi, f_lo, sc2, sh2)
                else:
                    norm(t3, f_hi, f_lo, col("ffn", layer * KD, KD))
                f0 = at_.ffn

                def one(i, half, b):
                    f = 4 * i + (2 * half + b)
                    n = 4 * i + (f0 + 2 * half + b + 1)
                    dve.drain()
                    if layer is None:
                        dve.wait_ge(slab_used, 4 * i + (at_.slab + 2 * half + 2))
                        dve.wait_ge(silu_ready, n)
                        V.tensor_tensor(ta, tsg, PS[:, 4 * half + 2 + b, :], ALU.mult)
                        dve.drain().then_inc(up_drained, 1)
                        dve.drain().then_inc(prod_ready, 1)
                    else:
                        dve.wait_ge(conv_started, 4 * i + (at_.conv + 2 * half + b + 1))
                        for tap in (1, 0):
                            for t, bank, fb in ((tg, 4 * half + b, 0), (tv, 4 * half + 2 + b, FB)):
                                w = COLS["conv_w"][0] + (layer * 3 + tap) * 2 * FB + fb
                                sh = 2 - tap
                                V.scalar_tensor_tensor(out=t[:, sh:], in0=PS[:, bank, 0:SEQ - sh],
                                                       scalar=cols[:, ds(f + w, 1)], in1=t[:, sh:],
                                                       op0=ALU.mult, op1=ALU.add)
                            last = dve.drain()
                        last.then_inc(conv_ready, 1)
                        dve.drain().then_inc(up_drained, 1)
                        dve.wait_ge(silu_ready, n)
                        V.tensor_tensor(ta, tsg, tv, ALU.mult).then_inc(prod_ready, 1)
                    dve.wait_ge(act_hi_ready, n)
                    V.tensor_tensor(a_lo[:, ds(f, 1), :], ta, a_hi[:, ds(f, 1), :].bitcast(f32), ALU.subtract
                                    ).then_inc(act_low_ready, 1)

                with dve.Fori(0, FB // 4) as i:
                    for half in (0, 1):
                        for b in (0, 1):
                            one(i, half, b)
                for b in (0, 1):
                    one(FB // 4, 0, b)
                at_.slab += N_UP
                at_.ffn += FB
                if layer is not None:
                    at_.conv += FB
                residual(N_DOWN, gt2 if layer is None else None)

            mlp(None)
            if stop <= 9:
                meet()
                return
            for layer in range(LAYERS):
                norm(t4, f_hi, f_lo, col("mix", layer * KD, KD))
                at_.slab += N_IN2
                drained = N_IN // 2 + 1 + N_GATE + 6 * layer
                for chunk, parts in enumerate((((0, 8, DIFF), (256, 8, DIFF)), ((256, 4, HD),), ((0, 4, HD),),
                                               ((0, 8, HD),), ((0, 8, HD),))):
                    dve.wait_ge(banks_drained, drained + chunk + 1)
                    for a, n, d in parts:
                        x = z2[:, chunk, :, a:a + n * d].rearrange("p t (h d) -> p t h d", d=d)
                        half, step = d // 8, (2 if d == DIFF else 1)
                        f1 = MLA_ROPE // 2
                        rotate(x[:, :, :, 0:half], x[:, :, :, half:2 * half], trig[:, 0, :, f1:f1 + 8:step],
                               trig[:, 1, :, f1:f1 + 8:step], rope_2, TT * n * half)
                    dve.drain().then_inc(rotated, 1)
                    if chunk == 3:
                        for i, (a, b) in enumerate((("lq1", "lk1"), ("lq2", "lk2"))):
                            then(V.tensor_tensor_reduce(out=otmp_2[:, 0, 0:DIFF], in0=row(a, layer * DIFF, DIFF),
                                                        in1=row(b, layer * DIFF, DIFF), scale=1.0, scalar=0.0,
                                                        op0=ALU.mult, op1=ALU.add, accum_out=small[:, 4 + i:5 + i]))
                        dve.drain().then_inc(lam_summed, 1)
                turn_counted(two_turns)
                meet()
                then(V.tensor_tensor(lam_c, small[:, 4:5], small[:, 5:6], ALU.subtract))
                then(V.tensor_scalar(lam_c, lam_c, LAM_INIT[layer], None, ALU.add))
                if layer == 0:
                    dve.wait_ge(strip_loaded, 16)
                attend(two_jobs, ring_2)
                meet()
                if stop <= 10:
                    return
                dve.wait_ge(diff_sq, layer + 1)
                V.tensor_reduce(out=stats[:, 0:16], in_=sq_2[:].rearrange("p (a d) -> p a d", d=HD), op=ALU.add,
                                axis=AX.X).then_inc(diff_sum, 1)
                turn_split_low(o2_splits[0:2])
                dve.wait_ge(diff_root, layer + 1)
                then(V.reciprocal(stats[:, 0:16], stats[:, 0:16]))
                then(V.tensor_scalar(stats[:, 0:16], stats[:, 0:16], 1.0 - LAM_INIT[layer], None, ALU.mult))
                scale_heads(O2[:, :, 768:1024].rearrange("p t (h d) -> p t h d", d=HD), stats[:, 0:16],
                            row("diff", layer * HD, HD))
                dve.drain().then_inc(diff_ready, 1)
                turn_split_low(o2_splits[2:8], bank0=2)
                residual(N_WOUT)
                if stop <= 11:
                    meet()
                    return
                mlp(layer)
                if stop <= 12:
                    meet()
                    return
            norm(t3, None, None, col("final", 0, KD))
            meet()


def kernel(**inputs):
    import numpy as np
    import concourse.bacc as bacc
    from concourse import mybir
    from concourse.bass_utils import run_bass_kernel_spmd

    arrays = host_arrays({k: np.asarray(v) for k, v in inputs.items()})
    nc = bacc.Bacc("TRN2", target_bir_lowering=False, num_devices=1)
    args = [nc.dram_tensor(n, a.shape, mybir.dt.from_np(a.dtype), kind="ExternalInput").ap()
            for n, a in arrays.items()]
    out = nc.dram_tensor("out_dram", (P, KD, SEQ), mybir.dt.float32, kind="ExternalOutput").ap()
    build(nc, *args, out)
    r = run_bass_kernel_spmd(nc, [arrays], core_ids=[0])
    got = r.results[0]["out_dram"]
    return np.ascontiguousarray(got.transpose(2, 1, 0).reshape(1, SEQ, D_MODEL))


def host_arrays(a):
    def column(v):
        return v.reshape(-1, P).T

    def padded(s):
        s = s.reshape(P, -1)
        return np.concatenate([s, np.zeros((P, SLAB - s.shape[1]), s.dtype)], 1) if s.shape[1] < SLAB else s

    def slabs(w, k, n):
        kk, nn = w.shape[0] // P, w.shape[1] // n
        v = w.reshape(kk // k, k, P, nn, n).transpose(3, 0, 2, 1, 4)
        return [padded(v[c, s]) for c in range(nn) for s in range(kk // k)]

    w = a["w_in"][0]
    edges = np.cumsum([0, Q_LORA, KV_LORA, MLA_ROPE, HEADS * HD] + [GROUPS * HD] * 6 + [3 * HEADS, D_MODEL, D_MODEL])
    cq, ckv, kpe, qn, kc, vc, ks, vs, kw, vw, gn, gm1, gm2 = (w[:, edges[i]:edges[i + 1]] for i in range(13))
    qn = qn.reshape(D_MODEL, GROUPS, REP, HD).transpose(0, 2, 1, 3).reshape(D_MODEL, -1)
    first = np.concatenate([qn, kc, vc, ks, vs, cq, ckv], 1)
    tail = np.concatenate([kw, vw, gn, kpe], 1)

    def up_slabs(wg, wu):
        g, u = slabs(wg, KD, 256), slabs(wu, KD, 256)
        return [s for pair in zip(g, u) for s in pair]

    def heads_last(w):
        return np.concatenate([w[512:], w[256:512], w[:256]], 0)

    stream = slabs(first, 4, 512) + slabs(tail, 4, TAIL) + slabs(a["mla_w_q_b"][0], 2, MLA_HEADS * MLA_QK)
    stream += slabs(a["mla_w_kv_b"][0], 2, 1024) + slabs(np.concatenate([gm1, gm2], 1), KD, 256)
    stream += slabs(a["w_o_mla"][0], 2, 1024) + slabs(a["w_o_nsa"][0], 2, 1024) + slabs(a["w_out"][0], 2, 1024)
    stream += up_slabs(a["ffn_w_gate"][0], a["ffn_w_up"][0]) + slabs(a["ffn_w_down"][0], 2, 1024)
    for layer in range(LAYERS):
        stream += slabs(a["w_in_2"][layer], 4, 512) + slabs(heads_last(a["w_out_2"][layer]), 2, 1024)
        stream += up_slabs(a["w_up_2"][layer][:, :D_FF], a["w_up_2"][layer][:, D_FF:])
        stream += slabs(a["w_down_2"][layer], 2, 1024)
    assert len(stream) == N_SLABS

    col_src = {"norm1": a["norm1_gain"], "norm2": a["norm2_gain"], "q_a": a["mla_q_a_gain"],
               "kv_a": a["mla_kv_a_gain"], "mix": a["g_mix_2"], "ffn": a["g_ffn_2"], "final": a["g_final_2"],
               "ada_b": a["ada_b"], "conv_w": a["conv_w_2"], "conv_b": a["conv_b_2"]}
    row_src = {"mla_q": a["mla_q_gain"], "mla_k": a["mla_k_gain"], "q": a["nsa_q_gain"], "kc": a["nsa_kc_gain"],
               "ks": a["nsa_ks_gain"], "kw": a["nsa_kw_gain"], "diff": a["g_diff_2"], "lq1": a["lambda_q1_2"],
               "lk1": a["lambda_k1_2"], "lq2": a["lambda_q2_2"], "lk2": a["lambda_k2_2"]}
    pos, pos2 = a["positions"].reshape(-1), a["positions_2"].reshape(-1)
    cmp_end = np.arange(N_CMP) * CMP_STRIDE + CMP_LEN - 1
    out = {
        "xT": a["x"].reshape(SEQ, KD, P).transpose(2, 1, 0),
        "slabs": np.stack(stream),
        "ada": a["ada_w"][0].T.reshape(N_ADA, P, D_MODEL),
        "c": a["c"].reshape(-1),
        "cols": np.concatenate([column(col_src[n]) for n in COLS], 1),
        "rows": np.concatenate([row_src[n].reshape(-1) for n in ROWS]),
        "consts": shape_constants(),
        "strips": mask_strips(),
        "pos": np.concatenate([column(pos), column(pos2)], 1).astype(np.int32),
        "cpos": pos[cmp_end].reshape(-1, 1).astype(np.int32),
        "cmpw": np.stack([a[n][0].reshape(CMP_CHUNKS, P, CMP_HIDDEN).transpose(1, 0, 2)
                          for n in ("cmp_w1_k", "cmp_w1_v")], 1),
        "cmpp": np.stack([a[n][0].reshape(CMP_CHUNKS, P).T for n in ("cmp_pos_k", "cmp_pos_v")], 1),
        "cmpw2": np.stack([a[n][0].reshape(2, P, HD).transpose(1, 0, 2) for n in ("cmp_w2_k", "cmp_w2_v")], 1),
    }
    return {f"{k}_dram": np.ascontiguousarray(v) for k, v in out.items()}


def mask_strips():
    dist = np.arange(P)[:, None] - (np.arange(SEQ)[None, :] - (SEQ - P))
    window = np.where((dist >= 0) & (dist < WINDOW), 0.0, NEG)
    count = (dist <= 128).astype(int) + (dist % 4 == 0) + (dist % 16 == 0)
    dilated = np.where((dist >= 0) & (count > 0), -np.log(np.maximum(count, 1)), NEG)
    return np.stack([window, dilated]).astype(np.float32)


def shape_constants():
    token = np.arange(SEQ).reshape(TT, P).T
    ends = np.arange(N_CMP) * CMP_STRIDE + CMP_LEN - 1
    dist = np.arange(P)[:, None] - (np.arange(SEQ)[None, :] - (SEQ - P))
    freq = np.concatenate([THETA ** (-np.arange(0, MLA_ROPE, 2) / MLA_ROPE), THETA ** (-np.arange(0, ROT, 2) / ROT)])
    parts = {"ident": np.eye(P), "mean": np.full((P, P), 1.0 / D_MODEL),
             "freq": np.broadcast_to(freq, (P, N_FREQ)), "rowvalid": token >= ends[0],
             "cmask": np.where(ends <= token[:, :, None], 0.0, NEG).reshape(P, -1),
             "causal": np.where(dist >= 0, 0.0, NEG)}
    return np.concatenate([np.asarray(parts[n], np.float32) for n in CONSTS], 1)
```

```python
import math
from contextlib import ExitStack

import numpy as np

import concourse.bass as bass
from concourse import mybir

D_MODEL, SEQ = 1024, 512
P = 128
KD = D_MODEL // P
TT = SEQ // P
LAYERS = 2
MLA_HEADS, MLA_NOPE, MLA_ROPE, MLA_V = 8, 64, 32, 64
MLA_QK = MLA_NOPE + MLA_ROPE
Q_LORA, KV_LORA = 768, 256
HEADS, GROUPS, HD = 8, 2, 64
REP = HEADS // GROUPS
ROT = HD // 4
CMP_LEN, CMP_STRIDE, CMP_HIDDEN = 32, 16, 256
N_CMP = (SEQ - CMP_LEN) // CMP_STRIDE + 1
CMP_CHUNKS = CMP_LEN * HD // P
WINDOW = 256
D_FF = 2816
FB = D_FF // P
SLAB = 2048
EPS = 1e-6
NEG = 1e30
N_MOD = 6
TAIL = 312
TAIL_VW, TAIL_G, TAIL_PE = 128, 256, 280
THETA = 500000.0
LAM_INIT = [0.8 - 0.6 * math.exp(-0.3 * layer) for layer in range(LAYERS)]
DIFF = 32

N_IN, N_TAIL, N_QB, N_KVB, N_GATE, N_OM, N_ON, N_WOUT = 8, 2, 3, 1, 8, 2, 2, 4
N_UP, N_DOWN, N_IN2 = D_FF // 128, FB // 2, 12
PER_LAYER = N_IN2 + N_WOUT + N_UP + N_DOWN
N_SLABS = (N_IN + N_TAIL + N_QB + N_KVB + N_GATE + N_OM + N_ON + N_WOUT + N_UP + N_DOWN
           + LAYERS * PER_LAYER)
N_ADA = N_MOD * KD

COLS = {}
for _name, _n in (("norm1", KD), ("norm2", KD), ("q_a", Q_LORA // P), ("kv_a", KV_LORA // P),
                  ("mix", LAYERS * KD), ("ffn", LAYERS * KD), ("final", KD), ("ada_b", N_ADA),
                  ("conv_w", LAYERS * 3 * 2 * FB), ("conv_b", LAYERS * 2 * FB)):
    COLS[_name] = sum(n for _, n in COLS.values()), _n
NCOL = sum(n for _, n in COLS.values())
ROWS = {}
for _name, _n in (("mla_q", MLA_QK), ("mla_k", MLA_QK), ("q", HD), ("kc", HD), ("ks", HD), ("kw", HD),
                  ("diff", LAYERS * HD), ("lq1", LAYERS * DIFF), ("lk1", LAYERS * DIFF),
                  ("lq2", LAYERS * DIFF), ("lk2", LAYERS * DIFF)):
    ROWS[_name] = sum(n for _, n in ROWS.values()), _n
NROW = sum(n for _, n in ROWS.values())
N_FREQ = MLA_ROPE // 2 + ROT // 2
CONSTS = {}
for _name, _n in (("ident", P), ("mean", P), ("freq", N_FREQ), ("rowvalid", TT), ("cmask", TT * N_CMP),
                  ("causal", SEQ)):
    CONSTS[_name] = sum(n for _, n in CONSTS.values()), _n
NCONST = sum(n for _, n in CONSTS.values())


def two_pi_parts():
    a = 6.28125
    b = float(np.float32(round((2 * math.pi - a) * 2 ** 20) / 2 ** 20))
    c = float(np.float32(2 * math.pi - a - b))
    return a, b, c


def build(nc, xT_d, slabs_d, ada_d, c_d, cols_d, rows_d, consts_d, strips_d, pos_d, cpos_d,
          cmpw_d, cmpp_d, cmpw2_d, out_d):
    f32, f32r, i32 = mybir.dt.float32, mybir.dt.float32r, mybir.dt.int32
    ALU, ACT, AX = mybir.AluOpType, mybir.ActivationFunctionType, mybir.AxisListType
    ds = bass.ds
    ctx = ExitStack()
    with ctx:
        def sb(name, shape, dt=f32):
            return ctx.enter_context(nc.sbuf_tensor(name, shape, dt))

        def sem(name):
            return ctx.enter_context(nc.semaphore(name))

        xT = sb("xT", [P, KD, SEQ])
        raw = sb("raw", [P, 2, SLAB])
        w_hi = sb("w_hi", [P, 2, SLAB], f32r)
        w_lo = sb("w_lo", [P, 2, SLAB], f32r)
        aux = sb("aux", [P, 2, D_MODEL])
        cols = sb("cols", [P, NCOL])
        rows = sb("rows", [P, NROW])
        consts = sb("consts", [P, NCONST])
        strip2 = sb("strip2", [P, SEQ])
        mod = sb("mod", [P, N_ADA])
        trig = sb("trig", [P, 2, TT, N_FREQ])
        ctrig = sb("ctrig", [P, 2, ROT // 2])
        posi = sb("posi", [P, 2 * TT + 1], i32)
        stats = sb("stats", [P, 256])
        small = sb("small", [P, 64])
        zero_c = sb("zero_c", [P, 2])
        negmax = sb("negmax", [P, 8])
        rowsum = sb("rowsum", [P, 4, TT])
        arena_at = -(-nc.sbuf_base // 32) * 32
        arena_size = 122880
        sb("arena", [P, arena_size // 4])

        def at(name, offset, shape, dt=f32):
            n = 4 * int(np.prod(shape[1:]))
            assert offset + n <= arena_size, (name, offset + n)
            return nc.alloc_sbuf_tensor_at(name, shape, dt, offset=arena_at + offset)

        z_tail = at("z_tail", 0, [P, TT, TAIL])
        z = at("z", 4992, [P, 4, TT, 512])
        h_hi = at("h_hi", 37760, [P, KD, SEQ], f32r)
        h_lo = at("h_lo", 54144, [P, KD, SEQ], f32r)
        cmpw = at("cmpw", 70528, [P, 2, CMP_CHUNKS, CMP_HIDDEN])
        t1 = at("t1", 4992, [P, KD + 1, SEQ])
        crow = at("crow", 115328, [P, D_MODEL])
        ada_first = at("ada_first", 37760, [P, 2 * KD, D_MODEL])
        qT_n = at("qT_n", 37760, [P, 4, SEQ])
        kT_n = at("kT_n", 45952, [P, 2, SEQ])
        ring_n = at("ring_n", 50048, [P, 9, SEQ])
        n_sq = at("n_sq", 50048, [P, HEADS * TT * HD])
        n_rope = at("n_rope", 37760, [P, 4, HEADS * TT * ROT // 2])
        n_sq2 = at("n_sq2", 66432, [P, 2, TT * GROUPS * HD])
        l_sq = at("l_sq", 41856, [P, 512])
        c_sq = at("c_sq", 58240, [P, GROUPS * HD])
        c_rope = at("c_rope", 59264, [P, 4, GROUPS * ROT // 2])
        c_stage = at("c_stage", 50048, [P, TT, 4, 2, HD])
        c_kT = at("c_kT", 58240, [P, 4, SEQ])
        flat = at("flat", 107392, [P, 2, CMP_CHUNKS, GROUPS, N_CMP])
        c_sm = at("c_sm", 50048, [P, REP, TT, 32])
        c_p = at("c_p", 62336, [P, GROUPS, REP * TT, 32])
        c_pT = at("c_pT", 54144, [P, REP * TT, P])
        otmp_n = at("otmp_n", 68480, [P, TT, HD])
        O_nsa = at("O_nsa", 103296, [P, TT, HEADS * HD])
        cmpw2 = sb("cmpw2", [P, 2, 2, HD])
        cmpp = sb("cmpp", [P, 2, CMP_CHUNKS])
        c_hid = sb("c_hid", [P, 2, GROUPS * N_CMP])
        c_k = sb("c_k", [P, GROUPS, HD])
        c_v = sb("c_v", [P, GROUPS, HD])
        c_kkT = sb("c_kkT", [P, N_CMP])
        q_m = at("q_m", 4992, [P, TT, MLA_HEADS * MLA_QK])
        ring_m = at("ring_m", 4992, [P, 9, SEQ])
        k_m = at("k_m", 21376, [P, TT, MLA_HEADS, MLA_QK])
        kv_m = at("kv_m", 37760, [P, TT, MLA_HEADS * (MLA_NOPE + MLA_V)])
        m_sq = at("m_sq", 54144, [P, TT * MLA_HEADS * MLA_QK])
        mk_sq = at("mk_sq", 86912, [P, TT * MLA_HEADS * MLA_QK])
        m_rope = at("m_rope", 54144, [P, 4, TT * MLA_HEADS * MLA_ROPE // 2])
        O_mla = at("O_mla", 54144, [P, TT, MLA_HEADS * MLA_V])
        c_hi = at("c_hi", 70528, [P, KD, SEQ], f32r)
        c_lo = at("c_lo", 86912, [P, KD, SEQ], f32r)
        qT_m = at("qT_m", 70528, [P, MLA_HEADS, SEQ])
        kT_m = at("kT_m", 86912, [P, MLA_HEADS, SEQ])
        gate = at("gate", 0, [P, 2 * KD, SEQ])
        t2 = at("t2", 0, [P, KD + 1, SEQ])
        OmT_hi = at("OmT_hi", 32768, [P, 4, SEQ], f32r)
        OmT_lo = at("OmT_lo", 40960, [P, 4, SEQ], f32r)
        g_hi = at("g_hi", 70528, [P, KD, SEQ], f32r)
        g_lo = at("g_lo", 86912, [P, KD, SEQ], f32r)
        OnT_hi = at("OnT_hi", 70528, [P, 4, SEQ], f32r)
        OnT_lo = at("OnT_lo", 78720, [P, 4, SEQ], f32r)
        mrg = at("mrg", 86912, [P, KD, SEQ])
        m_hi = at("m_hi", 0, [P, KD, SEQ], f32r)
        m_lo = at("m_lo", 16384, [P, KD, SEQ], f32r)
        mtmp = at("mtmp", 49152, [P, KD, SEQ])
        t3 = at("t3", 49152, [P, KD + 1, SEQ])
        f_hi = at("f_hi", 0, [P, KD, SEQ], f32r)
        f_lo = at("f_lo", 16384, [P, KD, SEQ], f32r)
        a_hi = at("a_hi", 32768, [P, FB, SEQ], f32r)
        a_lo = at("a_lo", 77824, [P, FB, SEQ], f32r)
        tg, tv = aux[:, 0, 0:SEQ], aux[:, 0, SEQ:2 * SEQ]
        ta, tsg = aux[:, 1, 0:SEQ], aux[:, 1, SEQ:2 * SEQ]
        z2 = at("z2", 32768, [P, 6, TT, 512])
        t4 = at("t4", 81920, [P, KD + 1, SEQ])
        T2 = at("T2", 0, [P, 16, SEQ])
        ring_2 = at("ring_2", 81920, [P, 9, SEQ])
        rope_2 = at("rope_2", 81920, [P, 4, 512])
        O2 = at("O2", 100352, [P, TT, D_MODEL])
        otmp_2 = at("otmp_2", 120832, [P, TT, HD])
        sq_2 = at("sq_2", 116736, [P, TT * 4 * HD])
        o_hi = at("o_hi", 0, [P, KD, SEQ], f32r)
        o_lo = at("o_lo", 16384, [P, KD, SEQ], f32r)

        PS = ctx.enter_context(nc.psum_tensor("PS", [P, 8, 512], f32))

        def const(name):
            a, n = CONSTS[name]
            return consts[:, a:a + n]

        def col(name, i=0, n=1):
            a = COLS[name][0]
            return cols[:, a + i:a + i + n]

        def row(name, i=0, n=None):
            a, m = ROWS[name]
            return rows[:, a + i:a + i + (n or m)]

        ident, mean_w = const("ident"), const("mean")
        causal = const("causal")
        eps_c = small[:, 0:1]
        lam_c = small[:, 2:3]

        const_loaded, crow_loaded, x_loaded = sem("const_loaded"), sem("crow_loaded"), sem("x_loaded")
        rest_loaded = sem("rest_loaded")
        ada_first_loaded = [sem(f"ada_first_loaded{q}") for q in range(4)]
        cmpw_loaded = sem("cmpw_loaded")
        strip_loaded = sem("strip_loaded")
        slab_loaded = [sem("slab_loaded0"), sem("slab_loaded1")]
        hi_done, slab_split, slab_used = sem("hi_done"), sem("slab_split"), sem("slab_used")
        zero_ready = sem("zero_ready")
        ada_loaded = [sem("ada_loaded0"), sem("ada_loaded1")]
        ada_used = sem("ada_used")
        arrived = {"pe": sem("pe_arrived"), "act": sem("act_arrived"), "dve": sem("dve_arrived")}
        x_ready, sq_ready, mean_ready, root_ready = sem("x_ready"), sem("sq_ready"), sem("mean_ready"), sem("root_ready")
        pair_ready = sem("pair_ready")
        part_ready, part_hi, part_low = sem("part_ready"), sem("part_hi"), sem("part_low")
        banks_drained, bank_done, bank_free = sem("banks_drained"), sem("bank_done"), sem("bank_free")
        act_low_ready, rotated, lam_summed = sem("act_low_ready"), sem("rotated"), sem("lam_summed")
        diff_sq, diff_sum, diff_root, diff_ready = sem("diff_sq"), sem("diff_sum"), sem("diff_root"), sem("diff_ready")
        up_drained = sem("up_drained")
        silu_ready, prod_ready, act_hi_ready = sem("silu_ready"), sem("prod_ready"), sem("act_hi_ready")
        conv_started, conv_ready = sem("conv_started"), sem("conv_ready")
        heads_sq, heads_sum, heads_root = sem("heads_sq"), sem("heads_sum"), sem("heads_root")
        latents_sq, latents_sum, latents_root = sem("latents_sq"), sem("latents_sum"), sem("latents_root")
        c_scored, c_shifted, c_probs = sem("c_scored"), sem("c_shifted"), sem("c_probs")
        c_turned, c_copied, c_valued = sem("c_turned"), sem("c_copied"), sem("c_valued")
        mla_sq, mla_sum, mla_root, mla_scaled = sem("mla_sq"), sem("mla_sum"), sem("mla_root"), sem("mla_scaled")
        turned = sem("turned")
        turned_act, turned_dve = sem("turned_act"), sem("turned_dve")
        scores_ready, scores_masked, probs_ready = sem("scores_ready"), sem("scores_masked"), sem("probs_ready")
        probsT_ready, copied_act, copied_dve = sem("probsT_ready"), sem("copied_act"), sem("copied_dve")
        pv_done, out_used = sem("pv_done"), sem("out_used")
        stored = sem("stored")

        block = ctx.enter_context(nc.Block())

        @block.sync
        def _(sp):
            def load_first_ada(q):
                sp.dma_start(ada_first[:, 4 * q:4 * q + 4, :], ada_d[4 * q:4 * q + 4].rearrange("c p f -> p c f")
                             ).then_inc(ada_first_loaded[q], 16)

            def load_slab(slot, n):
                src = slabs_d[n] if isinstance(n, int) else slabs_d[ds(n, 1)].rearrange("o p f -> (o p) f")
                sp.dma_start(raw[:, slot, :], src).then_inc(slab_loaded[slot], 16)

            def load_ada(slot, n):
                src = ada_d[n] if isinstance(n, int) else ada_d[ds(n, 1)].rearrange("o p f -> (o p) f")
                sp.dma_start(aux[:, slot, :], src).then_inc(ada_loaded[slot], 16)

            sp.dma_start(crow[:], c_d.partition_broadcast(P)).then_inc(crow_loaded, 16)
            load_first_ada(0)
            sp.dma_start(xT[:], xT_d).then_inc(x_loaded, 16)
            load_first_ada(1)
            for dst, src in ((cols[:], cols_d), (consts[:], consts_d)):
                sp.dma_start(dst, src).then_inc(const_loaded, 16)
            load_first_ada(2)
            load_first_ada(3)
            load_slab(0, 0)
            load_slab(1, 1)
            for dst, src in ((rows[:], rows_d.partition_broadcast(P)), (strip2[:], strips_d[0]),
                             (posi[:, 0:2 * TT], pos_d), (posi[0:N_CMP, TT * 2:TT * 2 + 1], cpos_d),
                             (cmpp[:], cmpp_d), (cmpw2[:], cmpw2_d)):
                sp.dma_start(dst, src).then_inc(rest_loaded, 16)
            for s in (0, 1):
                load_ada(s, 2 * KD + s)

            def two_slabs(i):
                for s in (0, 1):
                    sp.wait_ge(slab_split, 2 * i + (s - 1))
                    load_slab(s, 2 * i + s)

            def some_ada(i, n, m0):
                for k in range(n):
                    sp.wait_ge(ada_used, 4 * i + (m0 + k - 1))
                    load_ada(k % 2, 4 * i + (2 * KD + m0 + k))

            with sp.Fori(1, 4) as i:
                two_slabs(i)
                some_ada(i, 4, -2)
            two_slabs(4)
            some_ada(4, 2, -2)
            gates0 = (N_IN + N_TAIL + N_QB + N_KVB) // 2
            with sp.Fori(5, gates0) as i:
                two_slabs(i)
            with sp.Fori(gates0, gates0 + N_GATE // 2) as i:
                two_slabs(i)
                some_ada(i, 4, 2 * KD - 4 * gates0)
            with sp.Fori(gates0 + N_GATE // 2, N_SLABS // 2) as i:
                two_slabs(i)
            sp.wait_ge(slab_split, N_SLABS - 2)
            load_slab(0, N_SLABS - 1)
            first = KD * (4 + 2 * LAYERS)
            for k in range(0, KD, 2):
                sp.wait_ge(part_ready, first + k + 2)
                sp.dma_start(out_d[:, k:k + 2, :], t3[:, k:k + 2, :]).then_inc(stored, 16)
            sp.wait_ge(stored, 16 * KD // 2)

        @block.gpsimd
        def _(pool):
            nc.gpsimd.memset(zero_c[:], 0.0).then_inc(zero_ready, 1)
            pool.wait_ge(zero_ready, 1)
            zero = zero_c[:, 0:1].to_broadcast([P, SLAB])

            def split(slot, n, nth, first=False):
                pool.wait_ge(slab_loaded[slot], 16 * nth + 16)
                if not first:
                    pool.wait_ge(slab_used, n - 1)
                nc.gpsimd.tensor_tensor(w_hi[:, slot, :], raw[:, slot, :], zero, ALU.add).then_inc(hi_done, 1)
                pool.wait_ge(hi_done, n + 1)
                nc.gpsimd.tensor_tensor(w_lo[:, slot, :], raw[:, slot, :], w_hi[:, slot, :].bitcast(f32),
                                        ALU.subtract).then_inc(slab_split, 1)

            for s in (0, 1):
                split(s, s, 0, first=True)
            with pool.Fori(1, N_SLABS // 2) as i:
                for s in (0, 1):
                    split(s, 2 * i + s, i)
            split(0, N_SLABS - 1, N_SLABS // 2)

        class Place:

            def __init__(self):
                self.meets = self.slab = self.drain = self.norms = self.bank = 0
                self.tile = self.map = self.acopies = self.dcopies = 0
                self.turn = self.turn_a = self.turn_d = self.part = self.ffn = self.conv = 0
                self.x = self.free = self.pairs = 0

        def meeting(name, eng, at_):
            def meet(n=1):
                for _ in range(n):
                    at_.meets += 1
                    eng.drain().then_inc(arrived[name], 1)
                    for other in ("pe", "act", "dve"):
                        eng.wait_ge(arrived[other], at_.meets)
            return meet

        def slab_view(t, slot, k, n):
            return t[:, slot, 0:k * n].rearrange("p (k n) -> p k n", k=k)

        TURN_LAG, VALUE_LAG, TAKE_LAG = 3, 5, 6
        S_BANKS, PT_BANKS, O_BANKS = 4, 2, 2
        M_SLOTS, P_SLOTS, PT_SLOTS = 2, 4, 3

        FILL = (6, 1, 1, 1, 1)

        def map_tiles(jobs):
            return [(m, j) for m in range(len(jobs)) for j in (3, 0, 2, 1)]

        def masked_slot(ring, u, n):
            return ring[:, u % M_SLOTS, 0:n]

        def probs_slot(ring, u, cols_):
            return ring[:, M_SLOTS + u % P_SLOTS, cols_]

        def turned_slot(ring, u, cols_):
            return ring[:, M_SLOTS + P_SLOTS + u % PT_SLOTS, cols_]

        def last_of_map(u):
            return u % TT == TT - 1

        def key_range(job, j):
            lo = max(0, j - 2) if job["window"] else 0
            return lo, j - lo + 1

        def job(q, k, v, out, strip=None, window=False, coef=None, mode="set"):
            return dict(q=q, k=k, v=v, out=out, strip=strip, window=window, coef=coef, mode=mode)

        def sigm(h, b):
            return z_tail[:, :, TAIL_G + 3 * h + b]

        nsa_jobs = []
        for r in range(REP):
            for g in range(GROUPS):
                h, lo = g * REP + r, 64 * g
                for b, kslot, v in ((1, 0, lambda kb, g=g: z[:, 1, kb, 384 + 64 * g:448 + 64 * g]),
                                    (2, 1, lambda kb, g=g: z_tail[:, kb, TAIL_VW + 64 * g:TAIL_VW + 64 + 64 * g])):
                    nsa_jobs.append(job(qT_n[lo:lo + 64, r, :], kT_n[lo:lo + 64, kslot, :], v,
                                        O_nsa[:, :, 64 * h:64 * h + 64], strip2[:] if b == 2 else causal,
                                        window=b == 2, coef=sigm(h, b), mode="add"))
        mla_jobs = [job(qT_m[0:MLA_QK, h, :], kT_m[0:MLA_QK, h, :],
                        lambda kb, h=h: kv_m[:, kb, 128 * h + 64:128 * h + 128],
                        O_mla[:, :, 64 * h:64 * h + 64], causal) for h in range(MLA_HEADS)]
        two_jobs = []
        for h in range(8):
            lo = 64 * (h % 2)
            two_jobs.append(job(T2[lo:lo + 64, 8 + h // 2, :], T2[lo:lo + 64, 12 + h // 2, :],
                                lambda kb, h=h: z2[:, 5, kb, 64 * h:64 * h + 64],
                                O2[:, :, 64 * h:64 * h + 64], strip2[:]))
        for h in range(4):
            lo = 64 * (h % 2)
            two_jobs.append(job(T2[lo:lo + 64, 4 + h // 2, :], T2[lo:lo + 64, 6 + h // 2, :],
                                lambda kb, h=h: z2[:, 2, kb, 256 + 64 * h:320 + 64 * h],
                                O2[:, :, 512 + 64 * h:576 + 64 * h], causal))
        for h in range(4):
            for c in range(2):
                at0 = (2 * h + c) % 4 * DIFF
                two_jobs.append(job(T2[at0:at0 + DIFF, h // 2, :], T2[at0:at0 + DIFF, 2 + h // 2, :],
                                    lambda kb, h=h: z2[:, 1, kb, 64 * h:64 * h + 64],
                                    O2[:, :, 768 + 64 * h:832 + 64 * h], causal,
                                    coef="lam" if c else None, mode="sub" if c else "set"))

        def nsa_turns():
            out = [(lambda tt, r=r: z[:, 0, tt, 128 * r:128 * r + 128], P, qT_n[:, r, :], -HD ** -0.5)
                   for r in range(REP)]
            out.append((lambda tt: z[:, 1, tt, 256:384], P, kT_n[:, 0, :], 1.0))
            out.append((lambda tt: z_tail[:, tt, 0:128], P, kT_n[:, 1, :], 1.0))
            return out

        cmp_turns = [(lambda tt, i=i: c_stage[:, tt, i, :, :], P, c_kT[:, i, :], 1.0) for i in range(4)]
        mla_q_turns, mla_k_turns = [], []
        for h in range(MLA_HEADS):
            mla_q_turns.append((lambda tt, h=h: q_m[:, tt, MLA_QK * h:MLA_QK * h + MLA_QK], MLA_QK,
                              qT_m[0:MLA_QK, h, :], -MLA_QK ** -0.5))
            mla_k_turns.append((lambda tt, h=h: k_m[:, tt, h, :], MLA_QK, kT_m[0:MLA_QK, h, :], 1.0))
        two_turns, two_turn_chunk = [], []
        for slot, (chunk, at0, n, scale) in zip(
                (0, 2, 4, 6, 8, 12),
                ((0, 0, 2, -DIFF ** -0.5), (0, 256, 2, 1.0), (1, 256, 2, -HD ** -0.5), (2, 0, 2, 1.0),
                 (3, 0, 4, -HD ** -0.5), (4, 0, 4, 1.0))):
            for i in range(n):
                two_turns.append((lambda tt, c=chunk, a=at0 + 128 * i: z2[:, c, tt, a:a + 128], P,
                                  T2[:, slot + i, :], scale))
                two_turn_chunk.append(chunk)

        def turn_split(src, hi, lo, n, gains=None):
            return [(lambda tt, i=i: src(tt, i), hi[:, i, :], lo[:, i, :], gains[i] if gains else None)
                    for i in range(n)]

        c_splits = turn_split(lambda tt, i: z[:, 2, tt, 128 * i:128 * i + 128] if i < 4
                              else z[:, 3, tt, 128 * (i - 4):128 * (i - 4) + 128], c_hi, c_lo, 8,
                              [col("q_a", i) for i in range(6)] + [col("kv_a", i) for i in range(2)])
        om_splits = turn_split(lambda tt, i: O_mla[:, tt, 128 * i:128 * i + 128], OmT_hi, OmT_lo, 4)
        on_splits = turn_split(lambda tt, i: O_nsa[:, tt, 128 * i:128 * i + 128], OnT_hi, OnT_lo, 4)
        o2_splits = turn_split(lambda tt, i: O2[:, tt, 128 * i:128 * i + 128], o_hi, o_lo, 8)

        @block.tensor
        def _(pe):
            at_ = Place()
            meet = meeting("pe", pe, at_)

            def three(out, a_hi_, a_lo_, b_hi_, b_lo_, start, stop):
                nc.tensor.matmul(out, a_hi_, b_hi_, start=start, stop=False)
                nc.tensor.matmul(out, a_hi_, b_lo_, start=False, stop=False)
                return nc.tensor.matmul(out, a_lo_, b_hi_, start=False, stop=stop)

            def norm(t, residual=True):
                ks = (1, 3, 6, 7, 5) if residual else range(KD)
                for k in ks:
                    if residual and k < 6:
                        pe.wait_ge(pair_ready, at_.pairs + 1)
                        at_.pairs += 1
                    else:
                        pe.wait_ge(sq_ready, KD * at_.norms + k + 1)
                    last = nc.tensor.matmul(PS[:, 0, :], mean_w, t[:, k, :], start=k == ks[0], stop=k == ks[-1])
                last.then_inc(mean_ready, 1)
                at_.norms += 1

            def part_waits(n=KD):
                base = at_.part
                at_.part += n
                return lambda k: pe.wait_ge(part_low, base + k + 1)

            def slab_tokens(slot, hi, lo, k0, nk, n, banks, halves, start, stop, ready=None,
                            banks_ready=None):
                wh, wl = slab_view(w_hi, slot, nk, n), slab_view(w_lo, slot, nk, n)
                w = n // halves
                for k in range(nk):
                    if ready:
                        ready(k0 + k)
                    for tt in range(TT):
                        ts = slice(128 * tt, 128 * tt + 128)
                        if banks_ready and k == 0:
                            banks_ready(tt)
                        for hf in range(halves):
                            last = three(PS[:, banks + halves * tt + hf, 0:w], hi[:, k0 + k, ts], lo[:, k0 + k, ts],
                                         wh[:, k, w * hf:w * hf + w], wl[:, k, w * hf:w * hf + w],
                                         start and k == 0, stop and k == nk - 1)
                last.then_inc(slab_used, 1)
                return last

            def input_tokens(hi, lo, n_chunks):
                ready = part_waits()

                def two(i, first):
                    for par in (0, 1):
                        if not first:
                            pe.wait_ge(banks_drained, 2 * i + (at_.drain + par - 1))
                        for s in (0, 1):
                            pe.wait_ge(slab_split, 4 * i + (at_.slab + 2 * par + s + 1))
                            slab_tokens((at_.slab + s) % 2, hi, lo, 4 * s, 4, 512, 4 * par, 1, s == 0, s == 1,
                                        ready if first and par == 0 else None)
                two(0, True)
                with pe.Fori(1, n_chunks // 2) as i:
                    two(i, False)
                at_.slab += 2 * n_chunks
                at_.drain += n_chunks

            def slab_features(slot, nk, n, hi_k, lo_k, bank_of, start, stop, ready=None, bank_ready=None,
                              order=None, banks_signal=False):
                wh, wl = slab_view(w_hi, slot, nk, n), slab_view(w_lo, slot, nk, n)
                steps = ([(k, b) for b in order for k in range(nk)] if order
                         else [(k, b) for k in range(nk) for b in range(n // 128)])
                for k, b in steps:
                    if ready and b == 0:
                        ready(k)
                    if bank_ready and k == 0:
                        bank_ready(b)
                    bs = slice(128 * b, 128 * b + 128)
                    last = three(PS[:, bank_of(b), :], wh[:, k, bs], wl[:, k, bs], hi_k(k), lo_k(k),
                                 start and k == 0, stop and k == nk - 1)
                    if banks_signal and k == nk - 1 and b < n // 128 - 1:
                        last.then_inc(bank_done, 1)
                last.then_inc(slab_used, 1)

            def project(hi, lo, n, ready, bank_ready=None):
                for s in range(n):
                    pe.wait_ge(slab_split, at_.slab + 1)
                    slab_features(at_.slab % 2, 2, 1024, lambda k: hi[:, 2 * s + k, :], lambda k: lo[:, 2 * s + k, :],
                                  lambda b: b, s == 0, s == n - 1, ready=lambda k: ready(2 * s + k),
                                  bank_ready=bank_ready if s == 0 else None, banks_signal=s == n - 1)
                    at_.slab += 1

            def project_ffn():
                def bank_ready(b):
                    pe.wait_ge(up_drained, at_.ffn - (2 if b >= 4 else 1 - b % 2))

                def one(slot, n, k0, start, stop):
                    pe.wait_ge(slab_split, n + 1)

                    def part(t, k):
                        kk = k0 + k
                        return (t[:, kk, :] if isinstance(kk, int)
                                else t[:, ds(kk, 1), :].rearrange("p o f -> p (o f)"))
                    slab_features(slot, 2, 1024, lambda k: part(a_hi, k), lambda k: part(a_lo, k),
                                  lambda b: b, start, stop, bank_ready=bank_ready if start else None,
                                  order=(4, 5, 6, 7, 0, 2, 1, 3) if start else None, banks_signal=stop)
                base, par = at_.slab, at_.slab % 2
                pe.wait_ge(act_low_ready, at_.ffn - 2)
                one(par, base, 0, True, False)
                with pe.Fori(0, N_DOWN // 2 - 1) as i:
                    for s in (1, 2):
                        one((par + s) % 2, 2 * i + (base + s), 4 * i + 2 * s, False, False)
                for s in (N_DOWN - 2, N_DOWN - 1):
                    if s == N_DOWN - 1:
                        pe.wait_ge(act_low_ready, at_.ffn)
                    one((par + s) % 2, base + s, 2 * s, False, s == N_DOWN - 1)
                at_.slab += N_DOWN

            def feature_slab_fill(slot, quarter, n, hi, lo, ready=None):
                pe.wait_ge(slab_split, n + 1)
                slab_features(slot, 8, 256, lambda k: hi[:, k, :], lambda k: lo[:, k, :],
                              lambda b: 2 * quarter + b, True, True, ready=ready)

            def gates():
                ready, par = part_waits(), at_.slab % 2
                for q in range(4):
                    if q >= 2:
                        pe.wait_ge(turned_dve, at_.turn_d - (2 if q == 2 else 0))
                    feature_slab_fill((par + q) % 2, q, at_.slab + q, g_hi, g_lo, ready if q == 0 else None)
                for q in range(4):
                    pe.wait_ge(banks_drained, at_.drain + q + 1)
                    feature_slab_fill((par + q) % 2, q, at_.slab + 4 + q, g_hi, g_lo)
                at_.slab += N_GATE
                at_.drain += N_GATE

            def ffn_up():
                base, par, drained = at_.slab, at_.slab % 2, at_.ffn

                ready = part_waits()

                def pair(i, half, guarded):
                    for u in (0, 1):
                        if guarded:
                            pe.wait_ge(up_drained, 4 * i + (drained + 2 * half - 2))
                        feature_slab_fill((par + u) % 2, 2 * half + u, 4 * i + (base + 2 * half + u), f_hi, f_lo,
                                          ready if not guarded and half == u == 0 else None)
                pair(0, 0, False)
                pair(0, 1, False)
                with pe.Fori(1, FB // 4) as i:
                    pair(i, 0, True)
                    pair(i, 1, True)
                pair(FB // 4, 0, True)
                at_.slab += N_UP
                at_.ffn += FB

            def turn(items, split=False, bank0=0, ready=None):
                for n, it in enumerate(items):
                    src, w = it[0], (P if split else it[1])
                    if ready:
                        ready(n)
                    if n >= 8:
                        pe.wait_ge(turned_dve if n % 2 else turned_act,
                                   (at_.turn_d if n % 2 else at_.turn_a) + (n - 8) // 2 + 1)
                    for tt in range(TT):
                        last = nc.tensor.transpose(PS[0:w, (bank0 + n) % 8, 128 * tt:128 * tt + 128], src(tt), ident)
                    last.then_inc(turned, 1)
                at_.turn += len(items)
                at_.turn_a += len(items) if split else (len(items) + 1) // 2
                at_.turn_d += len(items) if split else len(items) // 2

            def release_clock(n):
                for _ in range(n):
                    nc.tensor.matmul(PS[:, 7, :], ident, causal, start=True, stop=True)

            def attend(jobs, ring):
                tiles = map_tiles(jobs)
                g0, m0 = at_.tile, at_.map
                copies = []
                a, d = at_.acopies, at_.dcopies
                for m, j in tiles:
                    if j == TT - 1:
                        d += 1
                        copies.append((copied_dve, d))
                    else:
                        a += 1
                        copies.append((copied_act, a))
                n = len(tiles)
                for step in range(n + VALUE_LAG):
                    if step < n:
                        m, j = tiles[step]
                        lo, nb = key_range(jobs[m], j)
                        if step >= S_BANKS:
                            pe.wait_ge(scores_masked, g0 + step - S_BANKS + 1)
                        nc.tensor.matmul(PS[:, step % S_BANKS, 0:128 * nb], jobs[m]["q"][:, 128 * j:128 * j + 128],
                                         jobs[m]["k"][:, 128 * lo:128 * (lo + nb)], start=True, stop=True
                                         ).then_inc(scores_ready, 1)
                    if TURN_LAG <= step < TURN_LAG + len(FILL):
                        release_clock(FILL[step - TURN_LAG])
                    u = step - TURN_LAG
                    if 0 <= u < n:
                        m, j = tiles[u]
                        lo, nb = key_range(jobs[m], j)
                        pe.wait_ge(probs_ready, g0 + u + 1)
                        if u >= PT_BANKS:
                            pe.wait_ge(*copies[u - PT_BANKS])
                        for b in range(nb):
                            last = nc.tensor.transpose(PS[:, S_BANKS + u % PT_BANKS, 128 * b:128 * b + 128],
                                                       probs_slot(ring, u, slice(128 * b, 128 * b + 128)), ident)
                        last.then_inc(probsT_ready, 1)
                    u = step - VALUE_LAG
                    if 0 <= u < n:
                        m, j = tiles[u]
                        lo, nb = key_range(jobs[m], j)
                        pe.wait_ge(*copies[u])
                        if u % TT == 0 and m >= O_BANKS:
                            pe.wait_ge(out_used, m0 + m - O_BANKS + 1)
                        for b in range(nb):
                            last = nc.tensor.matmul(PS[:, 6 + m % O_BANKS, 64 * j:64 * j + 64],
                                                    turned_slot(ring, u, slice(128 * b, 128 * b + 128)),
                                                    jobs[m]["v"](lo + b), start=b == 0, stop=b == nb - 1)
                        last.then_inc(pv_done, 1)
                at_.tile += n
                at_.map += len(jobs)
                at_.acopies, at_.dcopies = a, d

            meet()
            pe.wait_ge(const_loaded, 16 * 2)
            norm(t1, residual=False)
            input_tokens(h_hi, h_lo, 4)
            pe.wait_ge(banks_drained, at_.drain - 1)
            for s in (0, 1):
                pe.wait_ge(slab_split, at_.slab + 1)
                slab_tokens(s, h_hi, h_lo, 4 * s, 4, TAIL, 0, 1, s == 0, s == 1)
                at_.slab += 1
            at_.drain += 1
            meet()
            meet()
            turn(cmp_turns)
            meet()
            meet()
            for kv in (0, 1):
                for hf in (0, 1):
                    for c in range(CMP_CHUNKS):
                        nc.tensor.matmul(PS[:, hf, 0:GROUPS * N_CMP], cmpw[:, kv, c, 128 * hf:128 * hf + 128],
                                         flat[:, kv, c, :, :], start=c == 0, stop=c == CMP_CHUNKS - 1)
                meet(2)
                for g in range(GROUPS):
                    for hf in (0, 1):
                        nc.tensor.matmul(PS[0:N_CMP, 2, HD * g:HD * g + HD], c_hid[:, hf, N_CMP * g:N_CMP * g + N_CMP],
                                         cmpw2[:, kv, hf, :], start=hf == 0, stop=hf == 1)
                meet(2)
            turn(nsa_turns())
            meet(4)
            nc.tensor.transpose(PS[:, 7, 0:N_CMP], c_k[0:N_CMP, :, :].rearrange("p g d -> p (g d)"),
                                ident[0:N_CMP, 0:N_CMP])
            meet(2)
            for g in range(GROUPS):
                lo = 64 * g
                for i in range(REP * TT):
                    r, tt = divmod(i, TT)
                    last = nc.tensor.matmul(PS[:, 7 * g, 32 * i:32 * i + N_CMP],
                                            qT_n[lo:lo + 64, r, 128 * tt:128 * tt + 128],
                                            c_kkT[lo:lo + 64, :], start=True, stop=True)
                last.then_inc(c_scored, 1)
            for g in range(GROUPS):
                pe.wait_ge(c_probs, g + 1)
                if g:
                    pe.wait_ge(c_copied, 1)
                for i in range(REP * TT):
                    last = nc.tensor.transpose(PS[0:N_CMP, 1 + i // 4, 128 * (i % 4):128 * (i % 4) + 128],
                                               c_p[:, g, i, 0:N_CMP], ident)
                last.then_inc(c_turned, 1)
                pe.wait_ge(c_copied, g + 1)
                banks_ = (0, 7) if g else (5, 6)
                for i in range(REP * TT):
                    last = nc.tensor.matmul(PS[:, banks_[i // 8], 64 * (i % 8):64 * (i % 8) + 64],
                                            c_pT[0:N_CMP, i, :], c_v[0:N_CMP, g, :], start=True, stop=True)
                last.then_inc(c_valued, 1)
            meet(2)
            attend(nsa_jobs, ring_n)
            meet()
            turn(c_splits, split=True)
            base = at_.turn_d - KD
            for s in range(N_QB):
                pe.wait_ge(slab_split, at_.slab + 1)
                slab_tokens(at_.slab % 2, c_hi, c_lo, 2 * s, 2, Q_LORA, 0, 2, s == 0, s == N_QB - 1,
                            ready=lambda k: pe.wait_ge(turned_dve, base + k + 1),
                            banks_ready=(lambda tt: pe.wait_ge(turned_dve, base + 2 * tt + 2)) if s == 0 else None)
                at_.slab += 1
            meet(2)
            pe.wait_ge(slab_split, at_.slab + 1)
            slab_tokens(at_.slab % 2, c_hi, c_lo, 6, 2, 1024, 0, 2, True, True)
            at_.slab += 1
            meet()
            turn(mla_q_turns)

            def k_turn_ready(n):
                pe.wait_ge(mla_scaled, 1)
                if n % 2:
                    pe.wait_ge(turned_dve, q_dve + n // 2 + 1)
                else:
                    pe.wait_ge(turned_act, q_act + n // 2 + 1)
            q_act, q_dve = at_.turn_a - MLA_HEADS // 2, at_.turn_d - MLA_HEADS // 2
            turn(mla_k_turns, ready=k_turn_ready)
            meet()
            attend(mla_jobs, ring_m)
            meet()
            norm(t2, residual=False)
            turn(om_splits, split=True, bank0=4)
            gates()

            def on_bank_ready(n):
                pe.wait_ge(banks_drained, at_.drain - (3 if n < 2 else 2))

            turn(on_splits, split=True, ready=on_bank_ready)
            on_turned = at_.turn_d

            def om_bank_ready(b):
                if b < 4:
                    pe.wait_ge(turned_dve, on_turned - 3 + b)
                else:
                    pe.wait_ge(banks_drained, at_.drain - (1 if b < 6 else 0))

            project(OmT_hi, OmT_lo, N_OM, lambda k: None, om_bank_ready)
            project(OnT_hi, OnT_lo, N_ON, lambda k: None,
                    lambda b: pe.wait_ge(bank_free, at_.free + b + 1))
            project(m_hi, m_lo, N_WOUT, part_waits(),
                    lambda b: pe.wait_ge(bank_free, at_.free + 8 + b + 1))
            at_.free += 16

            def mlp():
                norm(t3)
                ffn_up()
                project_ffn()

            mlp()
            for layer in range(LAYERS):
                norm(t4)
                input_tokens(f_hi, f_lo, 6)

                def two_ready(n):
                    pe.wait_ge(rotated, 5 * layer + two_turn_chunk[n] + 1)
                    if n in (0, 4):
                        pe.wait_ge(banks_drained, at_.drain - (1 if n == 0 else 0))
                turn(two_turns, ready=two_ready)
                meet()
                attend(two_jobs, ring_2)
                meet()
                turn(o2_splits, split=True,
                     ready=lambda n: pe.wait_ge(diff_ready, layer + 1) if n == 6 else None)
                base = at_.turn_d - 8
                project(o_hi, o_lo, N_WOUT, lambda k: pe.wait_ge(turned_dve, base + k + 1),
                        lambda b: pe.wait_ge(turned_dve, base + b + 1))
                mlp()
            norm(t3)
            meet()

        @block.scalar
        def _(act):
            at_ = Place()
            meet = meeting("act", act, at_)
            A = nc.scalar.activation
            def norm(t, hi, shift=None, residual=True):
                A(small[:, 8:9], eps_c, ACT.Sqrt)
                for k in range(KD):
                    if residual:
                        act.wait_ge(x_ready, at_.x + k + 1)
                    A(t[:, k, :], xT[:, k, :], ACT.Square).then_inc(sq_ready, 1)
                if residual:
                    at_.x += KD
                at_.norms += 1
                act.wait_ge(mean_ready, at_.norms)
                A(t[:, KD, :], PS[:, 0, :], ACT.Sqrt, bias=eps_c).then_inc(root_ready, 1)
                if hi is not None:
                    high_parts(t, hi, shift)

            def high_parts(t, hi, shift=None):
                for k in range(KD):
                    act.wait_ge(part_ready, at_.part + k + 1)
                    if shift is None:
                        A(hi[:, k, :], t[:, k, :], ACT.Copy).then_inc(part_hi, 1)
                    else:
                        A(hi[:, k, :], t[:, k, :], ACT.Identity, bias=shift[:, k:k + 1]).then_inc(part_hi, 1)
                at_.part += KD

            def evacuate(dst, n_chunks):
                with act.Fori(0, n_chunks // 2) as i:
                    for par in (0, 1):
                        act.wait_ge(slab_used, 4 * i + (at_.slab + 2 * par + 2))
                        A(dst(2 * i + par), PS[:, 4 * par:4 * par + 4, :], ACT.Copy).then_inc(banks_drained, 1)
                at_.slab += 2 * n_chunks

            def turn(items):
                for n, (_, w, dst, scale) in enumerate(items):
                    if n % 2 == 0:
                        act.wait_ge(turned, at_.turn + n + 1)
                        A(dst, PS[0:w, n % 8, :], ACT.Copy, scale=scale).then_inc(turned_act, 1)
                at_.turn += len(items)

            def turn_split_high(items, bank0=0):
                for n, (_, hi, lo, gain) in enumerate(items):
                    act.wait_ge(turned, at_.turn + n + 1)
                    A(hi, PS[:, (bank0 + n) % 8, :], ACT.Copy, scale=1.0 if gain is None else gain).then_inc(turned_act, 1)
                at_.turn += len(items)

            def root(v, d):
                A(v, v, ACT.Sqrt, scale=1.0 / d, bias=eps_c[0:v.shape[0]])

            def attend(jobs, ring):
                tiles = map_tiles(jobs)
                g0 = at_.tile
                n = len(tiles)
                for step in range(n + TURN_LAG):
                    if step < n:
                        m, j = tiles[step]
                        _, nb = key_range(jobs[m], j)
                        act.wait_ge(scores_masked, g0 + step + 1)
                        if step >= P_SLOTS:
                            act.wait_ge(probsT_ready, g0 + step - P_SLOTS + 1)
                        A(probs_slot(ring, step, slice(0, 128 * nb)), masked_slot(ring, step, 128 * nb), ACT.Exp,
                          scale=-1.0,
                          bias=negmax[:, step % 8:step % 8 + 1],
                          accum_out=rowsum[:, m % 4, j:j + 1]).then_inc(probs_ready, 1)
                    u = step - TURN_LAG
                    if u >= 0 and tiles[u][1] != TT - 1:
                        _, nb = key_range(jobs[tiles[u][0]], tiles[u][1])
                        act.wait_ge(probsT_ready, g0 + u + 1)
                        if u >= PT_SLOTS:
                            act.wait_ge(pv_done, g0 + u - PT_SLOTS + 1)
                        A(turned_slot(ring, u, slice(0, 128 * nb)), PS[:, S_BANKS + u % PT_BANKS, 0:128 * nb],
                          ACT.Copy).then_inc(copied_act, 1)
                at_.tile += n

            act.wait_ge(crow_loaded, 16)
            A(crow[:], crow[:], ACT.Silu)
            meet()
            act.wait_ge(x_loaded, 16)
            norm(t1, h_hi, mod[:, 0:KD], residual=False)
            evacuate(lambda c: z[:, ds(c, 1), :, :], 4)
            act.dma_start(cmpw[:], cmpw_d).then_inc(cmpw_loaded, 16)
            act.wait_ge(slab_used, at_.slab + N_TAIL)
            A(z_tail[:], PS[:, 0:4, 0:TAIL], ACT.Copy).then_inc(banks_drained, 1)
            at_.slab += N_TAIL
            meet()
            A(z_tail[:, :, TAIL_G:TAIL_G + 24], z_tail[:, :, TAIL_G:TAIL_G + 24], ACT.Sigmoid)
            meet()
            turn(cmp_turns)
            meet()
            A(trig[:].rearrange("p c t f -> p (c t f)"), trig[:].rearrange("p c t f -> p (c t f)"), ACT.Sin)
            A(ctrig[0:N_CMP, :, :], ctrig[0:N_CMP, :, :], ACT.Sin)
            act.wait_ge(cmpw_loaded, 16)
            meet()
            for kv in (0, 1):
                if kv == 0:
                    A(n_sq[:], z[:, 0, :, :].rearrange("p t f -> p (t f)"), ACT.Square).then_inc(heads_sq, 1)
                    A(n_sq2[:, 0, :], z[:, 1, :, 256:384], ACT.Square)
                    A(n_sq2[:, 1, :], z_tail[:, :, 0:128], ACT.Square).then_inc(heads_sq, 1)
                    act.wait_ge(heads_sum, 1)
                    A(stats[:, 0:48], stats[:, 0:48], ACT.Sqrt, scale=1.0 / HD, bias=eps_c).then_inc(heads_root, 1)
                    for tt in range(TT):
                        for i, sl in enumerate((z[:, 2, tt, :], z[:, 3, tt, 0:256], z[:, 3, tt, 256:512])):
                            last = A(l_sq[:, 0:sl.shape[1]], sl, ACT.Square,
                                     accum_out=stats[:, 100 + 4 * i + tt:101 + 4 * i + tt])
                            act.drain()
                    act.drain().then_inc(latents_sq, 1)
                else:
                    act.wait_ge(latents_sum, 1)
                    root(stats[:, 100:104], Q_LORA)
                    A(stats[:, 108:112], stats[:, 108:112], ACT.Sqrt, scale=1.0 / KV_LORA, bias=eps_c
                      ).then_inc(latents_root, 1)
                meet()
                A(c_hid[:], PS[:, 0:2, 0:GROUPS * N_CMP], ACT.Silu)
                meet(2)
                A((c_v if kv else c_k)[0:N_CMP, :, :].rearrange("p g d -> p (g d)"), PS[0:N_CMP, 2, 0:GROUPS * HD],
                  ACT.Copy)
                meet()
            A(c_sq[0:N_CMP, :], c_k[0:N_CMP, :, :].rearrange("p g d -> p (g d)"), ACT.Square)
            meet(2)
            root(stats[0:N_CMP, 48:50], HD)
            turn(nsa_turns())
            meet(3)
            A(c_kkT[:], PS[:, 7, 0:N_CMP], ACT.Copy)
            meet()
            for g in range(GROUPS):
                act.wait_ge(c_shifted, g + 1)
                A(c_p[:, g, :, 0:N_CMP], c_sm[:, :, :, 0:N_CMP].rearrange("p r t n -> p (r t) n"), ACT.Exp,
                  scale=-1.0).then_inc(c_probs, 1)
                act.wait_ge(c_turned, g + 1)
                if g:
                    act.wait_ge(c_valued, 1)
                A(c_pT[0:N_CMP, :, :].rearrange("p i q -> p (i q)"),
                  PS[0:N_CMP, 1:5, :].rearrange("p b f -> p (b f)"), ACT.Copy).then_inc(c_copied, 1)
            meet(2)
            attend(nsa_jobs, ring_n)
            meet()
            turn_split_high(c_splits)
            meet()
            for tt in (0, 1):
                A(q_m[:, tt, :].rearrange("p (a b) -> p a b", a=2), PS[:, 2 * tt:2 * tt + 2, 0:Q_LORA // 2], ACT.Copy)
            meet()
            A(m_sq[:], q_m[:].rearrange("p t f -> p (t f)"), ACT.Square).then_inc(mla_sq, 1)
            act.wait_ge(mla_sum, 1)
            A(stats[:, 0:32], stats[:, 0:32], ACT.Sqrt, scale=1.0 / MLA_QK, bias=eps_c).then_inc(mla_root, 1)
            act.wait_ge(slab_used, at_.slab + N_QB + N_KVB)
            for tt in range(TT):
                A(kv_m[:, tt, :].rearrange("p (a b) -> p a b", a=2), PS[:, 2 * tt:2 * tt + 2, :], ACT.Copy)
            A(k_m[:, :, :, MLA_NOPE:MLA_QK],
              z_tail[:, :, TAIL_PE:TAIL].unsqueeze(2).to_broadcast([P, TT, MLA_HEADS, MLA_ROPE]), ACT.Copy)
            act.drain()
            A(k_m[:, :, :, 0:MLA_NOPE],
              kv_m[:].rearrange("p t (h d) -> p t h d", d=MLA_NOPE + MLA_V)[:, :, :, 0:MLA_NOPE], ACT.Copy)
            act.drain()
            A(mk_sq[:], k_m[:].rearrange("p t h d -> p (t h d)"), ACT.Square).then_inc(mla_sq, 1)
            meet()
            turn(mla_q_turns)
            act.wait_ge(mla_sum, 2)
            A(stats[:, 32:64], stats[:, 32:64], ACT.Sqrt, scale=1.0 / MLA_QK, bias=eps_c).then_inc(mla_root, 1)
            turn(mla_k_turns)
            meet()
            attend(mla_jobs, ring_m)
            meet()
            at_.slab += N_QB + N_KVB
            norm(t2, g_hi, mod[:, 0:KD], residual=False)
            turn_split_high(om_splits, bank0=4)
            for q in range(N_GATE):
                act.wait_ge(slab_used, at_.slab + q + 1)
                A(gate[:, 2 * q:2 * q + 2, :], PS[:, 2 * (q % 4):2 * (q % 4) + 2, :],
                  ACT.Sigmoid).then_inc(banks_drained, 1)
            turn_split_high(on_splits)
            high_parts(mrg, m_hi)
            at_.slab += N_GATE + N_OM + N_ON + N_WOUT

            def mlp(layer):
                norm(t3, f_hi, mod[:, 3 * KD:4 * KD] if layer is None else None)
                fill0, f0 = at_.slab, at_.ffn

                def one(i, half, b):
                    f = 4 * i + (2 * half + b)
                    fi = ds(f, 1)
                    if layer is None:
                        act.wait_ge(slab_used, 4 * i + (fill0 + 2 * half + 1))
                        A(tsg, PS[:, 4 * half + b, :], ACT.Silu).then_inc(silu_ready, 1)
                    else:
                        act.wait_ge(slab_used, 4 * i + (fill0 + 2 * half + 2))
                        for t, bank, fb in ((tg, 4 * half + b, 0), (tv, 4 * half + 2 + b, FB)):
                            w = COLS["conv_w"][0] + (layer * 3 + 2) * 2 * FB + fb
                            c = COLS["conv_b"][0] + layer * 2 * FB + fb
                            last = A(t, PS[:, bank, :], ACT.Identity, scale=cols[:, ds(f + w, 1)],
                                     bias=cols[:, ds(f + c, 1)])
                        last.then_inc(conv_started, 1)
                        act.wait_ge(conv_ready, 4 * i + (at_.conv + 2 * half + b + 1))
                        A(tsg, tg, ACT.Silu).then_inc(silu_ready, 1)
                    act.wait_ge(prod_ready, 4 * i + (f0 + 2 * half + b + 1))
                    A(a_hi[:, fi, :], ta, ACT.Copy).then_inc(act_hi_ready, 1)

                with act.Fori(0, FB // 4) as i:
                    for half in (0, 1):
                        for b in (0, 1):
                            one(i, half, b)
                for b in (0, 1):
                    one(FB // 4, 0, b)
                at_.slab += N_UP + N_DOWN
                at_.ffn += FB
                if layer is not None:
                    at_.conv += FB

            mlp(None)
            act.dma_start(strip2[:], strips_d[1]).then_inc(strip_loaded, 16)
            for layer in range(LAYERS):
                norm(t4, f_hi)
                evacuate(lambda c: z2[:, ds(c, 1), :, :], 6)
                act.wait_ge(lam_summed, layer + 1)
                A(small[:, 4:6], small[:, 4:6], ACT.Exp)
                turn(two_turns)
                meet()
                attend(two_jobs, ring_2)
                meet()
                A(sq_2[:], O2[:, :, 768:1024], ACT.Square).then_inc(diff_sq, 1)
                turn_split_high(o2_splits[0:2])
                act.wait_ge(diff_sum, layer + 1)
                A(stats[:, 0:16], stats[:, 0:16], ACT.Sqrt, scale=1.0 / HD, bias=eps_c).then_inc(diff_root, 1)
                turn_split_high(o2_splits[2:8], bank0=2)
                at_.slab += N_WOUT
                mlp(layer)
            norm(t3, None)
            meet()

        @block.vector
        def _(dve):
            at_ = Place()
            meet = meeting("dve", dve, at_)
            V = nc.vector

            def then(_ins):
                dve.drain()

            def low_part(k, t, hi, lo, shift=None):
                dve.wait_ge(part_hi, at_.part + k + 1)
                if shift is None:
                    V.tensor_tensor(lo[:, k, :], t[:, k, :], hi[:, k, :].bitcast(f32), ALU.subtract
                                    ).then_inc(part_low, 1)
                else:
                    V.scalar_tensor_tensor(out=lo[:, k, :], in0=t[:, k, :], scalar=shift[:, k:k + 1],
                                           in1=hi[:, k, :].bitcast(f32), op0=ALU.add, op1=ALU.subtract
                                           ).then_inc(part_low, 1)

            def norm(t, hi, lo, scale, shift=None):
                at_.norms += 1
                dve.wait_ge(root_ready, at_.norms)
                then(V.reciprocal(t[:, KD, :], t[:, KD, :]))
                for k in range(KD + 1):
                    if k < KD:
                        V.scalar_tensor_tensor(out=t[:, k, :], in0=xT[:, k, :], scalar=scale[:, k:k + 1],
                                               in1=t[:, KD, :], op0=ALU.mult, op1=ALU.mult
                                               ).then_inc(part_ready, 1)
                    if hi is not None and k > 0:
                        low_part(k - 1, t, hi, lo, shift)
                at_.part += KD

            def banks(use):
                for b in range(8):
                    if b < 7:
                        dve.wait_ge(bank_done, at_.bank + b + 1)
                    else:
                        dve.wait_ge(slab_used, at_.slab)
                    use(b)
                at_.bank += 7

            def residual(n, t, factor=None):
                at_.slab += n

                def use(k):
                    if factor is None:
                        i_ = V.tensor_tensor(xT[:, k, :], xT[:, k, :], PS[:, k, :], ALU.add)
                    else:
                        i_ = V.scalar_tensor_tensor(out=xT[:, k, :], in0=PS[:, k, :], scalar=factor[:, k:k + 1],
                                                    in1=xT[:, k, :], op0=ALU.mult, op1=ALU.add)
                    i_.then_inc(x_ready, 1)
                    if k in (3, 5, 7):
                        pair = k - 3
                        dve.wait_ge(sq_ready, KD * at_.norms + pair + 2)
                        V.tensor_tensor(t[:, pair + 1, :], t[:, pair + 1, :], t[:, pair, :], ALU.add
                                        ).then_inc(pair_ready, 1)
                banks(use)

            def turn(items):
                for n, (_, w, dst, scale) in enumerate(items):
                    if n % 2:
                        dve.wait_ge(turned, at_.turn + n + 1)
                        V.tensor_scalar(dst, PS[0:w, n % 8, :], scale, None, ALU.mult).then_inc(turned_dve, 1)
                at_.turn += len(items)

            def turn_split_low(items, bank0=0):
                for n, (_, hi, lo, gain) in enumerate(items):
                    dve.wait_ge(turned_act, at_.turn_a + n + 1)
                    V.scalar_tensor_tensor(out=lo, in0=PS[:, (bank0 + n) % 8, :], scalar=1.0 if gain is None else gain,
                                           in1=hi.bitcast(f32), op0=ALU.mult, op1=ALU.subtract
                                           ).then_inc(turned_dve, 1)
                at_.turn += len(items)
                at_.turn_a += len(items)

            def turn_counted(items):
                turn(items)
                at_.turn_a += (len(items) + 1) // 2

            def reduce_angles(ang, k, cosv, sinv):
                magic = 1.5 * 2.0 ** 23
                then(V.tensor_scalar(k, ang, 1.0 / (2 * math.pi), magic, ALU.mult, ALU.add))
                then(V.tensor_scalar(k, k, magic, None, ALU.subtract))
                for part in two_pi_parts():
                    then(V.scalar_tensor_tensor(out=ang, in0=k, scalar=-part, in1=ang, op0=ALU.mult, op1=ALU.add))
                then(V.tensor_scalar(sinv, ang, 3.1415925, -3.1415925, ALU.min, ALU.max))
                then(V.tensor_scalar(k, sinv, -1.0, None, ALU.mult))
                then(V.tensor_tensor(k, k, sinv, ALU.max))
                then(V.tensor_scalar(cosv, k, -1.0, math.pi / 2, ALU.mult, ALU.add))

            def rotate(x1, x2, cosv, sinv, tmp, n):
                shape = list(x1.shape)
                c, s = (v.unsqueeze(2).to_broadcast(shape) for v in (cosv, sinv))
                a, b, e, f = (tmp[0:shape[0], i, 0:n].rearrange("p (t h f) -> p t h f", t=shape[1], h=shape[2])
                              for i in range(4))
                V.tensor_tensor(a, x1, c, ALU.mult)
                V.tensor_tensor(b, x2, s, ALU.mult)
                V.tensor_tensor(e, x2, c, ALU.mult)
                then(V.tensor_tensor(f, x1, s, ALU.mult))
                V.tensor_tensor(x1, a, b, ALU.subtract)
                then(V.tensor_tensor(x2, e, f, ALU.add))

            def scale_heads(x, inv, gain, d0=0):
                shape = list(x.shape)
                then(V.tensor_tensor(x, x, inv.rearrange("p (t h) -> p t h", t=shape[1]).unsqueeze(3)
                                     .to_broadcast(shape), ALU.mult))
                part = x[:, :, :, d0:]
                then(V.tensor_tensor(part, part, gain[0:shape[0], d0:].unsqueeze(1).unsqueeze(1)
                                     .to_broadcast(list(part.shape)), ALU.mult))

            def attend(jobs, ring):
                tiles = map_tiles(jobs)
                g0, m0 = at_.tile, at_.map
                n = len(tiles)
                for step in range(n + TAKE_LAG):
                    if step < n:
                        m, j = tiles[step]
                        _, nb = key_range(jobs[m], j)
                        dve.wait_ge(scores_ready, g0 + step + 1)
                        if step >= M_SLOTS:
                            dve.wait_ge(probs_ready, g0 + step - M_SLOTS + 1)
                        V.tensor_tensor_reduce(out=masked_slot(ring, step, 128 * nb),
                                               in0=PS[:, step % S_BANKS, 0:128 * nb],
                                               in1=jobs[m]["strip"][:, SEQ - 128 * nb:SEQ], scale=1.0, scalar=NEG,
                                               op0=ALU.add, op1=ALU.min,
                                               accum_out=negmax[:, step % 8:step % 8 + 1]).then_inc(scores_masked, 1)
                    u = step - TURN_LAG
                    if 0 <= u < n and tiles[u][1] == TT - 1:
                        _, nb = key_range(jobs[tiles[u][0]], tiles[u][1])
                        dve.wait_ge(probsT_ready, g0 + u + 1)
                        if u >= PT_SLOTS:
                            dve.wait_ge(pv_done, g0 + u - PT_SLOTS + 1)
                        V.tensor_copy(turned_slot(ring, u, slice(0, 128 * nb)),
                                      PS[:, S_BANKS + u % PT_BANKS, 0:128 * nb]).then_inc(copied_dve, 1)
                    u = step - TAKE_LAG
                    if u >= 0 and last_of_map(u):
                        m = tiles[u][0]
                        dve.wait_ge(pv_done, g0 + u + 1)
                        finish(jobs[m], m)
                at_.tile += n
                at_.map += len(jobs)

            def finish(jb, m):
                inv = stats[:, 200 + 4 * (m % 2):204 + 4 * (m % 2)]
                then(V.reciprocal(inv, rowsum[:, m % 4, :]))
                if jb["coef"] == "lam":
                    then(V.tensor_scalar(inv, inv, lam_c, None, ALU.mult))
                elif jb["coef"] is not None:
                    then(V.tensor_tensor(inv, inv, jb["coef"], ALU.mult))
                o = PS[:, 6 + m % O_BANKS, 0:TT * HD].rearrange("p (t d) -> p t d", t=TT)
                by = inv.unsqueeze(2).to_broadcast([P, TT, HD])
                if jb["mode"] == "set":
                    V.tensor_tensor(jb["out"], o, by, ALU.mult)
                    dve.drain().then_inc(out_used, 1)
                else:
                    tmp = (otmp_2 if jb["mode"] == "sub" else otmp_n)[:]
                    V.tensor_tensor(tmp, o, by, ALU.mult)
                    dve.drain().then_inc(out_used, 1)
                    then(V.tensor_tensor(jb["out"], jb["out"], tmp, ALU.add if jb["mode"] == "add" else ALU.subtract))

            V.memset(small[:], EPS)
            meet()

            def modulate(row_, n):
                return V.scalar_tensor_tensor(out=row_, in0=row_, scalar=1.0, in1=crow[:], op0=ALU.mult,
                                              op1=ALU.mult, accum_out=mod[:, ds(n, 1)])

            def modulate_more(i0, i1):
                with dve.Fori(i0, i1) as i:
                    for s in (0, 1):
                        dve.wait_ge(ada_loaded[s], 16 * i + 16)
                        modulate(aux[:, s, :], 2 * i + (2 * KD + s))
                        dve.drain().then_inc(ada_used, 1)

            for n in range(2 * KD):
                if n % 4 == 0:
                    dve.wait_ge(ada_first_loaded[n // 4], 16)
                then(modulate(ada_first[:, n, :], n))
            dve.wait_ge(const_loaded, 16 * 2)
            dve.wait_ge(x_loaded, 16)
            then(V.tensor_tensor(mod[:, 0:2 * KD], mod[:, 0:2 * KD], col("ada_b", 0, 2 * KD), ALU.add))
            sh1, sc1, gt1, sh2, sc2, gt2 = (mod[:, KD * i:KD * i + KD] for i in range(N_MOD))
            then(V.scalar_tensor_tensor(out=sc1, in0=sc1, scalar=1.0, in1=col("norm1", 0, KD), op0=ALU.add,
                                        op1=ALU.mult))
            norm(t1, h_hi, h_lo, sc1, sh1)
            dve.wait_ge(rest_loaded, 16 * 6)
            posf = stats[:, 0:9]
            V.memset(trig[:].rearrange("p c t f -> p (c t f)"), 0.0)
            dve.drain()
            V.tensor_copy(posf[:, 0:8], posi[:, 0:8])
            then(V.tensor_copy(posf[0:N_CMP, 8:9], posi[0:N_CMP, 8:9]))
            ang = stats[:, 16:16 + TT * N_FREQ].rearrange("p (t f) -> p t f", t=TT)
            turns = stats[:, 120:120 + TT * N_FREQ].rearrange("p (t f) -> p t f", t=TT)
            freq = const("freq")
            for blk, a, n in ((0, 0, MLA_ROPE // 2), (1, MLA_ROPE // 2, ROT // 2)):
                V.tensor_tensor(ang[:, :, a:a + n], posf[:, 4 * blk:4 * blk + 4].unsqueeze(2).to_broadcast([P, TT, n]),
                                freq[:, a:a + n].unsqueeze(1).to_broadcast([P, TT, n]), ALU.mult)
            dve.drain()
            reduce_angles(ang, turns, trig[:, 0, :, :], trig[:, 1, :, :])
            cang, cturns = stats[0:N_CMP, 16:24], stats[0:N_CMP, 120:128]
            then(V.tensor_scalar(cang, freq[0:N_CMP, 0:MLA_ROPE // 2:2], posf[0:N_CMP, 8:9], None, ALU.mult))
            reduce_angles(cang, cturns, ctrig[0:N_CMP, 0, :], ctrig[0:N_CMP, 1, :])

            modulate_more(0, KD)
            meet()
            src = z[:, 1, :, 0:256].rearrange("p t (i d) -> p t i d", i=4)
            for dup in (0, 1):
                V.tensor_copy(c_stage[:, :, :, dup, :], src)
            meet()
            turn_counted(cmp_turns)
            meet()
            for kv in (0, 1):
                for half in (0, 1):
                    ps_ = slice(64 * half, 64 * half + 64)
                    for g in range(GROUPS):
                        v = c_kT[ps_, 2 * kv + g, :].rearrange("p (n m two) -> p m n two", m=8, two=2)
                        for mh in (0, 1):
                            V.tensor_tensor(flat[ps_, kv, 8 * mh:8 * mh + 8, g, :], v[:, :, mh:mh + N_CMP, half],
                                            cmpp[ps_, kv, 8 * mh:8 * mh + 8].unsqueeze(2)
                                            .to_broadcast([64, 8, N_CMP]), ALU.add)
            meet()
            cosn, sinn = (trig[:, i, :, 0:MLA_ROPE // 2:2] for i in (0, 1))
            half = ROT // 2

            def norm_heads(x, a, n, gain, c, s, tmp=n_rope):
                pn = x.shape[0]
                scale_heads(x, stats[0:pn, a:a + n], row(gain))
                rotate(x[:, :, :, 0:half], x[:, :, :, half:ROT], c, s, tmp, n * half)

            for kv in (0, 1):
                if kv == 0:
                    dve.wait_ge(heads_sq, 1)
                    V.tensor_reduce(out=stats[:, 0:32], in_=n_sq[:].rearrange("p (a d) -> p a d", d=HD), op=ALU.add,
                                    axis=AX.X)
                    dve.wait_ge(heads_sq, 2)
                    V.tensor_reduce(out=stats[:, 32:48], in_=n_sq2[:].rearrange("p a (b d) -> p (a b) d", d=HD),
                                    op=ALU.add, axis=AX.X)
                    dve.drain().then_inc(heads_sum, 1)
                    dve.wait_ge(heads_root, 1)
                    then(V.reciprocal(stats[:, 0:48], stats[:, 0:48]))
                    norm_heads(z[:, 0, :, :].rearrange("p t (h d) -> p t h d", d=HD), 0, 32, "q", cosn, sinn)
                else:
                    dve.wait_ge(latents_sq, 1)
                    V.tensor_tensor(stats[:, 100:104], stats[:, 100:104], stats[:, 104:108], ALU.add
                                    ).then_inc(latents_sum, 1)
                    norm_heads(z[:, 1, :, 256:384].rearrange("p t (h d) -> p t h d", d=HD), 32, 8, "ks", cosn, sinn)
                    norm_heads(z_tail[:, :, 0:128].rearrange("p t (h d) -> p t h d", d=HD), 40, 8, "kw", cosn, sinn)
                    dve.wait_ge(latents_root, 1)
                    then(V.reciprocal(stats[:, 100:112], stats[:, 100:112]))
                    for tt in range(TT):
                        V.tensor_scalar(z[:, 2, tt, :], z[:, 2, tt, :], stats[:, 100 + tt:101 + tt], None, ALU.mult)
                        V.tensor_scalar(z[:, 3, tt, 0:256], z[:, 3, tt, 0:256], stats[:, 100 + tt:101 + tt], None,
                                        ALU.mult)
                        V.tensor_scalar(z[:, 3, tt, 256:512], z[:, 3, tt, 256:512], stats[:, 108 + tt:109 + tt],
                                        None, ALU.mult)
                meet(4)
            meet()
            V.tensor_reduce(out=stats[0:N_CMP, 48:50], in_=c_sq[0:N_CMP, :].rearrange("p (a d) -> p a d", d=HD),
                            op=ALU.add, axis=AX.X)
            meet()
            turn_counted(nsa_turns())
            meet()
            then(V.reciprocal(stats[0:N_CMP, 48:50], stats[0:N_CMP, 48:50]))
            norm_heads(c_k[0:N_CMP, :, :].unsqueeze(1), 48, 2, "kc", ctrig[0:N_CMP, 0:1, :], ctrig[0:N_CMP, 1:2, :],
                       c_rope)
            meet(3)
            sums = stats[:, 80:112].rearrange("p (g r t) -> p g r t", g=GROUPS, r=REP)
            cm = const("cmask").rearrange("p (t n) -> p t n", t=TT)
            for g in range(GROUPS):
                dve.wait_ge(c_scored, g + 1)
                if g:
                    dve.wait_ge(c_probs, 1)
                sv = PS[:, 7 * g, :].rearrange("p (r t n) -> p r t n", r=REP, t=TT)[:, :, :, 0:N_CMP]
                mv = c_sm[:, :, :, 0:N_CMP]
                for r in range(REP):
                    V.tensor_tensor(mv[:, r], sv[:, r], cm, ALU.add)
                dve.drain()
                mn = stats[:, 64:80]
                then(V.tensor_reduce(out=mn, in_=mv.rearrange("p r t n -> p (r t) n"), op=ALU.min, axis=AX.X))
                mvf = mv.rearrange("p r t n -> p (r t) n")
                then(V.tensor_tensor(mvf, mvf, mn.unsqueeze(2).to_broadcast([P, REP * TT, N_CMP]), ALU.subtract
                                     ).then_inc(c_shifted, 1))
            for g in range(GROUPS):
                dve.wait_ge(c_probs, g + 1)
                s3 = sums[:, g, :, :]
                s2 = stats[:, 80 + 16 * g:96 + 16 * g]
                then(V.tensor_reduce(out=s2, in_=c_p[:, g, :, 0:N_CMP], op=ALU.add, axis=AX.X))
                then(V.reciprocal(s2, s2))
                then(V.tensor_tensor(s3, s3, const("rowvalid").unsqueeze(1).to_broadcast([P, REP, TT]), ALU.mult))
                for r in range(REP):
                    V.tensor_tensor(s3[:, r, :], s3[:, r, :], sigm(g * REP + r, 0), ALU.mult)
                dve.drain()
                dve.wait_ge(c_valued, g + 1)
                banks_ = (0, 7) if g else (5, 6)
                for r in range(REP):
                    h = g * REP + r
                    o = PS[:, banks_[r // 2], 256 * (r % 2):256 * (r % 2) + 256].rearrange("p (t d) -> p t d", t=TT)
                    V.tensor_tensor(O_nsa[:, :, 64 * h:64 * h + 64], o,
                                    s3[:, r, :].unsqueeze(2).to_broadcast([P, TT, HD]), ALU.mult)
            meet(2)
            attend(nsa_jobs, ring_n)
            meet()
            turn_split_low(c_splits)
            meet()
            for tt in (2, 3):
                V.tensor_copy(q_m[:, tt, :].rearrange("p (a b) -> p a b", a=2), PS[:, 2 * tt:2 * tt + 2, 0:Q_LORA // 2])
            meet()
            half = MLA_ROPE // 2

            def norm_mla(x, sq, a, gain, d0, nth):
                dve.wait_ge(mla_sq, nth)
                V.tensor_reduce(out=stats[:, a:a + 32], in_=sq[:].rearrange("p (a d) -> p a d", d=MLA_QK),
                                op=ALU.add, axis=AX.X).then_inc(mla_sum, 1)
                if nth == 2:
                    turn(mla_q_turns)
                    at_.turn_a += MLA_HEADS // 2
                dve.wait_ge(mla_root, nth)
                then(V.reciprocal(stats[:, a:a + 32], stats[:, a:a + 32]))
                scale_heads(x, stats[:, a:a + 32], row(gain), d0)
                rotate(x[:, :, :, MLA_NOPE:MLA_NOPE + half], x[:, :, :, MLA_NOPE + half:MLA_QK],
                       trig[:, 0, :, 0:half], trig[:, 1, :, 0:half], m_rope, 32 * half)

            then(V.tensor_tensor(row("mla_q", 0, MLA_NOPE), row("mla_q", 0, MLA_NOPE), row("mla_k", 0, MLA_NOPE),
                                 ALU.mult))
            norm_mla(q_m[:].rearrange("p t (h d) -> p t h d", d=MLA_QK), m_sq, 0, "mla_q", 0, 1)
            meet()
            norm_mla(k_m[:], mk_sq, 32, "mla_k", MLA_NOPE, 2)
            dve.drain().then_inc(mla_scaled, 1)
            turn_counted(mla_k_turns)
            meet()
            attend(mla_jobs, ring_m)
            meet()
            norm(t2, g_hi, g_lo, sc1, sh1)
            turn_split_low(om_splits, bank0=4)
            modulate_more(KD, 2 * KD)
            then(V.tensor_tensor(mod[:, 2 * KD:], mod[:, 2 * KD:], col("ada_b", 2 * KD, 4 * KD), ALU.add))
            then(V.scalar_tensor_tensor(out=sc2, in0=sc2, scalar=1.0, in1=col("norm2", 0, KD), op0=ALU.add,
                                        op1=ALU.mult))
            turn_split_low(on_splits)
            at_.slab = N_IN + N_TAIL + N_QB + N_KVB + N_GATE + N_OM

            def gate_mla(k):
                V.tensor_tensor(mrg[:, k, :], PS[:, k, :], gate[:, k, :], ALU.mult).then_inc(bank_free, 1)

            def gate_nsa(k):
                V.tensor_tensor(mtmp[:, k, :], PS[:, k, :], gate[:, KD + k, :], ALU.mult).then_inc(bank_free, 1)
            dve.wait_ge(banks_drained, N_IN // 2 + 1 + N_GATE)
            banks(gate_mla)
            at_.slab += N_ON
            banks(gate_nsa)
            dve.drain()
            for k in range(KD + 1):
                if k < KD:
                    V.tensor_tensor(mrg[:, k, :], mrg[:, k, :], mtmp[:, k, :], ALU.add).then_inc(part_ready, 1)
                if k > 0:
                    low_part(k - 1, mrg, m_hi, m_lo)
            at_.part += KD
            residual(N_WOUT, t3, gt1)

            def mlp(layer):
                if layer is None:
                    norm(t3, f_hi, f_lo, sc2, sh2)
                else:
                    norm(t3, f_hi, f_lo, col("ffn", layer * KD, KD))
                f0 = at_.ffn

                def one(i, half, b):
                    f = 4 * i + (2 * half + b)
                    n = 4 * i + (f0 + 2 * half + b + 1)
                    dve.drain()
                    if layer is None:
                        dve.wait_ge(slab_used, 4 * i + (at_.slab + 2 * half + 2))
                        dve.wait_ge(silu_ready, n)
                        V.tensor_tensor(ta, tsg, PS[:, 4 * half + 2 + b, :], ALU.mult)
                        dve.drain().then_inc(up_drained, 1)
                        dve.drain().then_inc(prod_ready, 1)
                    else:
                        dve.wait_ge(conv_started, 4 * i + (at_.conv + 2 * half + b + 1))
                        for tap in (1, 0):
                            for t, bank, fb in ((tg, 4 * half + b, 0), (tv, 4 * half + 2 + b, FB)):
                                w = COLS["conv_w"][0] + (layer * 3 + tap) * 2 * FB + fb
                                sh = 2 - tap
                                V.scalar_tensor_tensor(out=t[:, sh:], in0=PS[:, bank, 0:SEQ - sh],
                                                       scalar=cols[:, ds(f + w, 1)], in1=t[:, sh:],
                                                       op0=ALU.mult, op1=ALU.add)
                            last = dve.drain()
                        last.then_inc(conv_ready, 1)
                        dve.drain().then_inc(up_drained, 1)
                        dve.wait_ge(silu_ready, n)
                        V.tensor_tensor(ta, tsg, tv, ALU.mult).then_inc(prod_ready, 1)
                    dve.wait_ge(act_hi_ready, n)
                    V.tensor_tensor(a_lo[:, ds(f, 1), :], ta, a_hi[:, ds(f, 1), :].bitcast(f32), ALU.subtract
                                    ).then_inc(act_low_ready, 1)

                with dve.Fori(0, FB // 4) as i:
                    for half in (0, 1):
                        for b in (0, 1):
                            one(i, half, b)
                for b in (0, 1):
                    one(FB // 4, 0, b)
                at_.slab += N_UP
                at_.ffn += FB
                if layer is not None:
                    at_.conv += FB
                residual(N_DOWN, t4 if layer is None or layer < LAYERS - 1 else t3, gt2 if layer is None else None)

            mlp(None)
            for layer in range(LAYERS):
                norm(t4, f_hi, f_lo, col("mix", layer * KD, KD))
                at_.slab += N_IN2
                drained = N_IN // 2 + 1 + N_GATE + 6 * layer
                for chunk, parts in enumerate((((0, 8, DIFF), (256, 8, DIFF)), ((256, 4, HD),), ((0, 4, HD),),
                                               ((0, 8, HD),), ((0, 8, HD),))):
                    dve.wait_ge(banks_drained, drained + chunk + 1)
                    for a, n, d in parts:
                        x = z2[:, chunk, :, a:a + n * d].rearrange("p t (h d) -> p t h d", d=d)
                        half, step = d // 8, (2 if d == DIFF else 1)
                        f1 = MLA_ROPE // 2
                        rotate(x[:, :, :, 0:half], x[:, :, :, half:2 * half], trig[:, 0, :, f1:f1 + 8:step],
                               trig[:, 1, :, f1:f1 + 8:step], rope_2, TT * n * half)
                    dve.drain().then_inc(rotated, 1)
                    if chunk == 3:
                        for i, (a, b) in enumerate((("lq1", "lk1"), ("lq2", "lk2"))):
                            then(V.tensor_tensor_reduce(out=otmp_2[:, 0, 0:DIFF], in0=row(a, layer * DIFF, DIFF),
                                                        in1=row(b, layer * DIFF, DIFF), scale=1.0, scalar=0.0,
                                                        op0=ALU.mult, op1=ALU.add, accum_out=small[:, 4 + i:5 + i]))
                        dve.drain().then_inc(lam_summed, 1)
                turn_counted(two_turns)
                meet()
                then(V.tensor_tensor(lam_c, small[:, 4:5], small[:, 5:6], ALU.subtract))
                then(V.tensor_scalar(lam_c, lam_c, LAM_INIT[layer], None, ALU.add))
                if layer == 0:
                    dve.wait_ge(strip_loaded, 16)
                attend(two_jobs, ring_2)
                meet()
                dve.wait_ge(diff_sq, layer + 1)
                V.tensor_reduce(out=stats[:, 0:16], in_=sq_2[:].rearrange("p (a d) -> p a d", d=HD), op=ALU.add,
                                axis=AX.X).then_inc(diff_sum, 1)
                turn_split_low(o2_splits[0:2])
                dve.wait_ge(diff_root, layer + 1)
                then(V.reciprocal(stats[:, 0:16], stats[:, 0:16]))
                then(V.tensor_scalar(stats[:, 0:16], stats[:, 0:16], 1.0 - LAM_INIT[layer], None, ALU.mult))
                scale_heads(O2[:, :, 768:1024].rearrange("p t (h d) -> p t h d", d=HD), stats[:, 0:16],
                            row("diff", layer * HD, HD))
                dve.drain().then_inc(diff_ready, 1)
                turn_split_low(o2_splits[2:8], bank0=2)
                residual(N_WOUT, t3)
                mlp(layer)
            norm(t3, None, None, col("final", 0, KD))
            meet()


def kernel(**inputs):
    import numpy as np
    import concourse.bacc as bacc
    from concourse import mybir
    from concourse.bass_utils import run_bass_kernel_spmd

    arrays = host_arrays({k: np.asarray(v) for k, v in inputs.items()})
    nc = bacc.Bacc("TRN2", target_bir_lowering=False, num_devices=1)
    args = [nc.dram_tensor(n, a.shape, mybir.dt.from_np(a.dtype), kind="ExternalInput").ap()
            for n, a in arrays.items()]
    out = nc.dram_tensor("out_dram", (P, KD, SEQ), mybir.dt.float32, kind="ExternalOutput").ap()
    build(nc, *args, out)
    r = run_bass_kernel_spmd(nc, [arrays], core_ids=[0])
    got = r.results[0]["out_dram"]
    return np.ascontiguousarray(got.transpose(2, 1, 0).reshape(1, SEQ, D_MODEL))


def host_arrays(a):
    def column(v):
        return v.reshape(-1, P).T

    def padded(s):
        s = s.reshape(P, -1)
        return np.concatenate([s, np.zeros((P, SLAB - s.shape[1]), s.dtype)], 1) if s.shape[1] < SLAB else s

    def slabs(w, k, n):
        kk, nn = w.shape[0] // P, w.shape[1] // n
        v = w.reshape(kk // k, k, P, nn, n).transpose(3, 0, 2, 1, 4)
        return [padded(v[c, s]) for c in range(nn) for s in range(kk // k)]

    w = a["w_in"][0]
    edges = np.cumsum([0, Q_LORA, KV_LORA, MLA_ROPE, HEADS * HD] + [GROUPS * HD] * 6 + [3 * HEADS, D_MODEL, D_MODEL])
    cq, ckv, kpe, qn, kc, vc, ks, vs, kw, vw, gn, gm1, gm2 = (w[:, edges[i]:edges[i + 1]] for i in range(13))
    qn = qn.reshape(D_MODEL, GROUPS, REP, HD).transpose(0, 2, 1, 3).reshape(D_MODEL, -1)
    first = np.concatenate([qn, kc, vc, ks, vs, cq, ckv], 1)
    tail = np.concatenate([kw, vw, gn, kpe], 1)

    def up_slabs(wg, wu):
        g, u = slabs(wg, KD, 256), slabs(wu, KD, 256)
        return [s for pair in zip(g, u) for s in pair]

    def heads_last(w):
        return np.concatenate([w[512:], w[256:512], w[:256]], 0)

    stream = slabs(first, 4, 512) + slabs(tail, 4, TAIL) + slabs(a["mla_w_q_b"][0], 2, MLA_HEADS * MLA_QK)
    stream += slabs(a["mla_w_kv_b"][0], 2, 1024) + slabs(np.concatenate([gm1, gm2], 1), KD, 256)
    stream += slabs(a["w_o_mla"][0], 2, 1024) + slabs(a["w_o_nsa"][0], 2, 1024) + slabs(a["w_out"][0], 2, 1024)
    stream += up_slabs(a["ffn_w_gate"][0], a["ffn_w_up"][0]) + slabs(a["ffn_w_down"][0], 2, 1024)
    for layer in range(LAYERS):
        stream += slabs(a["w_in_2"][layer], 4, 512) + slabs(heads_last(a["w_out_2"][layer]), 2, 1024)
        stream += up_slabs(a["w_up_2"][layer][:, :D_FF], a["w_up_2"][layer][:, D_FF:])
        stream += slabs(a["w_down_2"][layer], 2, 1024)
    assert len(stream) == N_SLABS

    col_src = {"norm1": a["norm1_gain"], "norm2": a["norm2_gain"], "q_a": a["mla_q_a_gain"],
               "kv_a": a["mla_kv_a_gain"], "mix": a["g_mix_2"], "ffn": a["g_ffn_2"], "final": a["g_final_2"],
               "ada_b": a["ada_b"], "conv_w": a["conv_w_2"], "conv_b": a["conv_b_2"]}
    row_src = {"mla_q": a["mla_q_gain"], "mla_k": a["mla_k_gain"], "q": a["nsa_q_gain"], "kc": a["nsa_kc_gain"],
               "ks": a["nsa_ks_gain"], "kw": a["nsa_kw_gain"], "diff": a["g_diff_2"], "lq1": a["lambda_q1_2"],
               "lk1": a["lambda_k1_2"], "lq2": a["lambda_q2_2"], "lk2": a["lambda_k2_2"]}
    pos, pos2 = a["positions"].reshape(-1), a["positions_2"].reshape(-1)
    cmp_end = np.arange(N_CMP) * CMP_STRIDE + CMP_LEN - 1
    out = {
        "xT": a["x"].reshape(SEQ, KD, P).transpose(2, 1, 0),
        "slabs": np.stack(stream),
        "ada": a["ada_w"][0].T.reshape(N_ADA, P, D_MODEL),
        "c": a["c"].reshape(-1),
        "cols": np.concatenate([column(col_src[n]) for n in COLS], 1),
        "rows": np.concatenate([row_src[n].reshape(-1) for n in ROWS]),
        "consts": shape_constants(),
        "strips": mask_strips(),
        "pos": np.concatenate([column(pos), column(pos2)], 1).astype(np.int32),
        "cpos": pos[cmp_end].reshape(-1, 1).astype(np.int32),
        "cmpw": np.stack([a[n][0].reshape(CMP_CHUNKS, P, CMP_HIDDEN).transpose(1, 0, 2)
                          for n in ("cmp_w1_k", "cmp_w1_v")], 1),
        "cmpp": np.stack([a[n][0].reshape(CMP_CHUNKS, P).T for n in ("cmp_pos_k", "cmp_pos_v")], 1),
        "cmpw2": np.stack([a[n][0].reshape(2, P, HD).transpose(1, 0, 2) for n in ("cmp_w2_k", "cmp_w2_v")], 1),
    }
    return {f"{k}_dram": np.ascontiguousarray(v) for k, v in out.items()}


def mask_strips():
    dist = np.arange(P)[:, None] - (np.arange(SEQ)[None, :] - (SEQ - P))
    window = np.where((dist >= 0) & (dist < WINDOW), 0.0, NEG)
    count = (dist <= 128).astype(int) + (dist % 4 == 0) + (dist % 16 == 0)
    dilated = np.where((dist >= 0) & (count > 0), -np.log(np.maximum(count, 1)), NEG)
    return np.stack([window, dilated]).astype(np.float32)


def shape_constants():
    token = np.arange(SEQ).reshape(TT, P).T
    ends = np.arange(N_CMP) * CMP_STRIDE + CMP_LEN - 1
    dist = np.arange(P)[:, None] - (np.arange(SEQ)[None, :] - (SEQ - P))
    freq = np.concatenate([THETA ** (-np.arange(0, MLA_ROPE, 2) / MLA_ROPE), THETA ** (-np.arange(0, ROT, 2) / ROT)])
    parts = {"ident": np.eye(P), "mean": np.full((P, P), 1.0 / D_MODEL),
             "freq": np.broadcast_to(freq, (P, N_FREQ)), "rowvalid": token >= ends[0],
             "cmask": np.where(ends <= token[:, :, None], 0.0, NEG).reshape(P, -1),
             "causal": np.where(dist >= 0, 0.0, NEG)}
    return np.concatenate([np.asarray(parts[n], np.float32) for n in CONSTS], 1)
```
